# Optimizing a Trainium2 kernel written in Bass

```python
import math
import jax
import jax.numpy as jnp
from jax import lax
import numpy as np

D_MODEL = 1024
BATCH = 1
SEQ = 1024
DEPTH = 1
DEC_BATCH = 1
DEC_SEQ = 32
PAST_LEN = 512

CHUNK = 64
EPS = 1e-6
NEG_INF = -1e30
Q_BLOCK = 128

A_HEADS = 8
A_DK = 64
A_DV = 2 * A_DK

S_INNER = 2 * D_MODEL
S_HEAD_P = 64
S_HEADS = S_INNER // S_HEAD_P
S_GROUPS = 4
S_HPG = S_HEADS // S_GROUPS
S_STATE = 128
S_CONV = 4
S_CONV_DIM = S_INNER + 2 * S_GROUPS * S_STATE

P_HEADS = 8
P_NKEYS = 128
P_EXPERTS = P_NKEYS * P_NKEYS
P_DKEY = 128
P_TOPK = 16
P_BLOCK = 256

PLE_DIM = 256

C_Q = A_HEADS * 2 * A_DK
C_K = A_HEADS * 2 * A_DK
C_V = A_HEADS * A_DV
C_Z = S_INNER
C_XBC = S_CONV_DIM
C_DT = S_HEADS
C_GATE = 2 * D_MODEL
IN_COLS = C_Q + C_K + C_V + C_Z + C_XBC + C_DT + C_GATE
SPLIT_AT = (C_Q, C_Q + C_K, C_Q + C_K + C_V, C_Q + C_K + C_V + C_Z,
            C_Q + C_K + C_V + C_Z + C_XBC, C_Q + C_K + C_V + C_Z + C_XBC + C_DT)

kernel_name = 'hybrid_diffattn_ssd_peer_stream_step'

def _rms(xf):
    return xf * lax.rsqrt(jnp.mean(xf * xf, axis=-1, keepdims=True) + EPS)

def rms_norm(x, g):
    return (_rms(x.astype(jnp.float32)) * g.astype(jnp.float32)).astype(x.dtype)

def alibi_slopes():
    return 2.0 ** (-8.0 * (jnp.arange(A_HEADS, dtype=jnp.float32) + 1.0) / A_HEADS)

def diff_scores_apply(q, k, v, q_pos, k_pos, lam):
    s = jnp.einsum('bqhjd,bkhjd->bhjqk', q, k).astype(jnp.float32) * (A_DK ** -0.5)
    dist = jnp.abs(q_pos[:, None] - k_pos[None, :]).astype(jnp.float32)
    bias = -alibi_slopes()[:, None, None, None] * dist
    mask = (k_pos[None, :] // CHUNK) <= (q_pos[:, None] // CHUNK)
    a = jax.nn.softmax(jnp.where(mask, s + bias, NEG_INF), axis=-1)
    w = a[:, :, 0] - lam * a[:, :, 1]
    return jnp.einsum('bhqk,bkhd->bqhd', w.astype(v.dtype), v)

def diff_attention(q, k_all, v_all, q_pos, k_pos, lam, lam_init, sub_g, w_o):
    bsz, lq = q.shape[:2]
    if lq >= Q_BLOCK and lq % Q_BLOCK == 0:
        nb = lq // Q_BLOCK
        qb = jnp.swapaxes(q.reshape(bsz, nb, Q_BLOCK, A_HEADS, 2, A_DK), 0, 1)
        pb = q_pos.reshape(nb, Q_BLOCK)
        ob = lax.map(lambda t: diff_scores_apply(t[0], k_all, v_all, t[1], k_pos, lam), (qb, pb))
        o = jnp.swapaxes(ob, 0, 1).reshape(bsz, lq, A_HEADS, A_DV)
    else:
        o = diff_scores_apply(q, k_all, v_all, q_pos, k_pos, lam)
    o = rms_norm(o, sub_g) * (1.0 - lam_init)
    return o.reshape(bsz, lq, A_HEADS * A_DV) @ w_o

def causal_conv(xbc, past, w, b):
    xp = jnp.concatenate([past.astype(xbc.dtype), xbc], axis=1)
    y = lax.conv_general_dilated(xp, w[:, None, :].astype(xbc.dtype), window_strides=(1,),
                                 padding='VALID', dimension_numbers=('NWC', 'WIO', 'NWC'),
                                 feature_group_count=S_CONV_DIM)
    return jax.nn.silu(y + b.astype(xbc.dtype)), xp[:, -(S_CONV - 1):]

def ssd(x, dt, a, bm, cm, h0, q_len):
    bsz, length = x.shape[:2]
    nc = length // q_len
    xc = jnp.moveaxis(x.reshape(bsz, nc, q_len, S_GROUPS, S_HPG, S_HEAD_P), 1, 0)
    dtc = dt.reshape(bsz, nc, q_len, S_GROUPS, S_HPG)
    dac = jnp.moveaxis(dtc * a.reshape(S_GROUPS, S_HPG), 1, 0)
    dtc = jnp.moveaxis(dtc, 1, 0)
    bc = jnp.moveaxis(bm.reshape(bsz, nc, q_len, S_GROUPS, S_STATE), 1, 0)
    cc = jnp.moveaxis(cm.reshape(bsz, nc, q_len, S_GROUPS, S_STATE), 1, 0)
    causal = jnp.tril(jnp.ones((q_len, q_len), dtype=bool))[None, :, :, None, None]

    def step(h, inp):
        xk, dtk, dak, bk, ck = inp
        acum = jnp.cumsum(dak, axis=1)
        seg = acum[:, :, None] - acum[:, None, :]
        lmat = jnp.exp(jnp.where(causal, seg, -jnp.inf))
        cb = jnp.einsum('blgn,bsgn->blsg', ck, bk)
        m = cb[..., None] * lmat * dtk[:, None]
        y = jnp.einsum('blsgh,bsghp->blghp', m, xk)
        y = y + jnp.einsum('blgn,bghpn->blghp', ck, h) * jnp.exp(acum)[..., None]
        wdec = jnp.exp(acum[:, -1:] - acum) * dtk
        h_new = jnp.exp(acum[:, -1])[..., None, None] * h + jnp.einsum(
            'bsgn,bsghp->bghpn', bk, wdec[..., None] * xk)
        return h_new, y

    h_init = h0.reshape(bsz, S_GROUPS, S_HPG, S_HEAD_P, S_STATE)
    h_fin, ys = lax.scan(step, h_init, (xc, dtc, dac, bc, cc))
    y = jnp.moveaxis(ys, 0, 1).reshape(bsz, length, S_HEADS, S_HEAD_P)
    return y, h_fin.reshape(bsz, S_HEADS, S_HEAD_P, S_STATE)

def ssm_branch(z, xbc, dt_raw, conv_past, h0, lp, q_len):
    bsz, length = z.shape[:2]
    xbc_act, conv_new = causal_conv(xbc, conv_past, lp['conv_w'], lp['conv_b'])
    xs = xbc_act[..., :S_INNER].reshape(bsz, length, S_HEADS, S_HEAD_P).astype(jnp.float32)
    bm = xbc_act[..., S_INNER:S_INNER + S_GROUPS * S_STATE].reshape(
        bsz, length, S_GROUPS, S_STATE).astype(jnp.float32)
    cm = xbc_act[..., S_INNER + S_GROUPS * S_STATE:].reshape(
        bsz, length, S_GROUPS, S_STATE).astype(jnp.float32)
    dt = jax.nn.softplus(dt_raw.astype(jnp.float32) + lp['dt_bias'].astype(jnp.float32))
    a = -jnp.exp(lp['a_log'].astype(jnp.float32))
    y, h_fin = ssd(xs, dt, a, bm, cm, h0.astype(jnp.float32), q_len)
    y = y + lp['d_skip'].astype(jnp.float32)[:, None] * xs
    yg = y.reshape(bsz, length, S_INNER) * jax.nn.silu(z.astype(jnp.float32))
    yg = _rms(yg.reshape(bsz, length, S_GROUPS, S_INNER // S_GROUPS)).reshape(bsz, length, S_INNER)
    yg = (yg * lp['ssm_norm_g'].astype(jnp.float32)).astype(z.dtype)
    return yg @ lp['w_ssm_o'], conv_new, h_fin.astype(z.dtype)

def peer_ffn(h, wq, k1, k2, u, v):
    bsz, length, d = h.shape
    t = h.reshape(-1, d)
    n_tok = t.shape[0]
    nb = -(-n_tok // P_BLOCK)
    t = jnp.pad(t, ((0, nb * P_BLOCK - n_tok), (0, 0))).reshape(nb, P_BLOCK, d)
    half = P_DKEY // 2

    def block(tb):
        q = (tb @ wq).reshape(P_BLOCK, P_HEADS, P_DKEY)
        s1 = jnp.einsum('thd,nd->thn', q[..., :half], k1).astype(jnp.float32)
        s2 = jnp.einsum('thd,nd->thn', q[..., half:], k2).astype(jnp.float32)
        v1, i1 = lax.top_k(s1, P_TOPK)
        v2, i2 = lax.top_k(s2, P_TOPK)
        cand = (v1[..., :, None] + v2[..., None, :]).reshape(P_BLOCK, P_HEADS, P_TOPK * P_TOPK)
        cidx = (i1[..., :, None] * P_NKEYS + i2[..., None, :]).reshape(P_BLOCK, P_HEADS, P_TOPK * P_TOPK)
        sc, pos = lax.top_k(cand, P_TOPK)
        idx = jnp.take_along_axis(cidx, pos, axis=-1)
        g = jax.nn.softmax(sc, axis=-1)
        pre = jnp.einsum('td,thkd->thk', tb, u[idx])
        act = (jax.nn.gelu(pre.astype(jnp.float32)) * g).astype(tb.dtype)
        return jnp.einsum('thk,thkd->td', act, v[idx])

    out = lax.map(block, t).reshape(nb * P_BLOCK, d)[:n_tok]
    return out.reshape(bsz, length, d)

def hybrid_layer(x, p_i, k_past, v_past, conv_past, ssm_past, q_pos, k_pos, ssd_len, lp, lam_init):
    bsz, length = x.shape[:2]
    h = rms_norm(x, lp['norm_mix_g'])
    q, k, v, z, xbc, dt_raw, gates = jnp.split(h @ lp['w_in'], SPLIT_AT, axis=-1)
    q = q.reshape(bsz, length, A_HEADS, 2, A_DK)
    k = k.reshape(bsz, length, A_HEADS, 2, A_DK)
    v = v.reshape(bsz, length, A_HEADS, A_DV)
    k_all = k if k_past is None else jnp.concatenate([k_past.astype(k.dtype), k], axis=1)
    v_all = v if v_past is None else jnp.concatenate([v_past.astype(v.dtype), v], axis=1)
    f32 = jnp.float32
    lam = (jnp.exp(jnp.sum(lp['lam_q1'].astype(f32) * lp['lam_k1'].astype(f32)))
           - jnp.exp(jnp.sum(lp['lam_q2'].astype(f32) * lp['lam_k2'].astype(f32))) + lam_init)
    o_a = diff_attention(q, k_all, v_all, q_pos, k_pos, lam, lam_init, lp['attn_subln_g'], lp['w_attn_o'])
    if conv_past is None:
        conv_past = jnp.zeros((bsz, S_CONV - 1, S_CONV_DIM), x.dtype)
    if ssm_past is None:
        ssm_past = jnp.zeros((bsz, S_HEADS, S_HEAD_P, S_STATE), jnp.float32)
    o_s, conv_new, ssm_new = ssm_branch(z, xbc, dt_raw, conv_past, ssm_past, lp, ssd_len)
    g_a, g_s = jnp.split(gates, 2, axis=-1)
    x = x + (jax.nn.sigmoid(g_a) * o_a + jax.nn.sigmoid(g_s) * o_s) @ lp['w_out']
    x = x + peer_ffn(rms_norm(x, lp['norm_ffn_g']), lp['peer_wq'], lp['peer_k1'], lp['peer_k2'],
                     lp['peer_u'], lp['peer_v'])
    x = x + jax.nn.sigmoid(rms_norm(x, lp['norm_ple_g']) @ lp['ple_w_gate']) * (p_i @ lp['ple_w_proj'])
    return x, k, v, conv_new, ssm_new

def setup_inputs(seed: int = 0) -> dict:
    key = jax.random.key(seed)
    ks = iter(jax.random.split(key, 40))
    f32 = jnp.float32

    def nrm(shape, scale):
        return jax.random.normal(next(ks), shape, f32) * scale

    def gain(shape):
        return 1.0 + 0.02 * jax.random.normal(next(ks), shape, f32)

    dt0 = jnp.exp(jax.random.uniform(next(ks), (DEPTH, S_HEADS), f32)
                  * (math.log(0.1) - math.log(0.001)) + math.log(0.001))
    return {
        'x_prompt': nrm((BATCH, SEQ, D_MODEL), 1.0),
        'x_sample': nrm((DEC_BATCH, DEC_SEQ, D_MODEL), 1.0),
        'p_prompt': nrm((DEPTH, BATCH, SEQ, PLE_DIM), 1.0),
        'p_sample': nrm((DEPTH, DEC_BATCH, DEC_SEQ, PLE_DIM), 1.0),
        'cache_k': nrm((DEPTH, DEC_BATCH, PAST_LEN, A_HEADS, 2, A_DK), 1.0),
        'cache_v': nrm((DEPTH, DEC_BATCH, PAST_LEN, A_HEADS, A_DV), 1.0),
        'state_conv': nrm((DEPTH, DEC_BATCH, S_CONV - 1, S_CONV_DIM), 1.0),
        'state_ssm': nrm((DEPTH, DEC_BATCH, S_HEADS, S_HEAD_P, S_STATE), 0.5),
        'norm_mix_g': gain((DEPTH, D_MODEL)),
        'w_in': nrm((DEPTH, D_MODEL, IN_COLS), D_MODEL ** -0.5),
        'lam_q1': nrm((DEPTH, A_DK), 0.1),
        'lam_k1': nrm((DEPTH, A_DK), 0.1),
        'lam_q2': nrm((DEPTH, A_DK), 0.1),
        'lam_k2': nrm((DEPTH, A_DK), 0.1),
        'attn_subln_g': gain((DEPTH, A_DV)),
        'w_attn_o': nrm((DEPTH, A_HEADS * A_DV, D_MODEL), (A_HEADS * A_DV) ** -0.5),
        'conv_w': nrm((DEPTH, S_CONV, S_CONV_DIM), S_CONV ** -0.5),
        'conv_b': nrm((DEPTH, S_CONV_DIM), 0.02),
        'dt_bias': dt0 + jnp.log(-jnp.expm1(-dt0)),
        'a_log': jnp.log(jax.random.uniform(next(ks), (DEPTH, S_HEADS), f32, 1.0, 16.0)),
        'd_skip': 1.0 + 0.1 * jax.random.normal(next(ks), (DEPTH, S_HEADS), f32),
        'ssm_norm_g': gain((DEPTH, S_INNER)),
        'w_ssm_o': nrm((DEPTH, S_INNER, D_MODEL), S_INNER ** -0.5),
        'w_out': nrm((DEPTH, D_MODEL, D_MODEL), D_MODEL ** -0.5),
        'norm_ffn_g': gain((DEPTH, D_MODEL)),
        'peer_wq': nrm((DEPTH, D_MODEL, P_HEADS * P_DKEY), D_MODEL ** -0.5),
        'peer_k1': nrm((DEPTH, P_NKEYS, P_DKEY // 2), (P_DKEY // 2) ** -0.5),
        'peer_k2': nrm((DEPTH, P_NKEYS, P_DKEY // 2), (P_DKEY // 2) ** -0.5),
        'peer_u': nrm((DEPTH, P_EXPERTS, D_MODEL), D_MODEL ** -0.5),
        'peer_v': nrm((DEPTH, P_EXPERTS, D_MODEL), 0.3),
        'norm_ple_g': gain((DEPTH, D_MODEL)),
        'ple_w_gate': nrm((DEPTH, D_MODEL, D_MODEL), D_MODEL ** -0.5),
        'ple_w_proj': nrm((DEPTH, PLE_DIM, D_MODEL), PLE_DIM ** -0.5),
        'final_norm_g': gain((D_MODEL,)),
    }

def reference(x_prompt, x_sample, p_prompt, p_sample, cache_k, cache_v, state_conv, state_ssm,
              norm_mix_g, w_in, lam_q1, lam_k1, lam_q2, lam_k2, attn_subln_g, w_attn_o,
              conv_w, conv_b, dt_bias, a_log, d_skip, ssm_norm_g, w_ssm_o, w_out,
              norm_ffn_g, peer_wq, peer_k1, peer_k2, peer_u, peer_v,
              norm_ple_g, ple_w_gate, ple_w_proj, final_norm_g):

    def run_group(x, p, ck, cv, cconv, cssm, q_pos, k_pos, ssd_len):
        k_rows, v_rows, conv_rows, ssm_rows = [], [], [], []
        for i in range(DEPTH):
            lp = {
                'norm_mix_g': norm_mix_g[i], 'w_in': w_in[i],
                'lam_q1': lam_q1[i], 'lam_k1': lam_k1[i], 'lam_q2': lam_q2[i], 'lam_k2': lam_k2[i],
                'attn_subln_g': attn_subln_g[i], 'w_attn_o': w_attn_o[i],
                'conv_w': conv_w[i], 'conv_b': conv_b[i], 'dt_bias': dt_bias[i], 'a_log': a_log[i],
                'd_skip': d_skip[i], 'ssm_norm_g': ssm_norm_g[i], 'w_ssm_o': w_ssm_o[i],
                'w_out': w_out[i], 'norm_ffn_g': norm_ffn_g[i], 'peer_wq': peer_wq[i],
                'peer_k1': peer_k1[i], 'peer_k2': peer_k2[i], 'peer_u': peer_u[i], 'peer_v': peer_v[i],
                'norm_ple_g': norm_ple_g[i], 'ple_w_gate': ple_w_gate[i], 'ple_w_proj': ple_w_proj[i],
            }
            lam_init = 0.8 - 0.6 * math.exp(-0.3 * i)
            x, k_new, v_new, conv_new, ssm_new = hybrid_layer(
                x, p[i],
                None if ck is None else ck[i], None if cv is None else cv[i],
                None if cconv is None else cconv[i], None if cssm is None else cssm[i],
                q_pos, k_pos, ssd_len, lp, lam_init)
            k_rows.append(k_new)
            v_rows.append(v_new)
            conv_rows.append(conv_new)
            ssm_rows.append(ssm_new)
        return (rms_norm(x, final_norm_g), jnp.stack(k_rows), jnp.stack(v_rows),
                jnp.stack(conv_rows), jnp.stack(ssm_rows))

    lp_len = x_prompt.shape[1]
    pos_p = jnp.arange(lp_len, dtype=jnp.int32)
    y_prompt, k_prompt, v_prompt, conv_prompt, ssm_prompt = run_group(
        x_prompt, p_prompt, None, None, None, None, pos_p, pos_p, CHUNK)

    ls_len = x_sample.shape[1]
    past = cache_k.shape[2]
    q_pos_s = past + jnp.arange(ls_len, dtype=jnp.int32)
    k_pos_s = jnp.arange(past + ls_len, dtype=jnp.int32)
    y_sample, k_sample, v_sample, conv_sample, ssm_sample = run_group(
        x_sample, p_sample, cache_k, cache_v, state_conv, state_ssm, q_pos_s, k_pos_s, ls_len)

    return (y_prompt, y_sample, k_prompt, v_prompt, conv_prompt, ssm_prompt,
            k_sample, v_sample, conv_sample, ssm_sample)


_drawn_inputs = setup_inputs


def setup_inputs(seed=0):
    import zlib

    import numpy as np

    out = dict(_drawn_inputs(seed))
    spreads = {}
    factors = {'lam_k2': 2.975,
     'attn_subln_g': 13.178,
     'ssm_norm_g': 10.604,
     'norm_ffn_g': 9.847,
     'norm_ple_g': 64.0,
     'final_norm_g': 8.054}
    for name, (base, spread) in spreads.items():
        noise = np.random.default_rng([zlib.crc32(name.encode()), seed]).standard_normal(out[name].shape)
        drawn = base * np.exp(spread * noise) if base else spread * noise
        out[name] = jnp.asarray(drawn.astype(out[name].dtype))
    for name, factor in factors.items():
        out[name] = (out[name] * factor).astype(out[name].dtype)
    return out
```

```python
from contextlib import ExitStack

import numpy as np

import concourse.bass as bass
from concourse import mybir

F32 = mybir.dt.float32
U32 = mybir.dt.uint32
I32 = mybir.dt.int32
ALU = mybir.AluOpType
ACT = mybir.ActivationFunctionType
AX_X = mybir.AxisListType.X

P = 128
D = 1024
DK = D // P
SEQ, DEC, PAST = 1024, 32, 512
T = SEQ + DEC
NPT = SEQ // P
NT = NPT + 1
TP = NT * P
EPS = 1e-6
LAM_INIT = 0.8 - 0.6 * 1.0
H = 8
AK = 64
CH = 64
SIN = 2048
SH, SP_, SG, SN = 32, 64, 4, 128
SCONV, SCD = 4, 3072
PH, PNK, PTOP = 8, 128, 16
PSLOT = PH * PTOP
PLE = 256
C_Q, C_K, C_V, C_Z, C_XBC, C_DT, C_G = 0, 1024, 2048, 3072, 5120, 8192, 8224
IN_COLS = 10272
PANEL = 512
NSPLIT = 3
TS = T // NSPLIT
NEG = -1e30


def rows_of(t):
    return P if t < NPT else DEC


def hold(engine, gate, sem, value):
    engine.wait_ge(sem, value)
    engine.sem_inc(gate, 1)


class Stage:

    def __init__(self, nc, tag):
        self.nc, self.tag, self.stack, self.semaphores = nc, tag, ExitStack(), []

    def __enter__(self):
        self.stack.__enter__()
        return self

    def __exit__(self, *exc):
        if self.semaphores:
            self.nc.clear_and_free_semaphores(self.semaphores)
            self.nc.all_engine_barrier()
        return self.stack.__exit__(*exc)

    def sb(self, name, shape, dt=F32):
        return self.stack.enter_context(self.nc.sbuf_tensor(f"{self.tag}_{name}", shape, dt))

    def ps(self, name, shape, dt=F32):
        return self.stack.enter_context(self.nc.psum_tensor(f"{self.tag}_{name}", shape, dt))

    def sem(self, name):
        self.semaphores.append(self.nc.alloc_semaphore(name=f"{self.tag}_{name}"))
        return self.semaphores[-1]

    def sems(self, name, n):
        return [self.sem(f"{name}{i}") for i in range(n)]


def build_constants(nc, c):
    with Stage(nc, "cst") as s:
        filled, selected = s.sem("filled"), s.sem("selected")
        with nc.Block() as block:

            @block.gpsimd
            def _(pool):
                pool.memset(c.ident[:], 0.0).then_inc(filled, 1)
                pool.memset(c.ones[:], 1.0).then_inc(filled, 1)
                pool.memset(c.upper[:], 1.0).then_inc(filled, 1)
                pool.memset(c.below[:], 1.0).then_inc(filled, 1)
                pool.memset(c.neghalf[:], -0.5).then_inc(filled, 1)
                pool.memset(c.dt[:], 0.0).then_inc(filled, 1)
                pool.wait_ge(filled, 6)
                pool.affine_select(out=c.ident[:], in_=c.ident[:], compare_op=ALU.not_equal, fill=1.0, base=0,
                                   pattern=[[-1, P]], channel_multiplier=1).then_inc(selected, 1)
                pool.affine_select(out=c.upper[:], in_=c.upper[:], compare_op=ALU.is_ge, fill=0.0, base=0,
                                   pattern=[[1, P]], channel_multiplier=-1).then_inc(selected, 1)
                pool.affine_select(out=c.below[:], in_=c.below[:], compare_op=ALU.is_gt, fill=0.0, base=0,
                                   pattern=[[-1, P]], channel_multiplier=1).then_inc(selected, 1)
                pool.wait_ge(selected, 3)


def project_inputs(nc, io, dr, c):
    NB = 6
    with Stage(nc, "proj") as s:
        xt = s.sb("xt", [P, NT, D])
        hT = s.sb("hT", [P, DK, T])
        wp = [s.sb(f"wp{i}", [P, DK, PANEL]) for i in range(2)]
        wdt = s.sb("wdt", [P, DK, SH])
        stg = [s.sb(f"stg{i}", [P, PANEL]) for i in range(NB)]
        sq = s.sb("sq", [P, D])
        ss = s.sb("ss", [P, NT])
        rr = s.sb("rr", [P, NT])
        gm = s.sb("gm", [P, DK])
        bank = [s.ps(f"bank{i}", [P, PANEL]) for i in range(NB)]
        tb = [s.ps(f"tb{i}", [P, 4, P]) for i in range(2)]

        x_in, g_in, wdt_in = s.sems("x_in", NT), s.sem("g_in"), s.sem("wdt_in")
        ss_init, ss_done, ms_done, rr_done, xn_done = s.sem("ss_init"), s.sem("ss_done"), s.sem("ms_done"), s.sem("rr_done"), s.sem("xn_done")
        turned, hT_done = s.sem("turned"), s.sem("hT_done")
        panel_in, panel_used = s.sems("panel_in", 2), s.sems("panel_used", 2)
        mm_done, evac_done, stored = s.sems("mm_done", NB), s.sems("evac_done", NB), s.sems("stored", NB)
        gate = s.sem("gate")

        def w_cols(base, n=PANEL):
            return io["w_in"][0].rearrange("(k p) n -> p k n", p=P)[:, :, bass.ds(base, n)]

        RUNS = [("qk", 4, C_Q), ("xbc", 6, C_XBC), ("v", 2, C_V), ("z", 4, C_Z), ("g", 4, C_G)]
        UNITS = {"qk": 4 * NSPLIT, "xbc": 4 * NSPLIT, "v": NT, "z": NT, "g": NT}

        def runs(eng, body):
            pairs, visits = 0, 0
            for kind, n, col in RUNS:
                per = 2 * UNITS[kind] // NB
                if n == 2:
                    body(kind, 0, col, pairs, visits)
                else:
                    with eng.Fori(0, n // 2) as i:
                        body(kind, i, col, pairs, visits)
                pairs += n // 2
                visits += per * n // 2

        def per_pair(kind):
            return 2 * UNITS[kind] // NB

        with nc.Block() as block:

            @block.gpsimd
            def _(pool):
                pool.wait_ge(ms_done, 1)
                pool.tensor_tensor(rr[:], ss[:], c.neghalf[:, 0:NT], ALU.pow).then_inc(rr_done, 1)

                def loads(kind, i, col, pairs, visits):
                    for b in range(2):
                        pool.wait_ge(panel_used[b], i + (pairs + 1))
                        pool.sem_inc(gate, 1)
                        pool.dma_start(wp[b][:], w_cols(i * (2 * PANEL) + (col + b * PANEL))).then_inc(panel_in[b], 16)

                runs(pool, loads)

            @block.sync
            def _(sp):
                sp.dma_start(gm[:], io["norm_mix_g"].rearrange("a (k p) -> p (a k)", p=P),
                             allow_slow_non_contiguous=True).then_inc(g_in, 16)
                for t in range(NT):
                    n = rows_of(t)
                    src = io["x_prompt"][0, t * P:(t + 1) * P, :] if t < NPT else io["x_sample"][0]
                    sp.dma_start(xt[0:n, t, :], src).then_inc(x_in[t], 16)
                sp.dma_start(wdt[:], w_cols(C_DT, SH)).then_inc(wdt_in, 16)

                for slot in range(NB):
                    sp.sem_inc(stored[slot], 16)

                def stores(kind, i, col, pairs, visits):
                    U = UNITS[kind]
                    for b in range(2):
                        for u in range(U):
                            j = b * U + u
                            slot = j % NB
                            sp.wait_ge(evac_done[slot], i * per_pair(kind) + (visits + j // NB + 2))
                            if kind in ("qk", "xbc"):
                                blk, sl = divmod(u, NSPLIT)
                                base = (C_XBC - C_V if kind == "xbc" else 0)
                                row = i * (2 * PANEL) + ((col - base) + b * PANEL + blk * P)
                                sp.dma_start(dr["chan"][bass.ds(row, P), sl * TS:(sl + 1) * TS],
                                             stg[slot][:, 0:TS]).then_inc(stored[slot], 16)
                            elif kind == "v":
                                n = rows_of(u)
                                dst = (io["v_prompt_out"][u * P:(u + 1) * P, b * PANEL:(b + 1) * PANEL] if u < NPT
                                       else io["v_sample_out"][:, b * PANEL:(b + 1) * PANEL])
                                sp.dma_start(dst, stg[slot][0:n, :]).then_inc(stored[slot], 16)
                            else:
                                n = rows_of(u)
                                name = "zs" if kind == "z" else "gs"
                                sp.dma_start(dr[name][u * P:u * P + n, bass.ds(i * (2 * PANEL) + b * PANEL, PANEL)],
                                             stg[slot][0:n, :]).then_inc(stored[slot], 16)

                runs(sp, stores)
                total = sum(n // 2 * per_pair(k) for k, n, _ in RUNS)
                for slot in range(NB):
                    sp.wait_ge(stored[slot], 16 * (total + 1))

            @block.vector
            def _(dve):
                dve.memset(ss[:], 0.0).then_inc(ss_init, 1)
                dve.wait_ge(ss_done, NT)
                dve.tensor_scalar(ss[:], ss[:], 1.0 / D, EPS, ALU.mult, ALU.add).then_inc(ms_done, 1)
                dve.wait_ge(rr_done, 1)
                for t in range(NT):
                    n = rows_of(t)
                    dve.tensor_scalar(xt[0:n, t, :], xt[0:n, t, :], rr[0:n, t:t + 1], None, ALU.mult).then_inc(xn_done, 1)
                dve.wait_ge(g_in, 16)
                for t in range(NT):
                    n = rows_of(t)
                    for h in range(2):
                        dve.wait_ge(turned, 2 * t + h + 1)
                        dve.tensor_tensor(hT[:, 4 * h:4 * h + 4, t * P:t * P + n], tb[h][:, :, 0:n],
                                          gm[:, 4 * h:4 * h + 4].unsqueeze(2).broadcast_to([P, 4, n]),
                                          ALU.mult).then_inc(hT_done, 1)

            @block.scalar
            def _(act):
                for b in range(2):
                    act.sem_inc(panel_used[b], 1)
                for slot in range(1, NB):
                    act.sem_inc(evac_done[slot], 1)
                act.wait_ge(ss_init, 1)
                for t in range(NT):
                    n = rows_of(t)
                    act.wait_ge(x_in[t], 16)
                    if t:
                        act.wait_ge(ss_done, t)
                    act.activation(sq[0:n, :], xt[0:n, t, :], ACT.Square, accum_out=ss[0:n, t:t + 1]).then_inc(ss_done, 1)
                act.wait_ge(mm_done[0], 1)
                act.activation(c.dt[:, 0:NPT, :], bank[0][:, 0:NPT * SH].rearrange("p (t h) -> p t h", h=SH), ACT.Copy)
                act.activation(c.dt[0:DEC, NPT, :], bank[0][0:DEC, NPT * SH:NT * SH], ACT.Copy).then_inc(evac_done[0], 1)

                def evacuate(kind, i, col, pairs, visits):
                    U = UNITS[kind]
                    f = {"z": ACT.Silu, "g": ACT.Sigmoid}.get(kind, ACT.Copy)
                    for j in range(2 * U):
                        slot, u = j % NB, j % U
                        chan = kind in ("qk", "xbc")
                        n, w = (P, TS) if chan else (rows_of(u), PANEL)
                        act.wait_ge(mm_done[slot], i * per_pair(kind) + (visits + j // NB + 1 + (slot == 0)))
                        act.wait_ge(stored[slot], (i * per_pair(kind) + (visits + j // NB + 1)) * 16)
                        act.activation(stg[slot][0:n, 0:w], bank[slot][0:n, 0:w], f).then_inc(evac_done[slot], 1)
                        if u == U - 1:
                            act.sem_inc(panel_used[j // U], 1)

                runs(act, evacuate)

            @block.tensor
            def _(pe):
                for t in range(NT):
                    n = rows_of(t)
                    pe.wait_ge(xn_done, t + 1)
                    for h in range(2):
                        if t:
                            pe.wait_ge(hT_done, 2 * (t - 1) + h + 1)
                        for k in range(4):
                            mm = pe.transpose(tb[h][:, k, 0:n], xt[0:n, t, (4 * h + k) * P:(4 * h + k + 1) * P],
                                              c.ident[0:n, 0:n])
                        mm.then_inc(turned, 1)
                pe.wait_ge(hT_done, 2 * NT)
                pe.wait_ge(wdt_in, 16)
                for t in range(NT):
                    n = rows_of(t)
                    for k in range(DK):
                        mm = pe.matmul(bank[0][0:n, t * SH:(t + 1) * SH], hT[:, k, t * P:t * P + n], wdt[:, k, :],
                                       start=(k == 0), stop=(k == DK - 1))
                mm.then_inc(mm_done[0], 1)

                def products(kind, i, col, pairs, visits):
                    U = UNITS[kind]
                    for b in range(2):
                        pe.wait_ge(panel_in[b], (i + (pairs + 1)) * 16)
                        for u in range(U):
                            j = b * U + u
                            slot = j % NB
                            pe.wait_ge(evac_done[slot], i * per_pair(kind) + (visits + j // NB + 1))
                            for k in range(DK):
                                if kind in ("qk", "xbc"):
                                    blk, sl = divmod(u, NSPLIT)
                                    mm = pe.matmul(bank[slot][:, 0:TS], wp[b][:, k, blk * P:(blk + 1) * P],
                                                   hT[:, k, sl * TS:(sl + 1) * TS], start=(k == 0), stop=(k == DK - 1))
                                else:
                                    n = rows_of(u)
                                    mm = pe.matmul(bank[slot][0:n, :], hT[:, k, u * P:u * P + n], wp[b][:, k, :],
                                                   start=(k == 0), stop=(k == DK - 1))
                            mm.then_inc(mm_done[slot], 1)

                runs(pe, products)


def build_distances(nc, negdist):
    with Stage(nc, "dist") as s:
        dist_i, dist_done = s.sem("dist_i"), s.sem("dist_done")
        iot = s.sb("iot", [P, SEQ], I32)
        with nc.Block() as block:

            @block.gpsimd
            def _(pool):
                pool.iota(iot[:], [[-1, SEQ]], base=SEQ - P, channel_multiplier=1).then_inc(dist_i, 1)

            @block.vector
            def _(dve):
                dve.wait_ge(dist_i, 1)
                dve.tensor_copy(negdist[:], iot[:]).then_inc(dist_done, 1)
                dve.wait_ge(dist_done, 1)
                dve.tensor_scalar(negdist[:], negdist[:], 4.0, None, ALU.mult).then_inc(dist_done, 1)
                dve.wait_ge(dist_done, 2)
                dve.scalar_tensor_tensor(out=negdist[:], in0=negdist[:], scalar=-1.0, in1=negdist[:],
                                         op0=ALU.mult, op1=ALU.min).then_inc(dist_done, 1)
                dve.wait_ge(dist_done, 3)
                dve.memset(negdist[0:CH, SEQ - CH:SEQ], NEG).then_inc(dist_done, 1)
                dve.wait_ge(dist_done, 4)


def differential_attention(nc, io, dr, c, negdist):
    SAMPLE = NPT
    STEPS = 2 * NT
    KC = PAST // P

    def groups(n):
        blocks = [(k, P) for k in range(n + 1)] if n < SAMPLE else [(k, P) for k in range(KC)] + [(KC, DEC)]
        return [blocks[g:g + 4] for g in range(0, len(blocks), 4)]

    jobs = [("k", 0, g) for g in range(4)]
    for m in range(1, STEPS + 1):
        jobs += [("w", m - 1, g) for g in range(len(groups((m - 1) % NT)))]
        if m == NT - 1:
            jobs += [("k", 1, g) for g in range(4)]
    assert len(jobs) % 2 == 0
    turn_of = {job: j for j, job in enumerate(jobs)}
    TURNS = len(jobs) // 2

    with Stage(nc, "attn") as s:
        qT = [s.sb(f"qT{b}", [P, T]) for b in range(2)]
        kT = [s.sb(f"kT{b}", [P, T]) for b in range(2)]
        vt = [s.sb(f"vt{b}", [P, NT, P]) for b in range(2)]
        kc = [s.sb(f"kc{b}", [P, KC, P]) for b in range(2)]
        vc = [s.sb(f"vc{b}", [P, KC, P]) for b in range(2)]
        kcT = [s.sb(f"kcT{b}", [P, PAST]) for b in range(2)]
        krow = [s.sb(f"krow{b}", [P, NT, P]) for b in range(2)]
        orow = [s.sb(f"orow{b}", [P, NT, P]) for b in range(2)]
        e = [[s.sb(f"e{j}{p}", [P, SEQ]) for p in range(2)] for j in range(2)]
        w = [s.sb(f"w{p}", [P, SEQ]) for p in range(2)]
        wT = [s.sb(f"wT{p}", [P, 4, P]) for p in range(2)]
        top = [s.sb(f"top{p}", [P, 2]) for p in range(2)]
        ntop = [s.sb(f"ntop{p}", [P, 2]) for p in range(2)]
        tot = [s.sb(f"tot{p}", [P, 2]) for p in range(2)]
        inv = [s.sb(f"inv{p}", [P, 2]) for p in range(2)]
        lv = s.sb("lv", [P, 4, AK])
        lp = s.sb("lp", [P, 2, AK])
        ld = s.sb("ld", [P, 2])
        le = s.sb("le", [P, 2])
        lam = s.sb("lam", [P, 1])
        S = [s.ps(f"S{j}", [P, SEQ]) for j in range(2)]
        tp = [s.ps(f"tp{p}", [P, 4, P]) for p in range(2)]
        ob = [s.ps(f"ob{p}", [P, 512]) for p in range(2)]

        lam_in, lam_step, lam_exp = s.sem("lam_in"), s.sem("lam_step"), s.sem("lam_exp")
        head_in, head_used, stored = s.sems("head_in", 2), s.sems("head_used", 2), s.sems("stored", 2)
        scored, biased, ntop_done, exp_done = s.sems("scored", 2), s.sems("biased", 2), s.sem("ntop_done"), s.sems("exp_done", 2)
        inv_done, scaled, w_done, slope_done = s.sem("inv_done"), s.sem("scaled"), s.sem("w_done"), s.sem("slope_done")
        turned, turn_out, o_done, o_out, gate = s.sems("turned", 2), s.sems("turn_out", 2), s.sem("o_done"), s.sem("o_out"), s.sem("gate")
        dve_gate, pe_gate = s.sem("dve_gate"), s.sem("pe_gate")

        def step_of(i, m, ahead=1):
            return i * STEPS + (m + ahead)

        def turn_val(i, j, ahead=1):
            return i * TURNS + (j // 2 + ahead)

        with nc.Block() as block:

            @block.gpsimd
            def _(pool):
                with pool.Fori(0, H // 2) as i:
                    for b in range(2):
                        pool.wait_ge(head_used[b], i + 1)
                        pool.sem_inc(gate, 1)
                        col = i * (2 * P) + b * P
                        pool.dma_start(qT[b][:], dr["chan"][bass.ds(col, P), :]).then_inc(head_in[b], 16)
                        pool.dma_start(kT[b][:], dr["chan"][bass.ds(col + C_K, P), :]).then_inc(head_in[b], 16)
                        cols = bass.ds(col, P)
                        pool.dma_start(vt[b][:, 0:NPT, :], io["v_prompt_out"].rearrange("(t p) c -> p t c", p=P)[:, :, cols]
                                       ).then_inc(head_in[b], 16)
                        pool.dma_start(vt[b][0:DEC, NPT, :], io["v_sample_out"][:, cols]).then_inc(head_in[b], 16)
                        pool.dma_start(kc[b][:], io["cache_k2"].rearrange("(t p) c -> p t c", p=P)[:, :, cols]
                                       ).then_inc(head_in[b], 16)
                        pool.dma_start(vc[b][:], io["cache_v2"].rearrange("(t p) c -> p t c", p=P)[:, :, cols]
                                       ).then_inc(head_in[b], 16)

            @block.sync
            def _(sp):
                for n, name in enumerate(("lam_q1", "lam_k1", "lam_q2", "lam_k2")):
                    sp.dma_start(lv[:, n, :], io[name].broadcast_to([P, AK])).then_inc(lam_in, 16)
                for b in range(2):
                    sp.sem_inc(stored[b], 64)
                with sp.Fori(0, H // 2) as i:
                    for b in range(2):
                        sp.wait_ge(o_out, step_of(i, NT * b + NT - 1, 3))
                        cols = bass.ds(i * (2 * P) + b * P, P)
                        sp.dma_start(io["k_prompt_out"].rearrange("(t p) c -> p t c", p=P)[:, :, cols],
                                     krow[b][:, 0:NPT, :]).then_inc(stored[b], 16)
                        sp.dma_start(io["k_sample_out"][:, cols], krow[b][0:DEC, NPT, :]).then_inc(stored[b], 16)
                        sp.dma_start(dr["att"][0:SEQ, :].rearrange("(t p) c -> p t c", p=P)[:, :, cols],
                                     orow[b][:, 0:NPT, :]).then_inc(stored[b], 16)
                        sp.dma_start(dr["att"][SEQ:T, cols], orow[b][0:DEC, NPT, :]).then_inc(stored[b], 16)
                for b in range(2):
                    sp.wait_ge(stored[b], 64 * (H // 2 + 1))

            @block.vector
            def _(dve):
                for j in range(2):
                    dve.sem_inc(biased[j], 1)
                dve.sem_inc(w_done, 2)
                dve.sem_inc(slope_done, 1)
                dve.wait_ge(lam_in, 64)
                lq = lv[:].rearrange("p (a b) k -> p a b k", b=2)
                dve.tensor_tensor(lp[:], lq[:, :, 0, :], lq[:, :, 1, :], ALU.mult).then_inc(lam_step, 1)
                dve.wait_ge(lam_step, 1)
                dve.tensor_reduce(ld[:], lp[:], AX_X, ALU.add).then_inc(lam_step, 1)
                dve.wait_ge(lam_exp, 1)
                dve.tensor_tensor(lam[:], le[:, 0:1], le[:, 1:2], ALU.subtract).then_inc(lam_step, 1)
                dve.wait_ge(lam_step, 3)
                dve.tensor_scalar(lam[:], lam[:], LAM_INIT, None, ALU.add).then_inc(lam_step, 1)
                dve.wait_ge(lam_step, 4)

                def shape_of(m):
                    n = m % NT
                    return (P, (n + 1) * P, SEQ - (n + 1) * P) if n < SAMPLE else (DEC, PAST + DEC, SEQ - P - PAST)

                def bias_and_max(i, m):
                    p = m % 2
                    r, W, off = shape_of(m)
                    dve.wait_ge(slope_done, i * 2 + (m // NT + 1))
                    dve.wait_ge(w_done, step_of(i, m))
                    for j in range(2):
                        hold(dve, dve_gate, scored[j], step_of(i, m))
                        dve.tensor_tensor_reduce(e[j][p][0:r, 0:W], S[j][0:r, 0:W], negdist[0:r, off:off + W], 1.0, -3.0e38,
                                                 ALU.add, ALU.max, top[p][0:r, j:j + 1]).then_inc(biased[j], 1)
                    for j in range(2):
                        dve.wait_ge(biased[j], step_of(i, m, 2))
                    dve.tensor_scalar(ntop[p][0:r, :], top[p][0:r, :], -AK ** -0.5, None, ALU.mult).then_inc(ntop_done, 1)

                def combine(i, m):
                    p = m % 2
                    r, W, _ = shape_of(m)
                    for j in range(2):
                        dve.wait_ge(exp_done[j], step_of(i, m))
                    dve.reciprocal(inv[p][0:r, :], tot[p][0:r, :]).then_inc(inv_done, 1)
                    dve.wait_ge(inv_done, step_of(i, m))
                    dve.tensor_scalar(e[1][p][0:r, 0:W], e[1][p][0:r, 0:W], inv[p][0:r, 1:2], lam[0:r, 0:1],
                                      ALU.mult, ALU.mult).then_inc(scaled, 1)
                    dve.wait_ge(scaled, step_of(i, m))
                    dve.wait_ge(o_done, step_of(i, m))
                    dve.scalar_tensor_tensor(out=w[p][0:r, 0:W], in0=e[0][p][0:r, 0:W], scalar=inv[p][0:r, 0:1],
                                             in1=e[1][p][0:r, 0:W], op0=ALU.mult, op1=ALU.subtract).then_inc(w_done, 1)

                with dve.Fori(0, H // 2) as i:
                    for m in range(STEPS + 1):
                        if m < STEPS:
                            bias_and_max(i, m)
                        if m % NT == NT - 1:
                            dve.tensor_scalar(negdist[:], negdist[:], 0.5, None, ALU.mult).then_inc(slope_done, 1)
                        if m:
                            combine(i, m - 1)

            @block.scalar
            def _(act):
                for b in range(2):
                    act.sem_inc(head_used[b], 1)
                    act.sem_inc(turn_out[b], 1)
                act.sem_inc(o_out, 2)
                act.wait_ge(lam_step, 2)
                act.activation(le[:], ld[:], ACT.Exp).then_inc(lam_exp, 1)

                def exps(i, m):
                    p = m % 2
                    r, W = (P, (m % NT + 1) * P) if m % NT < SAMPLE else (DEC, PAST + DEC)
                    act.wait_ge(ntop_done, step_of(i, m))
                    for j in range(2):
                        act.activation(e[j][p][0:r, 0:W], e[j][p][0:r, 0:W], ACT.Exp, bias=ntop[p][0:r, j:j + 1],
                                       scale=AK ** -0.5, accum_out=tot[p][0:r, j:j + 1]).then_inc(exp_done[j], 1)

                def weights_out(i, m):
                    r = P if m % NT < SAMPLE else DEC
                    for g, blocks in enumerate(groups(m % NT)):
                        j = turn_of["w", m, g]
                        act.wait_ge(turned[j % 2], turn_val(i, j))
                        act.wait_ge(o_done, step_of(i, m, 2))
                        full = [q for q in blocks if q[1] == P]
                        if full:
                            f = len(full)
                            act.activation(wT[j % 2][:, 0:f, 0:r], tp[j % 2][:, 0:f, 0:r], ACT.Copy).then_inc(turn_out[j % 2], 1)
                        else:
                            act.activation(wT[j % 2][0:DEC, 0, 0:r], tp[j % 2][0:DEC, 0, 0:r], ACT.Copy).then_inc(turn_out[j % 2], 1)

                def keys_out(i, b):
                    act.wait_ge(stored[b], (i + 1) * 64)
                    for g in range(4):
                        j = turn_of["k", b, g]
                        act.wait_ge(turned[j % 2], turn_val(i, j))
                        if g < 2:
                            a = act.activation(krow[b][:, 4 * g:4 * g + 4, :], tp[j % 2][:], ACT.Copy)
                        elif g == 2:
                            a = act.activation(krow[b][0:DEC, NPT, :], tp[j % 2][0:DEC, 0, :], ACT.Copy)
                        else:
                            a = act.activation(kcT[b][:].rearrange("p (t k) -> p t k", k=P), tp[j % 2][:], ACT.Copy)
                        a.then_inc(turn_out[j % 2], 1)

                def o_to_rows(i, m):
                    n, b = m % NT, m // NT
                    r = P if n < SAMPLE else DEC
                    act.wait_ge(o_done, step_of(i, m, 3))
                    act.activation(orow[b][0:r, n, :], ob[m % 2][0:r, 0:P], ACT.Copy).then_inc(o_out, 1)
                    if n == SAMPLE:
                        act.sem_inc(head_used[b], 1)

                with act.Fori(0, H // 2) as i:
                    keys_out(i, 0)
                    for m in range(STEPS + 2):
                        if m < STEPS:
                            exps(i, m)
                        if 1 <= m <= STEPS:
                            weights_out(i, m - 1)
                        if m == NT - 1:
                            keys_out(i, 1)
                        if m >= 2:
                            o_to_rows(i, m - 2)

            @block.tensor
            def _(pe):
                pe.sem_inc(o_done, 2)

                def keys_turned(i, b):
                    pe.wait_ge(head_in[b], (i + 1) * 96)
                    for g in range(4):
                        j = turn_of["k", b, g]
                        pe.wait_ge(turn_out[j % 2], turn_val(i, j))
                        out = tp[j % 2]
                        if g < 2:
                            for k in range(4):
                                t = pe.transpose(out[:, k, :], kT[b][:, (4 * g + k) * P:(4 * g + k + 1) * P], c.ident[:])
                        elif g == 2:
                            t = pe.transpose(out[0:DEC, 0, :], kT[b][:, SEQ:T], c.ident[:])
                        else:
                            for k in range(KC):
                                t = pe.transpose(out[:, k, :], kc[b][:, k, :], c.ident[:])
                        t.then_inc(turned[j % 2], 1)

                def scores(i, m):
                    b, n = m // NT, m % NT
                    for j in range(2):
                        hold(pe, pe_gate, biased[j], step_of(i, m))
                        half = slice(AK * j, AK * j + AK)
                        if n < SAMPLE:
                            W = (n + 1) * P
                            for k in range(0, W, 512):
                                x = min(W, k + 512)
                                mm = pe.matmul(S[j][:, k:x], qT[b][half, n * P:(n + 1) * P], kT[b][half, k:x],
                                               start=True, stop=True)
                        else:
                            jj = turn_of["k", b, 3]
                            hold(pe, pe_gate, turn_out[jj % 2], turn_val(i, jj, 2))
                            pe.matmul(S[j][0:DEC, 0:PAST], qT[b][half, SEQ:T], kcT[b][half, :], start=True, stop=True)
                            mm = pe.matmul(S[j][0:DEC, PAST:PAST + DEC], qT[b][half, SEQ:T], kT[b][half, SEQ:T],
                                           start=True, stop=True)
                        mm.then_inc(scored[j], 1)

                def weights_turned(i, m):
                    r = P if m % NT < SAMPLE else DEC
                    pe.wait_ge(w_done, step_of(i, m, 3))
                    for g, blocks in enumerate(groups(m % NT)):
                        j = turn_of["w", m, g]
                        hold(pe, pe_gate, turn_out[j % 2], turn_val(i, j))
                        for k, (blk, size) in enumerate(blocks):
                            t = pe.transpose(tp[j % 2][0:size, k, 0:r], w[m % 2][0:r, blk * P:blk * P + size],
                                             c.ident[0:r, 0:r])
                        t.then_inc(turned[j % 2], 1)

                def product(i, m):
                    b, n = m // NT, m % NT
                    r = P if n < SAMPLE else DEC
                    pe.wait_ge(o_out, step_of(i, m))
                    gs = groups(n)
                    for g, blocks in enumerate(gs):
                        j = turn_of["w", m, g]
                        hold(pe, pe_gate, turn_out[j % 2], turn_val(i, j, 2))
                        for k, (blk, size) in enumerate(blocks):
                            val = (vt[b][:, blk, :] if n < SAMPLE else vc[b][:, blk, :] if size == P
                                   else vt[b][0:DEC, NPT, :])
                            mm = pe.matmul(ob[m % 2][0:r, 0:P], wT[j % 2][0:size, k, 0:r], val,
                                           start=(g == 0 and k == 0), stop=(g == len(gs) - 1 and k == len(blocks) - 1))
                    mm.then_inc(o_done, 1)

                with pe.Fori(0, H // 2) as i:
                    keys_turned(i, 0)
                    scores(i, 0)
                    for m in range(STEPS + 1):
                        if m:
                            weights_turned(i, m - 1)
                        if m == NT - 1:
                            keys_turned(i, 1)
                        if m + 1 < STEPS:
                            scores(i, m + 1)
                        if m:
                            product(i, m - 1)


def attend(nc, io, dr, c):
    with Stage(nc, "bias") as s:
        negdist = s.sb("negdist", [P, SEQ])
        build_distances(nc, negdist)
        differential_attention(nc, io, dr, c, negdist)


def causal_convolution(nc, io, dr, c):
    BLOCKS = SCD // P
    RUNS = [("x", SIN // P), ("B", SG), ("C", SG)]
    PRE = SCONV - 1
    S0 = PRE + SEQ
    LEN = S0 + PRE + DEC
    OUT = LEN - PRE
    with Stage(nc, "conv") as s:
        taps = s.sb("taps", [(SCONV + 1) * BLOCKS, P])
        tapsT = s.sb("tapsT", [P, SCONV + 1, BLOCKS])
        past = s.sb("past", [PRE * BLOCKS, P])
        pastT = s.sb("pastT", [P, PRE, BLOCKS])
        tail = s.sb("tail", [P, 2, BLOCKS, PRE])
        tailr = s.sb("tailr", [P, 2, PRE, BLOCKS])
        tailT = s.sb("tailT", [PRE * BLOCKS, 2, P])
        xb = [s.sb(f"xb{b}", [P, LEN]) for b in range(2)]
        cv = [s.sb(f"cv{b}", [P, OUT]) for b in range(2)]
        ya = [s.sb(f"ya{b}", [P, OUT]) for b in range(2)]
        rows = [s.sb(f"rows{b}", [P, NT, P]) for b in range(2)]
        tp = [[s.ps(f"tp{b}{q}", [P, 4, P]) for q in range(3)] for b in range(2)]
        small = s.ps("small", [P, 512])

        taps_in, tail_in, small_turned, small_out, tail_regrouped = (s.sem(n) for n in ("taps_in", "tail_in", "small_turned", "small_out", "tail_regrouped"))
        xb_in, past_put, zeroed = s.sems("xb_in", 2), s.sems("past_put", 2), s.sem("zeroed")
        convolved, activated = s.sems("convolved", 2), s.sems("activated", 2)
        turned, rows_out = s.sems("turned", 2), s.sems("rows_out", 2)
        stored_rows, stored_chan, tail_stored, gate = s.sems("stored_rows", 2), s.sems("stored_chan", 2), s.sem("tail_stored"), s.sem("gate")

        def runs(eng, body):
            v = vr = vc = blk = 0
            for kind, n in RUNS:
                with eng.Fori(0, n // 2) as i:
                    body(kind, i, v, vr, vc, blk)
                v += n // 2
                vr += n // 2 if kind != "C" else 0
                vc += n // 2 if kind != "x" else 0
                blk += n

        with nc.Block() as block:

            @block.gpsimd
            def _(pool):
                for b in range(2):
                    pool.memset(xb[b][:, 0:PRE], 0.0).then_inc(zeroed, 1)
                pool.wait_ge(small_out, 2)

                def loads(kind, i, v, vr, vc, blk):
                    for b in range(2):
                        n = i * 2 + (blk + b)
                        hold(pool, gate, convolved[b], (i + (v + 1)) * 4)
                        row = i * (2 * P) + ((blk + b) * P + C_V)
                        pool.tensor_copy(xb[b][:, S0:S0 + PRE], pastT[:, :, bass.ds(n, 1)].rearrange("p r c -> p (r c)")).then_inc(past_put[b], 1)
                        pool.dma_start(xb[b][:, PRE:S0], dr["chan"][bass.ds(row, P), 0:SEQ]).then_inc(xb_in[b], 16)
                        pool.dma_start(xb[b][:, S0 + PRE:LEN], dr["chan"][bass.ds(row, P), SEQ:T]).then_inc(xb_in[b], 16)

                runs(pool, loads)

            @block.sync
            def _(sp):
                sp.dma_start(taps[0:SCONV * BLOCKS, :], io["conv_w"][0].rearrange("r (c p) -> (r c) p", p=P)).then_inc(taps_in, 16)
                sp.dma_start(taps[SCONV * BLOCKS:, :], io["conv_b"].rearrange("a (c p) -> (a c) p", p=P)).then_inc(taps_in, 16)
                sp.dma_start(past[:], io["state_conv"][0, 0].rearrange("r (c p) -> (r c) p", p=P)).then_inc(taps_in, 16)
                xbc = dr["chan"][C_V:C_V + SCD, :].rearrange("(c p) t -> p c t", p=P)
                sp.dma_start(tail[:, 0, :, :], xbc[:, :, SEQ - PRE:SEQ]).then_inc(tail_in, 16)
                sp.dma_start(tail[:, 1, :, :], xbc[:, :, T - PRE:T]).then_inc(tail_in, 16)
                sp.wait_ge(small_out, 4)
                for q, name in enumerate(("conv_prompt_out", "conv_sample_out")):
                    sp.dma_start(io[name].rearrange("r (c p) -> (r c) p", p=P), tailT[:, q, :]).then_inc(tail_stored, 16)
                for b in range(2):
                    sp.sem_inc(stored_rows[b], 32)
                    sp.sem_inc(stored_chan[b], 32)

                def stores(kind, i, v, vr, vc, blk):
                    for b in range(2):
                        if kind != "x":
                            row = i * (2 * P) + (blk + b - SIN // P) * P
                            sp.wait_ge(activated[b], i + (v + 2))
                            sp.dma_start(dr["bc"][bass.ds(row, P), 0:SEQ], ya[b][:, 0:SEQ]).then_inc(stored_chan[b], 16)
                            sp.dma_start(dr["bc"][bass.ds(row, P), SEQ:T], ya[b][:, S0:S0 + DEC]).then_inc(stored_chan[b], 16)
                        if kind != "C":
                            cols = bass.ds(i * (2 * P) + (blk + b) * P, P)
                            sp.wait_ge(rows_out[b], (i + (vr + 2)) * 3)
                            sp.dma_start(dr["xtok"][0:SEQ, :].rearrange("(t p) c -> p t c", p=P)[:, :, cols],
                                         rows[b][:, 0:NPT, :]).then_inc(stored_rows[b], 16)
                            sp.dma_start(dr["xtok"][SEQ:T, cols], rows[b][0:DEC, NPT, :]).then_inc(stored_rows[b], 16)

                runs(sp, stores)
                sp.wait_ge(tail_stored, 32)
                for b in range(2):
                    sp.wait_ge(stored_rows[b], 32 * (1 + (SIN // P + SG) // 2))
                    sp.wait_ge(stored_chan[b], 32 * (1 + SG))

            @block.vector
            def _(dve):
                for b in range(2):
                    dve.sem_inc(convolved[b], 4)
                dve.wait_ge(tail_in, 32)
                for q in range(2):
                    dve.tensor_copy(tailr[:, q, :, :], tail[:, q, :, :].rearrange("p c r -> p r c")).then_inc(tail_regrouped, 1)
                dve.wait_ge(zeroed, 2)
                dve.wait_ge(small_out, 2)

                def convolve(kind, i, v, vr, vc, blk):
                    for b in range(2):
                        n = i * 2 + (blk + b)
                        base = (i + (v + 1)) * 4

                        def tap(k):
                            return tapsT[:, k, bass.ds(n, 1)]

                        dve.wait_ge(xb_in[b], (i + (v + 1)) * 32)
                        dve.wait_ge(past_put[b], i + (v + 1))
                        dve.wait_ge(activated[b], i + (v + 1))
                        dve.tensor_scalar(cv[b][:], xb[b][:, PRE:LEN], tap(PRE), tap(SCONV), ALU.mult, ALU.add).then_inc(convolved[b], 1)
                        for k in range(PRE):
                            dve.wait_ge(convolved[b], base + (k + 1))
                            dve.scalar_tensor_tensor(out=cv[b][:], in0=xb[b][:, k:k + OUT], scalar=tap(k), in1=cv[b][:],
                                                     op0=ALU.mult, op1=ALU.add).then_inc(convolved[b], 1)

                runs(dve, convolve)

            @block.scalar
            def _(act):
                for b in range(2):
                    act.sem_inc(activated[b], 1)
                    act.sem_inc(rows_out[b], 3)
                act.wait_ge(small_turned, 4)
                act.activation(tapsT[:].rearrange("p r c -> p (r c)"), small[:, 0:(SCONV + 1) * BLOCKS], ACT.Copy).then_inc(small_out, 1)
                act.activation(pastT[:].rearrange("p r c -> p (r c)"), small[:, P:P + PRE * BLOCKS], ACT.Copy).then_inc(small_out, 1)
                for q in range(2):
                    act.activation(tailT[:, q, :], small[0:PRE * BLOCKS, (2 + q) * P:(3 + q) * P], ACT.Copy).then_inc(small_out, 1)

                def activate(kind, i, v, vr, vc, blk):
                    for b in range(2):
                        act.wait_ge(convolved[b], (i + (v + 2)) * 4)
                        act.wait_ge(turned[b], i * (3 if kind != "C" else 0) + (vr + 1) * 3)
                        act.wait_ge(stored_chan[b], i * (32 if kind != "x" else 0) + (vc + 1) * 32)
                        act.activation(ya[b][:], cv[b][:], ACT.Silu).then_inc(activated[b], 1)
                    for b in range(2):
                        if kind == "C":
                            continue
                        act.wait_ge(stored_rows[b], (i + (vr + 1)) * 32)
                        for q in range(3):
                            act.wait_ge(turned[b], i * 3 + (vr * 3 + q + 4))
                            if q < 2:
                                a = act.activation(rows[b][:, 4 * q:4 * q + 4, :], tp[b][q][:], ACT.Copy)
                            else:
                                a = act.activation(rows[b][0:DEC, NPT, :], tp[b][q][0:DEC, 0, :], ACT.Copy)
                            a.then_inc(rows_out[b], 1)

                runs(act, activate)

            @block.tensor
            def _(pe):
                for b in range(2):
                    pe.sem_inc(turned[b], 3)
                pe.wait_ge(taps_in, 48)
                n = (SCONV + 1) * BLOCKS
                pe.transpose(small[:, 0:n], taps[:], c.ident[0:n, 0:n]).then_inc(small_turned, 1)
                n = PRE * BLOCKS
                pe.transpose(small[:, P:P + n], past[:], c.ident[0:n, 0:n]).then_inc(small_turned, 1)
                for q in range(2):
                    pe.wait_ge(tail_regrouped, q + 1)
                    pe.transpose(small[0:n, (2 + q) * P:(3 + q) * P], tailr[:, q, :, :].rearrange("p r c -> p (r c)"),
                                 c.ident[:]).then_inc(small_turned, 1)

                def turn(kind, i, v, vr, vc, blk):
                    if kind == "C":
                        return
                    for b in range(2):
                        pe.wait_ge(activated[b], i + (v + 2))
                        for q in range(3):
                            pe.wait_ge(rows_out[b], i * 3 + (vr * 3 + q + 1))
                            if q < 2:
                                for k in range(4):
                                    t = pe.transpose(tp[b][q][:, k, :], ya[b][:, (4 * q + k) * P:(4 * q + k + 1) * P], c.ident[:])
                            else:
                                t = pe.transpose(tp[b][q][0:DEC, 0, :], ya[b][:, S0:S0 + DEC], c.ident[:])
                            t.then_inc(turned[b], 1)

                runs(pe, turn)


def step_sizes(nc, io, c, m):
    with Stage(nc, "dt") as s:
        W = [P, NT, SH]
        bias, alog = s.sb("bias", [P, SH]), s.sb("alog", [P, SH])
        z, e, u, ln, d0, one, acum = (s.sb(n, W) for n in ("z", "e", "u", "ln", "d0", "one", "acum"))
        cum, last = s.ps("cum", [P, 512]), s.ps("last", [P, 512])
        vec_in, v, a, p = s.sem("vec_in"), s.sem("dve_step"), s.sem("act_step"), s.sem("pe_step")

        def wide(x):
            return x[:].unsqueeze(1).broadcast_to(W)

        def flat(x):
            return x[:].rearrange("p t h -> p (t h)")

        cums, lasts = cum[:, 0:NT * SH], last[:, 0:NT * SH]
        with nc.Block() as block:

            @block.sync
            def _(sp):
                sp.dma_start(bias[:], io["dt_bias"].broadcast_to([P, SH])).then_inc(vec_in, 16)
                sp.dma_start(alog[:], io["a_log"].broadcast_to([P, SH])).then_inc(vec_in, 16)

            @block.vector
            def _(dve):
                count = [0]

                def step(ins):
                    ins.then_inc(v, 1)
                    count[0] += 1
                    dve.wait_ge(v, count[0])

                dve.wait_ge(vec_in, 32)
                step(dve.tensor_tensor(z[:], c.dt[:], wide(bias), ALU.add))
                step(dve.scalar_tensor_tensor(out=flat(e), in0=flat(z), scalar=-1.0, in1=flat(z), op0=ALU.mult, op1=ALU.min))
                dve.wait_ge(a, 1)
                step(dve.tensor_scalar(u[:], e[:], 1.0, None, ALU.add))
                step(dve.tensor_scalar(d0[:], u[:], -1.0, None, ALU.add))
                step(dve.tensor_scalar(one[:], d0[:], 0.0, None, ALU.is_equal))
                step(dve.tensor_tensor(d0[:], d0[:], one[:], ALU.add))
                step(dve.reciprocal(d0[:], d0[:]))
                step(dve.tensor_tensor(d0[:], d0[:], e[:], ALU.mult))
                dve.wait_ge(a, 2)
                step(dve.tensor_tensor(ln[:], ln[:], one[:], ALU.add))
                step(dve.tensor_tensor(ln[:], ln[:], d0[:], ALU.mult))
                step(dve.scalar_tensor_tensor(out=flat(c.dt), in0=flat(z), scalar=0.0, in1=flat(ln), op0=ALU.max, op1=ALU.add))
                step(dve.memset(c.dt[DEC:2 * DEC, NPT, :], 0.0))
                step(dve.memset(c.dt[2 * DEC:P, NPT, :], 0.0))
                dve.wait_ge(a, 3)
                step(dve.tensor_scalar(alog[:], alog[:], -1.0, None, ALU.mult))
                step(dve.tensor_tensor(m.da[:], c.dt[:], wide(alog), ALU.mult))
                assert count[0] == 15
                dve.wait_ge(p, 3)
                dve.wait_ge(a, 5)
                step(dve.tensor_copy(flat(acum), cums))
                step(dve.tensor_tensor(flat(acum), lasts, flat(acum), ALU.subtract))
                dve.wait_ge(a, 6)
                step(dve.tensor_tensor(m.wdec[:], m.wdec[:], c.dt[:], ALU.mult))

            @block.scalar
            def _(act):
                act.wait_ge(v, 2)
                act.activation(e[:], e[:], ACT.Exp).then_inc(a, 1)
                act.wait_ge(v, 3)
                act.activation(ln[:], u[:], ACT.Ln).then_inc(a, 1)
                act.wait_ge(vec_in, 32)
                act.activation(alog[:], alog[:], ACT.Exp).then_inc(a, 1)
                act.wait_ge(p, 3)
                act.activation(flat(m.ecum), cums, ACT.Exp).then_inc(a, 1)
                act.activation(flat(m.elast), lasts, ACT.Exp).then_inc(a, 1)
                act.wait_ge(v, 17)
                act.activation(m.wdec[:], acum[:], ACT.Exp).then_inc(a, 1)

            @block.tensor
            def _(pe):
                pe.wait_ge(v, 15)
                pe.matmul(cums, c.upper[:], flat(m.da), start=True, stop=True).then_inc(p, 1)
                pe.matmul(last[:, 0:NPT * SH], c.ones[:], m.da[:, 0:NPT, :].rearrange("p t h -> p (t h)"),
                          start=True, stop=True).then_inc(p, 1)
                pe.matmul(last[:, NPT * SH:NT * SH], c.ones[0:DEC, :], m.da[0:DEC, NPT, :], start=True, stop=True).then_inc(p, 1)


def state_in(nc, src, m, c):
    with Stage(nc, "hin") as s:
        raw = s.sb("raw", [P, SIN // P, P])
        tp = [s.ps(f"tp{q}", [P, 4, P]) for q in range(4)]
        raw_in, turned, out = s.sem("raw_in"), s.sem("turned"), s.sem("out")
        with nc.Block() as block:

            @block.gpsimd
            def _(pool):
                pool.dma_start(raw[:], src.rearrange("(b p) n -> p b n", p=P)).then_inc(raw_in, 16)

            @block.tensor
            def _(pe):
                pe.wait_ge(raw_in, 16)
                for q in range(4):
                    for k in range(4):
                        t = pe.transpose(tp[q][:, k, :], raw[:, 4 * q + k, :], c.ident[:])
                    t.then_inc(turned, 1)

            @block.vector
            def _(dve):
                for q in range(4):
                    dve.wait_ge(turned, q + 1)
                    dve.tensor_copy(m.state[:, 512 * q:512 * q + 512], tp[q][:].rearrange("p k n -> p (k n)")).then_inc(out, 1)


def state_out(nc, dst, m, c, tag):
    with Stage(nc, tag) as s:
        raw = s.sb("raw", [P, SIN // P, P])
        tp = [s.ps(f"tp{q}", [P, 4, P]) for q in range(4)]
        turned, out, stored = s.sem("turned"), s.sem("out"), s.sem("stored")
        with nc.Block() as block:

            @block.tensor
            def _(pe):
                for q in range(4):
                    for k in range(4):
                        t = pe.transpose(tp[q][:, k, :], m.state[:, (4 * q + k) * P:(4 * q + k + 1) * P], c.ident[:])
                    t.then_inc(turned, 1)

            @block.vector
            def _(dve):
                for q in range(4):
                    dve.wait_ge(turned, q + 1)
                    dve.tensor_copy(raw[:, 4 * q:4 * q + 4, :], tp[q][:]).then_inc(out, 1)

            @block.sync
            def _(sp):
                sp.wait_ge(out, 4)
                sp.dma_start(dst.rearrange("(b p) n -> p b n", p=P), raw[:]).then_inc(stored, 16)
                sp.wait_ge(stored, 16)


def ssd_scan(nc, io, dr, c, m, sample):
    G = SG
    GH = SH // SG
    GW = GH * SP_
    r = DEC if sample else P
    TL = r
    PAIRS = 1 if sample else NPT // 2
    BODY = 1 if sample else 2
    with Stage(nc, "ssds" if sample else "ssdp") as s:
        xt = [s.sb(f"xt{b}", [P, SIN + G * SN]) for b in range(2)]
        bc = [s.sb(f"bc{b}", [P, 2 * G, TL]) for b in range(2)]
        zt = [s.sb(f"zt{b}", [P, SIN]) for b in range(2)]
        R = [s.sb(f"R{q}", [P, GH, TL]) for q in range(2)]
        L = [s.sb(f"L{q}", [P, GH, TL]) for q in range(2)]
        M = [s.sb(f"M{g}", [P, GH, TL]) for g in range(G)]
        cbm = s.sb("cbm", [P, G, TL])
        dtx, dx, wx = s.sb("dtx", [P, SIN]), s.sb("dx", [P, SIN]), s.sb("wx", [P, SIN])
        carried = s.sb("carried", [P, GW])
        y = [s.sb(f"y{b}", [P, SIN]) for b in range(2)]
        yn = [s.sb(f"yn{b}", [P, SIN]) for b in range(2)]
        ss, ms, rr = (s.sb(n, [P, G]) for n in ("ss", "ms", "rr"))
        skip = s.sb("skip", [P, SH])
        seg = [s.ps(f"seg{q}", [P, GH * TL if not sample else 1024]) for q in range(2)]
        cb, yp, yi, hs = (s.ps(n, [P, 512]) for n in ("cb", "yp", "yi", "hs"))

        pe_gate, pool_gate = s.sem("pe_gate"), s.sem("pool_gate")
        skip_in, tile_in, tile_used, yn_stored = s.sem("skip_in"), s.sems("tile_in", 2), s.sems("tile_used", 2), s.sems("yn_stored", 2)
        R_done, seg_done, L_done, M_done = s.sem("R_done"), s.sem("seg_done"), s.sem("L_done"), s.sem("M_done")
        cb_done, cbm_done, dtx_done, dx_done, wx_done = (s.sem(n) for n in ("cb_done", "cbm_done", "dtx_done", "dx_done", "wx_done"))
        yi_done, yp_done, y_step, hs_done, h_step = (s.sem(n) for n in ("yi_done", "yp_done", "y_step", "hs_done", "h_step"))
        ss_done, ms_done, rr_done, yn_done, state_zero = (s.sem(n) for n in ("ss_done", "ms_done", "rr_done", "yn_done", "state_zero"))

        def tiles(eng, body):
            if sample:
                body(0, 0)
            else:
                with eng.Fori(0, PAIRS) as i:
                    for b in range(BODY):
                        body(i, b)

        def val(i, b, per, ahead):
            return i * (BODY * per) + (b * per + ahead)

        def cols(i, b):
            return slice(NPT, NT) if sample else bass.ds(i * 2 + b, 1)

        def tok(i, b):
            return slice(SEQ, T) if sample else bass.ds(i * (2 * P) + b * P, P)

        def by_head(x, i, b, width, g0=0, g1=SH):
            return x[0:r, cols(i, b), g0:g1].rearrange("p t h -> p (t h)").unsqueeze(2).broadcast_to([r, g1 - g0, width])

        def heads(x):
            return x.rearrange("p (h q) -> p h q", q=SP_)

        def of_group(g):
            return slice(g * GW, (g + 1) * GW)

        with nc.Block() as block:

            @block.sync
            def _(sp):
                sp.dma_start(skip[:], io["d_skip"].broadcast_to([P, SH])).then_inc(skip_in, 16)

                def loads(i, b):
                    sp.wait_ge(tile_used[b], i + 1)
                    sp.dma_start(xt[b][0:r, :], dr["xtok"][tok(i, b), :]).then_inc(tile_in[b], 16)
                    sp.dma_start(bc[b][:], dr["bc"].rearrange("(g p) t -> p g t", p=P)[:, :, tok(i, b)]).then_inc(tile_in[b], 16)
                    sp.dma_start(zt[b][0:r, :], dr["zs"][tok(i, b), :]).then_inc(tile_in[b], 16)

                tiles(sp, loads)
                for b in range(BODY):
                    sp.wait_ge(yn_stored[b], 16 * (PAIRS + 1))

            @block.gpsimd
            def _(pool):
                pool.wait_ge(skip_in, 16)

                def tile(i, b):
                    pool.wait_ge(tile_in[b], (i + 1) * 48)
                    pool.wait_ge(h_step, val(i, b, 5, 5))
                    pool.tensor_tensor(heads(dx[0:r, :]), heads(xt[b][0:r, 0:SIN]),
                                       skip[0:r, :].unsqueeze(2).broadcast_to([r, SH, SP_]), ALU.mult).then_inc(dx_done, 1)
                    pool.tensor_tensor(heads(wx[0:r, :]), heads(xt[b][0:r, 0:SIN]), by_head(m.wdec, i, b, SP_), ALU.mult).then_inc(wx_done, 1)
                    hold(pool, pool_gate, ss_done, val(i, b, G, G))
                    pool.tensor_scalar(ms[0:r, :], ss[0:r, :], 1.0 / GW, EPS, ALU.mult, ALU.add).then_inc(ms_done, 1)
                    pool.wait_ge(ms_done, val(i, b, 1, 1))
                    pool.tensor_tensor(rr[0:r, :], ms[0:r, :], c.neghalf[0:r, 0:G], ALU.pow).then_inc(rr_done, 1)

                tiles(pool, tile)

            @block.scalar
            def _(act):
                act.sem_inc(L_done, 2)
                act.sem_inc(yn_done, 2 * G)
                for b in range(BODY):
                    act.sem_inc(yn_stored[b], 16)

                def tile(i, b):
                    for g in range(G):
                        act.wait_ge(seg_done, val(i, b, G, g + 3))
                        act.wait_ge(M_done, val(i, b, G, g + 1))
                        act.activation(L[g % 2][0:r], seg[g % 2][0:r, 0:GH * TL].rearrange("p (h l) -> p h l", h=GH),
                                       ACT.Exp).then_inc(L_done, 1)
                    act.wait_ge(yn_stored[b], (i + 1) * 16)
                    for g in range(G):
                        act.wait_ge(y_step, val(i, b, 4 * G, 4 * g + 8))
                        act.activation(yn[b][0:r, of_group(g)], y[b][0:r, of_group(g)], ACT.Square, accum_out=ss[0:r, g:g + 1]).then_inc(ss_done, 1)
                    act.wait_ge(rr_done, val(i, b, 1, 1))
                    for g in range(G):
                        act.activation(yn[b][0:r, of_group(g)], y[b][0:r, of_group(g)], ACT.Copy,
                                       scale=rr[0:r, g:g + 1]).then_inc(yn_done, 1)
                    act.wait_ge(yn_done, val(i, b, G, 3 * G))
                    act.dma_start(dr["yg"][tok(i, b), :], yn[b][0:r, :]).then_inc(yn_stored[b], 16)

                tiles(act, tile)

            @block.vector
            def _(dve):
                dve.sem_inc(M_done, 2)
                dve.sem_inc(cbm_done, 1)
                dve.sem_inc(y_step, 4)
                dve.sem_inc(h_step, 5)
                if not sample:
                    dve.memset(m.state[:], 0.0).then_inc(state_zero, 1)
                    dve.wait_ge(state_zero, 1)
                for b in range(BODY):
                    dve.sem_inc(tile_used[b], 1)

                def tile(i, b):
                    def decays(g):
                        dve.wait_ge(seg_done, val(i, b, G, g + 1))
                        dve.tensor_tensor(R[g % 2][0:r], by_head(m.da, i, b, TL, g * GH, (g + 1) * GH),
                                          c.upper[0:r, 0:TL].unsqueeze(1).broadcast_to([r, GH, TL]), ALU.mult).then_inc(R_done, 1)

                    def mix(g):
                        dve.wait_ge(L_done, val(i, b, G, g + 3))
                        dve.tensor_tensor(M[g][0:r], L[g % 2][0:r], cbm[0:r, g, :].unsqueeze(1).broadcast_to([r, GH, TL]),
                                          ALU.mult).then_inc(M_done, 1)

                    def output(g):
                        own = val(i, b, 4 * G, 4 * g + 4)
                        dve.wait_ge(yi_done, val(i, b, G, g + 1))
                        dve.tensor_tensor(heads(carried[0:r, :]), heads(yi[0:r, 0:GW]), by_head(m.ecum, i, b, SP_, g * GH, (g + 1) * GH),
                                          ALU.mult).then_inc(y_step, 1)
                        dve.wait_ge(y_step, own + 1)
                        dve.wait_ge(yp_done, val(i, b, G, g + 1))
                        dve.wait_ge(yn_done, val(i, b, G, G))
                        dve.tensor_tensor(y[b][0:r, of_group(g)], yp[0:r, 0:GW], carried[0:r, :], ALU.add).then_inc(y_step, 1)
                        dve.wait_ge(y_step, own + 2)
                        dve.wait_ge(dx_done, val(i, b, 1, 1))
                        dve.tensor_tensor(y[b][0:r, of_group(g)], y[b][0:r, of_group(g)], dx[0:r, of_group(g)], ALU.add).then_inc(y_step, 1)
                        dve.wait_ge(y_step, own + 3)
                        dve.tensor_tensor(y[b][0:r, of_group(g)], y[b][0:r, of_group(g)], zt[b][0:r, of_group(g)], ALU.mult).then_inc(y_step, 1)

                    dve.wait_ge(tile_in[b], (i + 1) * 48)
                    decays(0)
                    decays(1)
                    dve.wait_ge(cb_done, val(i, b, 1, 1))
                    dve.tensor_tensor(cbm[0:r], cb[0:r, 0:G * TL].rearrange("p (g l) -> p g l", g=G),
                                      c.upper[0:r, 0:TL].unsqueeze(1).broadcast_to([r, G, TL]), ALU.mult).then_inc(cbm_done, 1)
                    dve.tensor_tensor(heads(dtx[0:r, :]), heads(xt[b][0:r, 0:SIN]), by_head(c.dt, i, b, SP_), ALU.mult).then_inc(dtx_done, 1)
                    dve.wait_ge(cbm_done, val(i, b, 1, 2))
                    mix(0)
                    decays(2)
                    mix(1)
                    decays(3)
                    mix(2)
                    output(0)
                    mix(3)
                    output(1)
                    output(2)
                    output(3)
                    elast = m.elast[:, cols(i, b), :].rearrange("p t h -> p (t h)").unsqueeze(2).broadcast_to([P, SH, SP_])
                    dve.tensor_tensor(heads(m.state[:]), heads(m.state[:]), elast, ALU.mult).then_inc(h_step, 1)
                    dve.wait_ge(h_step, val(i, b, 5, 6))
                    for g in range(G):
                        dve.wait_ge(hs_done, val(i, b, G, g + 1))
                        dve.tensor_tensor(m.state[:, of_group(g)], m.state[:, of_group(g)], hs[:, 0:GW], ALU.add).then_inc(h_step, 1)
                    dve.wait_ge(h_step, val(i, b, 5, 10))
                    dve.sem_inc(tile_used[b], 1)

                tiles(dve, tile)

            @block.tensor
            def _(pe):
                pe.sem_inc(seg_done, 2)

                def tile(i, b):
                    def decay_sums(g):
                        pe.wait_ge(R_done, val(i, b, G, g + 1))
                        hold(pe, pe_gate, L_done, val(i, b, G, g + 1))
                        flat = R[g % 2][0:r].rearrange("p h l -> p (h l)")
                        for k in range(0, GH * TL, 512):
                            x = min(k + 512, GH * TL)
                            mm = pe.matmul(seg[g % 2][0:r, k:x], c.below[0:r, 0:r], flat[:, k:x], start=True, stop=True)
                        mm.then_inc(seg_done, 1)

                    def from_state(g):
                        hold(pe, pe_gate, y_step, val(i, b, 4 * G, 4 * g + 1))
                        pe.matmul(yi[0:r, 0:GW], bc[b][:, G + g, :], m.state[:, of_group(g)], start=True, stop=True).then_inc(yi_done, 1)

                    def within(g):
                        pe.wait_ge(M_done, val(i, b, G, g + 3))
                        hold(pe, pe_gate, y_step, val(i, b, 4 * G, 4 * g + 2))
                        for h in range(GH):
                            at = (g * GH + h) * SP_
                            mm = pe.matmul(yp[0:r, h * SP_:(h + 1) * SP_], M[g][0:r, h, :], dtx[0:r, at:at + SP_], start=True, stop=True)
                        mm.then_inc(yp_done, 1)

                    pe.wait_ge(tile_in[b], (i + 1) * 48)
                    hold(pe, pe_gate, cbm_done, val(i, b, 1, 1))
                    for g in range(G):
                        mm = pe.matmul(cb[0:r, g * TL:(g + 1) * TL], bc[b][:, g, :], bc[b][:, G + g, :], start=True, stop=True)
                    mm.then_inc(cb_done, 1)
                    decay_sums(0)
                    decay_sums(1)
                    pe.wait_ge(h_step, val(i, b, 5, 5))
                    from_state(0)
                    pe.wait_ge(dtx_done, val(i, b, 1, 1))
                    within(0)
                    decay_sums(2)
                    decay_sums(3)
                    for g in range(1, G):
                        from_state(g)
                        within(g)
                    pe.wait_ge(wx_done, val(i, b, 1, 1))
                    for g in range(G):
                        hold(pe, pe_gate, h_step, val(i, b, 5, g + 6 if g else 5))
                        pe.matmul(hs[:, 0:GW], xt[b][0:r, SIN + g * SN:SIN + (g + 1) * SN], wx[0:r, of_group(g)],
                                  start=True, stop=True).then_inc(hs_done, 1)

                tiles(pe, tile)


class SsmHeld:

    def __init__(self, s):
        self.da, self.ecum, self.elast, self.wdec = (s.sb(n, [P, NT, SH]) for n in ("da", "ecum", "elast", "wdec"))
        self.state = s.sb("state", [P, SIN])


def state_space(nc, io, dr, c):
    with Stage(nc, "ssm") as s:
        m = SsmHeld(s)
        step_sizes(nc, io, c, m)
        ssd_scan(nc, io, dr, c, m, sample=False)
        state_out(nc, io["ssm_prompt_out"], m, c, "houtp")
        state_in(nc, io["state_ssm"][0, 0].rearrange("h p n -> (h p) n"), m, c)
        ssd_scan(nc, io, dr, c, m, sample=True)
        state_out(nc, io["ssm_sample_out"], m, c, "houts")


def over_tiles(eng, step):
    step(0, 0, 0, P, P)
    with eng.Fori(0, (NPT - 2) // 2) as i:
        step(i * 2 + 1, i, 1, P, P)
        step(i * 2 + 2, i + 1, 0, P, P)
    step(NPT - 1, NPT // 2 - 1, 1, P, DEC)
    step(NPT, NPT // 2, 0, DEC, None)


def tokens(t, r):
    return slice(SEQ, T) if r == DEC else bass.ds(t * P, P)


def mix_branches(nc, io, dr, c):
    OT, YT = D // P, SIN // P
    HALF = 512
    OY = 2 + 4
    with Stage(nc, "mix") as s:
        wa, ws, wo = s.sb("wa", [P, OT, D]), s.sb("ws", [P, YT, D]), s.sb("wo", [P, OT, D])
        gsub, gssm = s.sb("gsub", [P, 1]), s.sb("gssm", [P, YT])
        ot = s.sb("ot", [P, D])
        yt = s.sb("yt", [P, SIN])
        gt = [s.sb(f"gt{b}", [P, 2 * D]) for b in range(2)]
        xt = [s.sb(f"xt{b}", [P, D]) for b in range(2)]
        sq = s.sb("sq", [P, D])
        oT, yT, sT = s.sb("oT", [P, OT, P]), s.sb("yT", [P, YT, P]), s.sb("sT", [P, OT, P])
        ss, ms, rr = (s.sb(n, [P, H]) for n in ("ss", "ms", "rr"))
        tb = [s.ps(f"tb{q}", [P, 4, P]) for q in range(2)]
        oa, os_, xo = (s.ps(n, [P, D]) for n in ("oa", "os", "xo"))

        w_in, g_in, weighted = s.sems("w_in", 3), s.sem("g_in"), s.sem("weighted")
        o_in, y_in, gt_in, xt_in, x1_stored = s.sem("o_in"), s.sem("y_in"), s.sems("gt_in", 2), s.sems("xt_in", 2), s.sems("x1_stored", 2)
        squared, summed, ms_done, rr_done, o_normed = (s.sem(n) for n in ("squared", "summed", "ms_done", "rr_done", "o_normed"))
        oy_turned, oy_out, s_turned, s_out = (s.sem(n) for n in ("oy_turned", "oy_out", "s_turned", "s_out"))
        projected, gated, multiplied, added = (s.sem(n) for n in ("projected", "gated", "multiplied", "added"))
        pe_gate, pool_gate = s.sem("pe_gate"), s.sem("pool_gate")

        with nc.Block() as block:

            @block.sync
            def _(sp):
                sp.dma_start(gsub[:], io["attn_subln_g"].rearrange("a p -> p a"), allow_slow_non_contiguous=True).then_inc(g_in, 16)
                sp.dma_start(gssm[:], io["ssm_norm_g"].rearrange("a (k p) -> p (a k)", p=P), allow_slow_non_contiguous=True).then_inc(g_in, 16)
                for dst, name, q in ((wa, "w_attn_o", 0), (ws, "w_ssm_o", 1), (wo, "w_out", 2)):
                    sp.dma_start(dst[:], io[name][0].rearrange("(k p) n -> p k n", p=P)).then_inc(w_in[q], 16)

                def store(t, k, b, r, nxt):
                    sp.wait_ge(added, t + 2)
                    sp.dma_start(dr["x1"][tokens(t, r), :], xt[b][0:r, :]).then_inc(x1_stored[b], 16)

                over_tiles(sp, store)
                for b in range(2):
                    sp.wait_ge(x1_stored[b], 16 * (NT // 2 + 2 - b))

            @block.gpsimd
            def _(pool):
                for b in range(2):
                    pool.sem_inc(x1_stored[b], 16)

                def tile(t, k, b, r, nxt):
                    rows = tokens(t, r)
                    x = io["x_sample"][0] if r == DEC else io["x_prompt"][0, rows, :]
                    hold(pool, pool_gate, oy_turned, t * OY + 2)
                    pool.dma_start(ot[0:r, :], dr["att"][rows, :]).then_inc(o_in, 16)
                    hold(pool, pool_gate, oy_turned, t * OY + OY)
                    pool.dma_start(yt[0:r, :], dr["yg"][rows, :]).then_inc(y_in, 16)
                    hold(pool, pool_gate, ms_done, t + 1)
                    pool.tensor_tensor(rr[0:r, :], ms[0:r, :], c.neghalf[0:r, 0:H], ALU.pow).then_inc(rr_done, 1)
                    hold(pool, pool_gate, x1_stored[b], (k + 1) * 16)
                    pool.dma_start(xt[b][0:r, :], x).then_inc(xt_in[b], 16)
                    hold(pool, pool_gate, s_turned, t * 2 + 2)
                    pool.dma_start(gt[b][0:r, :], dr["gs"][rows, :]).then_inc(gt_in[b], 16)

                over_tiles(pool, tile)

            @block.vector
            def _(dve):
                dve.sem_inc(gated, 3)
                dve.sem_inc(added, 1)
                dve.sem_inc(o_normed, 1)
                dve.wait_ge(g_in, 32)
                dve.wait_ge(w_in[0], 16)
                dve.tensor_scalar(wa[:].rearrange("p k n -> p (k n)"), wa[:].rearrange("p k n -> p (k n)"), gsub[:, 0:1],
                                  1.0 - LAM_INIT, ALU.mult, ALU.mult).then_inc(weighted, 1)
                dve.wait_ge(w_in[1], 16)
                for k in range(YT):
                    dve.tensor_scalar(ws[:, k, :], ws[:, k, :], gssm[:, k:k + 1], None, ALU.mult).then_inc(weighted, 1)

                def norm(t, r):
                    dve.wait_ge(squared, t + 1)
                    dve.tensor_reduce(ss[0:r, :], sq[0:r, :].rearrange("p (h v) -> p h v", h=H), AX_X, ALU.add).then_inc(summed, 1)
                    dve.wait_ge(summed, t + 1)
                    dve.tensor_scalar(ms[0:r, :], ss[0:r, :], 1.0 / P, EPS, ALU.mult, ALU.add).then_inc(ms_done, 1)
                    dve.wait_ge(rr_done, t + 1)
                    o3 = ot[0:r, :].rearrange("p (h v) -> p h v", h=H)
                    dve.tensor_tensor(o3, o3, rr[0:r, :].unsqueeze(2).broadcast_to([r, H, P]), ALU.mult).then_inc(o_normed, 1)

                def gate(t, k, b, r):
                    g = gt[b]
                    dve.wait_ge(gt_in[b], (k + 1) * 16)
                    dve.wait_ge(projected, t * 2 + 3)
                    dve.tensor_tensor(g[0:r, 0:D], g[0:r, 0:D], oa[0:r, :], ALU.mult).then_inc(gated, 1)
                    dve.wait_ge(projected, t * 2 + 4)
                    dve.tensor_tensor(g[0:r, D:2 * D], g[0:r, D:2 * D], os_[0:r, :], ALU.mult).then_inc(gated, 1)
                    dve.wait_ge(gated, t * 3 + 5)
                    dve.tensor_tensor(g[0:r, 0:D], g[0:r, 0:D], g[0:r, D:2 * D], ALU.add).then_inc(gated, 1)

                def add(t, k, b, r):
                    dve.wait_ge(xt_in[b], (k + 1) * 16)
                    dve.wait_ge(multiplied, t + 2)
                    dve.tensor_tensor(xt[b][0:r, :], xt[b][0:r, :], xo[0:r, :], ALU.add).then_inc(added, 1)

                def tile(t, k, b, r, nxt):
                    if nxt:
                        norm(t + 1, nxt)
                    gate(t, k, b, r)
                    if not (isinstance(t, int) and t == 0):
                        add(t - 1, k - 1 + b, 1 - b, P)

                norm(0, P)
                over_tiles(dve, tile)
                add(NPT, NPT // 2, 0, DEC)

            @block.scalar
            def _(act):
                act.sem_inc(s_out, 4)

                def square(t, r):
                    act.wait_ge(o_in, t * 16 + 16)
                    act.activation(sq[0:r, :], ot[0:r, :], ACT.Square).then_inc(squared, 1)

                def tile(t, k, b, r, nxt):
                    act.wait_ge(projected, t * 2 + 2)
                    for j in range(OY):
                        act.wait_ge(oy_turned, t * OY + (OY + j + 1))
                        dst = oT[:, 4 * j:4 * j + 4, 0:r] if j < 2 else yT[:, 4 * (j - 2):4 * (j - 2) + 4, 0:r]
                        act.activation(dst, tb[j % 2][:, :, 0:r], ACT.Copy).then_inc(oy_out, 1)
                    if nxt:
                        square(t + 1, nxt)
                    if not (isinstance(t, int) and t == 0):
                        sums_out(t - 1, P)

                def sums_out(t, r):
                    act.wait_ge(multiplied, t + 1)
                    for j in range(2):
                        act.wait_ge(s_turned, t * 2 + (4 + j + 1))
                        act.activation(sT[:, 4 * j:4 * j + 4, 0:r], tb[j][:, :, 0:r], ACT.Copy).then_inc(s_out, 1)

                square(0, P)
                over_tiles(act, tile)
                sums_out(NPT, DEC)

            @block.tensor
            def _(pe):
                pe.sem_inc(oy_turned, OY)
                pe.sem_inc(s_turned, 4)
                pe.sem_inc(projected, 2)
                pe.sem_inc(multiplied, 1)
                pe.wait_ge(weighted, 1 + YT)
                pe.wait_ge(w_in[2], 16)

                def project(t, k, b, r):
                    for j in range(OY):
                        if j == 0:
                            pe.wait_ge(o_normed, t + 2)
                        if j == 2:
                            pe.wait_ge(y_in, t * 16 + 16)
                        if j < 2:
                            hold(pe, pe_gate, s_out, t * 2 + (j + 1))
                        else:
                            hold(pe, pe_gate, oy_out, t * OY + (j - 1))
                        src = ot if j < 2 else yt
                        for q in range(4):
                            at = (4 * (j if j < 2 else j - 2) + q) * P
                            x = pe.transpose(tb[j % 2][:, q, 0:r], src[0:r, at:at + P], c.ident[0:r, 0:r])
                        x.then_inc(oy_turned, 1)
                    for out, xT, w, n, need, step in ((oa, oT, wa, OT, 2, 1), (os_, yT, ws, YT, OY, 2)):
                        pe.wait_ge(oy_out, t * OY + need)
                        hold(pe, pe_gate, gated, t * 3 + step)
                        for h in range(0, D, HALF):
                            for q in range(n):
                                x = pe.matmul(out[0:r, h:h + HALF], xT[:, q, 0:r], w[:, q, h:h + HALF], start=(q == 0), stop=(q == n - 1))
                        x.then_inc(projected, 1)

                def multiply(t, b, r, last):
                    pe.wait_ge(gated, t * 3 + 6)
                    for j in range(2):
                        if last:
                            pe.wait_ge(s_out, t * 2 + (j + 3))
                            pe.wait_ge(oy_out, t * OY + OY)
                        else:
                            hold(pe, pe_gate, oy_out, t * OY + (OY + 5 + j))
                        for q in range(4):
                            x = pe.transpose(tb[j][:, q, 0:r], gt[b][0:r, (4 * j + q) * P:(4 * j + q + 1) * P], c.ident[0:r, 0:r])
                        x.then_inc(s_turned, 1)
                    pe.wait_ge(s_out, t * 2 + 6)
                    hold(pe, pe_gate, added, t + 1)
                    for h in range(0, D, HALF):
                        for q in range(OT):
                            x = pe.matmul(xo[0:r, h:h + HALF], sT[:, q, 0:r], wo[:, q, h:h + HALF], start=(q == 0), stop=(q == OT - 1))
                    x.then_inc(multiplied, 1)

                def tile(t, k, b, r, nxt):
                    project(t, k, b, r)
                    if not (isinstance(t, int) and t == 0):
                        multiply(t - 1, 1 - b, P, False)

                over_tiles(pe, tile)
                multiply(NPT, 0, DEC, True)


def retrieve_and_finish(nc, io, dr, c):
    CHUNK8 = 8
    ITS = PSLOT // CHUNK8
    HALF = 512
    PREP_ACT, PREP_PE, PREP_DVE = 10, 6, 7
    FIN_ACT, FIN_PE, FIN_DVE = 10, 6, 15
    TK = 22
    TK_NEG = 14
    with Stage(nc, "peer") as s:
        wq, wg, we = s.sb("wq", [P, DK, D]), s.sb("wg", [P, DK, D]), s.sb("we", [P, PLE // P, D])
        gffn, gfin, gple = s.sb("gffn", [P, D]), s.sb("gfin", [P, D]), s.sb("gple", [P, DK])
        keys = s.sb("keys", [P, P])
        keysT = s.sb("keysT", [P, P])
        zero = s.sb("zero", [P, P])
        iota16 = s.sb("iota16", [P, PTOP])
        x1 = [s.sb(f"x1{b}", [P, D]) for b in range(2)]
        h2 = [s.sb(f"h2{b}", [P, D]) for b in range(2)]
        idx = [s.sb(f"idx{b}", [P, PSLOT], U32) for b in range(2)]
        gw = [s.sb(f"gw{b}", [P, PSLOT]) for b in range(2)]
        hT, qT = s.sb("hT", [P, DK, P]), s.sb("qT", [P, PH, P])
        s12 = s.sb("s12", [P, 2, PH, PNK])
        u = [s.sb(f"u{q}", [P, D]) for q in range(CHUNK8)]
        v = [s.sb(f"v{q}", [P, D]) for q in range(CHUNK8)]
        diag = [s.sb(f"diag{q}", [P, P]) for q in range(CHUNK8)]
        stage = [s.sb(f"stage{q}", [P, CHUNK8], U32) for q in range(2)]
        pre, ge, aw = ([s.sb(f"{n}{q}", [P, CHUNK8]) for q in range(2)] for n in ("pre", "ge", "aw"))
        cs, cs2 = s.sb("cs", [P, 2, PNK]), s.sb("cs2", [P, 2, PNK])
        top, topi, topf = s.sb("top", [P, 2, PTOP]), s.sb("topi", [P, 2, PTOP], U32), s.sb("topf", [P, 2, PTOP])
        cand, cand2 = s.sb("cand", [P, PTOP * PTOP]), s.sb("cand2", [P, PTOP * PTOP])
        best, pos, ab, abf = s.sb("best", [P, PTOP]), s.sb("pos", [P, PTOP], U32), s.sb("ab", [P, 2, PTOP], U32), s.sb("abf", [P, 2, PTOP])
        hot, sel = s.sb("hot", [P, 2, PTOP, PTOP]), s.sb("sel", [P, 2, PTOP])
        negbest, ex, tot, rtot = s.sb("negbest", [P, 1]), s.sb("ex", [P, PTOP]), s.sb("tot", [P, 1]), s.sb("rtot", [P, 1])
        pss, pr, pt = s.sb("pss", [P, 1]), s.sb("pr", [P, 1]), s.sb("pt", [P, 1])
        fss, fr, ft = s.sb("fss", [P, 1]), s.sb("fr", [P, 1]), s.sb("ft", [P, 1])
        x2, h3, y = s.sb("x2", [P, D]), s.sb("h3", [P, D]), s.sb("y", [P, D])
        pl, plT = s.sb("pl", [P, PLE]), s.sb("plT", [P, PLE // P, P])

        acc = s.ps("acc", [P, D])
        tb = [s.ps(f"tb{q}", [P, 4, P]) for q in range(2)]
        sb_ = [s.ps(f"sb{q}", [P, 4, P]) for q in range(2)]
        fo = s.ps("fo", [P, D])

        w_in, vec_in, once, once_pe, once_act, iota_done = (s.sem(n) for n in ("w_in", "vec_in", "once", "once_pe", "once_act", "iota_done"))
        x1_in, pl_in, y_stored = s.sems("x1_in", 2), s.sem("pl_in"), s.sem("y_stored")
        prep_act, prep_pe, prep_dve = s.sem("prep_act"), s.sem("prep_pe"), s.sem("prep_dve")
        fin_act, fin_pe, fin_dve = s.sem("fin_act"), s.sem("fin_pe"), s.sem("fin_dve")
        tk, exp_done, idx_done = s.sem("tk"), s.sem("exp_done"), s.sem("idx_done")
        staged, u_in, v_in = s.sem("staged"), s.sems("u_in", CHUNK8), s.sems("v_in", CHUNK8)
        u_done, v_done, gelu_done, aw_done, diag_done = (s.sem(n) for n in ("u_done", "v_done", "gelu_done", "aw_done", "diag_done"))
        acc_done, acc_out = s.sem("acc_done"), s.sem("acc_out")
        pool_gate, pe_gate, dve_gate = s.sem("pool_gate"), s.sem("pe_gate"), s.sem("dve_gate")

        def gather_loops(eng, iteration, t, b, r, between, middle):
            for lo, hi in ((0, PH // 2), (PH // 2, PH)):
                with eng.Fori(lo, hi) as i:
                    for q in range(2):
                        iteration(t, b, r, i, q)
                    between(i)
                if lo == 0:
                    middle()

        def count(t, i, q):
            return t * ITS + (i * 2 + q)

        def nothing(*a):
            pass

        with nc.Block() as block:

            @block.sync
            def _(sp):
                sp.dma_start(wq[:], io["peer_wq"][0].rearrange("(k p) n -> p k n", p=P)).then_inc(w_in, 16)
                sp.dma_start(gffn[:], io["norm_ffn_g"].broadcast_to([P, D])).then_inc(vec_in, 16)
                sp.dma_start(gfin[:], io["final_norm_g"].rearrange("(a d) -> a d", a=1).broadcast_to([P, D])).then_inc(vec_in, 16)
                sp.dma_start(keys[:, 0:P // 2], io["peer_k1"][0]).then_inc(vec_in, 16)
                sp.dma_start(keys[:, P // 2:P], io["peer_k2"][0]).then_inc(vec_in, 16)
                sp.dma_start(gple[:], io["norm_ple_g"].rearrange("a (k p) -> p (a k)", p=P), allow_slow_non_contiguous=True).then_inc(vec_in, 16)

                def load_x1(t, k, b, r):
                    sp.wait_ge(acc_done, t + 1)
                    sp.dma_start(x1[b][0:r, :], dr["x1"][tokens(t, r), :]).then_inc(x1_in[b], 16)

                def finish(t, r):
                    src = io["p_sample"][0, 0] if r == DEC else io["p_prompt"][0, 0, tokens(t, r), :]
                    dst = io["y_sample_out"] if r == DEC else io["y_prompt_out"][tokens(t, r), :]
                    sp.wait_ge(fin_pe, t * FIN_PE + 3)
                    sp.dma_start(pl[0:r, :], src).then_inc(pl_in, 16)
                    sp.wait_ge(fin_dve, t * FIN_DVE + FIN_DVE)
                    sp.dma_start(dst, y[0:r, :]).then_inc(y_stored, 16)

                load_x1(0, 0, 0, P)
                sp.dma_start(wg[:], io["ple_w_gate"][0].rearrange("(k p) n -> p k n", p=P)).then_inc(w_in, 16)
                sp.dma_start(we[:], io["ple_w_proj"][0].rearrange("(k p) n -> p k n", p=P)).then_inc(w_in, 16)

                def tile(t, k, b, r, nxt):
                    if nxt:
                        load_x1(t + 1, k + b, 1 - b, nxt)
                    if not (isinstance(t, int) and t == 0):
                        finish(t - 1, P)

                sp.sem_inc(y_stored, 16)
                over_tiles(sp, tile)
                finish(NPT, DEC)
                sp.wait_ge(y_stored, 16 * (NT + 1))

            @block.gpsimd
            def _(pool):
                pool.iota(stage[0][:].bitcast(I32), [[1, CHUNK8]], base=0, channel_multiplier=0).then_inc(iota_done, 1)
                pool.iota(stage[1][:].bitcast(I32), [[1, CHUNK8]], base=CHUNK8, channel_multiplier=0).then_inc(iota_done, 1)
                pool.memset(zero[:], 0.0).then_inc(iota_done, 1)
                pool.wait_ge(once, 2)

                def iteration(t, b, r, i, q):
                    g = count(t, i, q)
                    pool.tensor_copy(stage[q][0:r, :], idx[b][0:r, bass.ds(i * (2 * CHUNK8) + q * CHUNK8, CHUNK8)]).then_inc(staged, 1)
                    hold(pool, pool_gate, staged, g + 1)
                    for table, ring, arrived, used in (("peer_u", u, u_in, u_done), ("peer_v", v, v_in, v_done)):
                        for k in range(CHUNK8):
                            hold(pool, pool_gate, used, g * CHUNK8 + (k + 1))
                            pool.indirect_dma_start(ring[k][0:r, :], None, io[table][0], bass.IndirectOffsetOnAxis(
                                ap=stage[q][0:r, k:k + 1], axis=0)).then_inc(arrived[k], 16)

                def tile(t, k, b, r, nxt):
                    hold(pool, pool_gate, idx_done, t * PH + PH)
                    gather_loops(pool, iteration, t, b, r, nothing, nothing)

                over_tiles(pool, tile)

            @block.vector
            def _(dve):
                dve.wait_ge(iota_done, 3)
                for q in range(2):
                    dve.tensor_copy(iota16[:, q * CHUNK8:(q + 1) * CHUNK8], stage[q][:]).then_inc(once, 1)
                dve.sem_inc(u_done, CHUNK8)
                dve.wait_ge(vec_in, 80)

                def rsqrt(step, ms, root, tmp, act_sem, act_val):
                    step(dve.tensor_scalar(ms, ms, 1.0 / D, EPS, ALU.mult, ALU.add))
                    dve.wait_ge(act_sem, act_val)
                    step(dve.reciprocal(root, tmp))
                    step(dve.tensor_tensor(tmp, root, root, ALU.mult))
                    step(dve.tensor_tensor(tmp, tmp, ms, ALU.mult))
                    step(dve.tensor_scalar(tmp, tmp, -0.5, 1.5, ALU.mult, ALU.add))
                    step(dve.tensor_tensor(root, root, tmp, ALU.mult))

                def stepper(sem, base):
                    done = [0]

                    def step(ins):
                        ins.then_inc(sem, 1)
                        done[0] += 1
                        hold(dve, dve_gate, sem, base + done[0])
                    return step, done

                def prepare(t, b, r):
                    step, done = stepper(prep_dve, t * PREP_DVE)
                    dve.wait_ge(prep_act, t * PREP_ACT + 1)
                    rsqrt(step, pss[0:r, :], pr[0:r, :], pt[0:r, :], prep_act, t * PREP_ACT + 2)
                    step(dve.scalar_tensor_tensor(out=h2[b][0:r, :], in0=x1[b][0:r, :], scalar=pr[0:r, 0:1], in1=gffn[0:r, :],
                                                  op0=ALU.mult, op1=ALU.mult))
                    assert done[0] == PREP_DVE

                def choose(t, b, r, i):
                    n = t * PH + i
                    base = n * TK
                    step, done = stepper(tk, base)

                    def both(make):
                        for m in range(2):
                            make(m).then_inc(tk, 1)
                        done[0] += 2
                        hold(dve, dve_gate, tk, base + done[0])

                    dve.wait_ge(prep_act, t * PREP_ACT + PREP_ACT)
                    step(dve.tensor_copy(cs[0:r], s12[0:r, :, bass.ds(i, 1), :].rearrange("p m h n -> p m (h n)")))
                    both(lambda m: dve.max(top[0:r, m, 0:8], cs[0:r, m, :]))
                    both(lambda m: dve.match_replace(cs2[0:r, m, :], top[0:r, m, 0:8], cs[0:r, m, :], -3.0e38))
                    both(lambda m: dve.max(top[0:r, m, 8:16], cs2[0:r, m, :]))
                    for m in range(2):
                        dve.max_index(topi[0:r, m, 0:8], top[0:r, m, 0:8], cs[0:r, m, :])
                        dve.max_index(topi[0:r, m, 8:16], top[0:r, m, 8:16], cs2[0:r, m, :])
                    step(dve.tensor_tensor(cand[0:r, :].rearrange("p (a b) -> p a b", b=PTOP),
                                           top[0:r, 0, :].unsqueeze(2).broadcast_to([r, PTOP, PTOP]),
                                           top[0:r, 1, :].unsqueeze(1).broadcast_to([r, PTOP, PTOP]), ALU.add))
                    step(dve.max(best[0:r, 0:8], cand[0:r, :]))
                    step(dve.match_replace(cand2[0:r, :], best[0:r, 0:8], cand[0:r, :], -3.0e38))
                    step(dve.max(best[0:r, 8:16], cand2[0:r, :]))
                    dve.max_index(pos[0:r, 0:8], best[0:r, 0:8], cand[0:r, :])
                    step(dve.max_index(pos[0:r, 8:16], best[0:r, 8:16], cand2[0:r, :]))
                    step(dve.tensor_copy(topf[0:r], topi[0:r]))
                    step(dve.tensor_scalar(negbest[0:r, :], best[0:r, 0:1], -1.0, None, ALU.mult))
                    assert done[0] == TK_NEG, done
                    dve.tensor_scalar(ab[0:r, 0, :], pos[0:r, :], 4, None, ALU.logical_shift_right)
                    step(dve.tensor_scalar(ab[0:r, 1, :], pos[0:r, :], PTOP - 1, None, ALU.bitwise_and))
                    step(dve.tensor_copy(abf[0:r], ab[0:r]))
                    for m in range(2):
                        hm = dve.tensor_tensor(hot[0:r, m], abf[0:r, m, :].unsqueeze(2).broadcast_to([r, PTOP, PTOP]),
                                               iota16[0:r, :].unsqueeze(1).broadcast_to([r, PTOP, PTOP]), ALU.is_equal)
                    step(hm)
                    for m in range(2):
                        hm = dve.tensor_tensor(hot[0:r, m], hot[0:r, m], topf[0:r, m, :].unsqueeze(1).broadcast_to([r, PTOP, PTOP]), ALU.mult)
                    step(hm)
                    step(dve.tensor_reduce(sel[0:r], hot[0:r], AX_X, ALU.add))
                    step(dve.scalar_tensor_tensor(out=idx[b][0:r, bass.ds(i * PTOP, PTOP)], in0=sel[0:r, 0, :], scalar=float(PNK),
                                                  in1=sel[0:r, 1, :], op0=ALU.mult, op1=ALU.add))
                    dve.wait_ge(exp_done, n + 1)
                    step(dve.reciprocal(rtot[0:r, :], tot[0:r, :]))
                    step(dve.tensor_scalar(gw[b][0:r, bass.ds(i * PTOP, PTOP)], ex[0:r, :], rtot[0:r, 0:1], None, ALU.mult))
                    assert done[0] == TK, done
                    dve.sem_inc(idx_done, 1)

                def iteration(t, b, r, i, q):
                    g = count(t, i, q)
                    for k in range(CHUNK8):
                        dve.wait_ge(u_in[k], g * 16 + 16)
                        dve.tensor_tensor_reduce(u[k][0:r, :], u[k][0:r, :], h2[b][0:r, :], 1.0, 0.0, ALU.mult, ALU.add,
                                                 pre[q][0:r, k:k + 1]).then_inc(u_done, 1)
                    dve.wait_ge(gelu_done, g + 1)
                    dve.tensor_tensor(aw[q][0:r, :], ge[q][0:r, :], gw[b][0:r, bass.ds(i * (2 * CHUNK8) + q * CHUNK8, CHUNK8)],
                                      ALU.mult).then_inc(aw_done, 1)

                def finish(t, r):
                    step, done = stepper(fin_dve, t * FIN_DVE)
                    a = t * FIN_ACT
                    dve.wait_ge(fin_act, a + 1)
                    rsqrt(step, fss[0:r, :], fr[0:r, :], ft[0:r, :], fin_act, a + 2)
                    dve.wait_ge(fin_act, a + 8)
                    dve.wait_ge(fin_pe, t * FIN_PE + 6 + 3)
                    step(dve.tensor_tensor(y[0:r, :], y[0:r, :], fo[0:r, :], ALU.mult))
                    step(dve.tensor_tensor(y[0:r, :], y[0:r, :], x2[0:r, :], ALU.add))
                    dve.wait_ge(fin_act, a + 9)
                    rsqrt(step, fss[0:r, :], fr[0:r, :], ft[0:r, :], fin_act, a + 10)
                    step(dve.scalar_tensor_tensor(out=y[0:r, :], in0=y[0:r, :], scalar=fr[0:r, 0:1], in1=gfin[0:r, :],
                                                  op0=ALU.mult, op1=ALU.mult))
                    assert done[0] == FIN_DVE, done

                def tile(t, k, b, r, nxt):
                    if nxt:
                        prepare(t + 1, 1 - b, nxt)
                    gather_loops(dve, iteration, t, b, r,
                                 (lambda i: choose(t + 1, 1 - b, nxt, i)) if nxt else nothing,
                                 (lambda: finish(t - 1, P)) if not (isinstance(t, int) and t == 0) else nothing)

                prepare(0, 0, P)
                dve.wait_ge(w_in, 48)
                for k in range(DK):
                    dve.tensor_scalar(wg[:, k, :], wg[:, k, :], gple[:, k:k + 1], None, ALU.mult).then_inc(once, 1)
                with dve.Fori(0, PH) as i:
                    choose(0, 0, P, i)
                over_tiles(dve, tile)
                finish(NPT, DEC)

            @block.scalar
            def _(act):
                act.sem_inc(acc_out, 1)
                act.wait_ge(once_pe, 1)
                act.activation(keysT[:], tb[0][:, 0, :], ACT.Copy).then_inc(once_act, 1)

                def prepare(t, k, b, r):
                    a = t * PREP_ACT
                    act.wait_ge(x1_in[b], k * 16 + 16)
                    act.activation(h2[b][0:r, :], x1[b][0:r, :], ACT.Square, accum_out=pss[0:r, :]).then_inc(prep_act, 1)
                    act.wait_ge(prep_dve, t * PREP_DVE + 1)
                    act.activation(pt[0:r, :], pss[0:r, :], ACT.Sqrt).then_inc(prep_act, 1)
                    for j in range(2):
                        act.wait_ge(prep_pe, t * PREP_PE + (j + 1))
                        act.activation(hT[:, 4 * j:4 * j + 4, 0:r], tb[j][:, :, 0:r], ACT.Copy).then_inc(prep_act, 1)
                    for j in range(2):
                        act.wait_ge(prep_pe, t * PREP_PE + (j + 3))
                        act.activation(qT[:, 4 * j:4 * j + 4, 0:r], tb[j][:, :, 0:r], ACT.Copy).then_inc(prep_act, 1)
                    for j in range(2):
                        act.wait_ge(prep_pe, t * PREP_PE + (j + 5))
                        for m in range(2):
                            act.activation(s12[0:r, m, 4 * j:4 * j + 4, :], sb_[m][0:r, :, :], ACT.Copy).then_inc(prep_act, 1)

                def choose(t, b, r, i):
                    n = t * PH + i
                    act.wait_ge(tk, n * TK + TK_NEG)
                    act.activation(ex[0:r, :], best[0:r, :], ACT.Exp, bias=negbest[0:r, 0:1], accum_out=tot[0:r, :]).then_inc(exp_done, 1)

                def iteration(t, b, r, i, q):
                    g = count(t, i, q)
                    act.wait_ge(u_done, g * CHUNK8 + 2 * CHUNK8)
                    act.activation(ge[q][0:r, :], pre[q][0:r, :], ACT.Gelu_apprx_tanh).then_inc(gelu_done, 1)
                    act.wait_ge(aw_done, g + 1)
                    for k in range(CHUNK8):
                        act.wait_ge(v_done, g * CHUNK8 + (k + 1))
                        act.activation(diag[k][0:r, 0:r], c.ident[0:r, 0:r], ACT.Copy, scale=aw[q][0:r, k:k + 1]).then_inc(diag_done, 1)

                def sum_out(t, r):
                    act.wait_ge(acc_done, t + 3)
                    act.activation(x2[0:r, :], acc[0:r, :], ACT.Copy).then_inc(acc_out, 1)

                def finish(t, r):
                    d, p = t * FIN_DVE, t * FIN_PE + 3
                    act.wait_ge(acc_out, t + 2)
                    act.activation(h3[0:r, :], x2[0:r, :], ACT.Square, accum_out=fss[0:r, :]).then_inc(fin_act, 1)
                    act.wait_ge(fin_dve, d + 1)
                    act.activation(ft[0:r, :], fss[0:r, :], ACT.Sqrt).then_inc(fin_act, 1)
                    act.wait_ge(fin_dve, d + 6)
                    act.activation(h3[0:r, :], x2[0:r, :], ACT.Copy, scale=fr[0:r, 0:1]).then_inc(fin_act, 1)
                    for j in range(2):
                        act.wait_ge(fin_pe, p + (j + 1))
                        act.activation(hT[:, 4 * j:4 * j + 4, 0:r], tb[j][:, :, 0:r], ACT.Copy).then_inc(fin_act, 1)
                    act.wait_ge(fin_pe, p + 3)
                    act.activation(plT[:, :, 0:r], sb_[0][:, 0:2, 0:r], ACT.Copy).then_inc(fin_act, 1)
                    act.wait_ge(y_stored, t * 16 + 16)
                    for j in range(2):
                        act.wait_ge(fin_pe, p + (j + 4))
                        act.activation(y[0:r, j * HALF:(j + 1) * HALF], fo[0:r, j * HALF:(j + 1) * HALF], ACT.Sigmoid).then_inc(fin_act, 1)
                    act.wait_ge(fin_dve, d + 8)
                    act.activation(h3[0:r, :], y[0:r, :], ACT.Square, accum_out=fss[0:r, :]).then_inc(fin_act, 1)
                    act.wait_ge(fin_dve, d + 9)
                    act.activation(ft[0:r, :], fss[0:r, :], ACT.Sqrt).then_inc(fin_act, 1)

                def tile(t, k, b, r, nxt):
                    if nxt:
                        prepare(t + 1, k + b, 1 - b, nxt)
                    gather_loops(act, iteration, t, b, r,
                                 (lambda i: choose(t + 1, 1 - b, nxt, i)) if nxt else nothing,
                                 (lambda: finish(t - 1, P)) if not (isinstance(t, int) and t == 0) else nothing)
                    sum_out(t, r)

                prepare(0, 0, 0, P)
                with act.Fori(0, PH) as i:
                    choose(0, 0, P, i)
                over_tiles(act, tile)
                finish(NPT, DEC)

            @block.tensor
            def _(pe):
                pe.sem_inc(acc_done, 2)
                pe.sem_inc(v_done, CHUNK8)
                pe.sem_inc(fin_pe, 3)
                pe.wait_ge(vec_in, 80)
                pe.transpose(tb[0][:, 0, :], keys[:], c.ident[:]).then_inc(once_pe, 1)
                pe.wait_ge(once_act, 1)
                pe.wait_ge(iota_done, 3)

                def turn(src, r):
                    for j in range(2):
                        for q in range(4):
                            at = (4 * j + q) * P
                            x = pe.transpose(tb[j][:, q, 0:r], src[0:r, at:at + P], c.ident[0:r, 0:r])
                        yield x

                def prepare(t, b, r):
                    a = t * PREP_ACT
                    hold(pe, pe_gate, prep_dve, t * PREP_DVE + PREP_DVE)
                    for x in turn(h2[b], r):
                        x.then_inc(prep_pe, 1)
                    hold(pe, pe_gate, prep_act, a + 4)
                    for j in range(2):
                        for h in range(4):
                            for k in range(DK):
                                at = (4 * j + h) * P
                                x = pe.matmul(tb[j][:, h, 0:r], wq[:, k, at:at + P], hT[:, k, 0:r], start=(k == 0), stop=(k == DK - 1))
                        x.then_inc(prep_pe, 1)
                    for j in range(2):
                        hold(pe, pe_gate, prep_act, a + (6 if j == 0 else 8))
                        for m in range(2):
                            half = slice(m * P // 2, (m + 1) * P // 2)
                            for h in range(4):
                                x = pe.matmul(sb_[m][0:r, h, :], qT[half, 4 * j + h, 0:r], keysT[half, :], start=True, stop=True)
                        x.then_inc(prep_pe, 1)

                def iteration(t, b, r, i, q):
                    g = count(t, i, q)
                    for k in range(CHUNK8):
                        pe.wait_ge(diag_done, g * CHUNK8 + (k + 1))
                        hold(pe, pe_gate, v_in[k], g * 16 + 16)
                        for h in range(0, D, HALF):
                            x = pe.matmul(acc[0:r, h:h + HALF], diag[k][0:r, 0:r], v[k][0:r, h:h + HALF], start=False, stop=False)
                        x.then_inc(v_done, 1)

                def open_sum(t, b, r):
                    hold(pe, pe_gate, acc_out, t + 1)
                    for h in range(0, D, HALF):
                        pe.matmul(acc[0:r, h:h + HALF], c.ident[0:r, 0:r], x1[b][0:r, h:h + HALF], start=True, stop=False)

                def close_sum(t, b, r):
                    for h in range(0, D, HALF):
                        x = pe.matmul(acc[0:r, h:h + HALF], zero[0:r, 0:r], x1[b][0:r, h:h + HALF], start=False, stop=True)
                    x.then_inc(acc_done, 1)

                def finish(t, r):
                    a = t * FIN_ACT
                    hold(pe, pe_gate, pl_in, t * 16 + 16)
                    hold(pe, pe_gate, fin_act, a + 3)
                    for x in turn(h3, r):
                        x.then_inc(fin_pe, 1)
                    for q in range(PLE // P):
                        x = pe.transpose(sb_[0][:, q, 0:r], pl[0:r, q * P:(q + 1) * P], c.ident[0:r, 0:r])
                    x.then_inc(fin_pe, 1)
                    hold(pe, pe_gate, fin_act, a + 5)
                    for h in range(2):
                        for k in range(DK):
                            x = pe.matmul(fo[0:r, h * HALF:(h + 1) * HALF], hT[:, k, 0:r], wg[:, k, h * HALF:(h + 1) * HALF],
                                          start=(k == 0), stop=(k == DK - 1))
                        x.then_inc(fin_pe, 1)
                    hold(pe, pe_gate, fin_act, a + 8)
                    for h in range(2):
                        for k in range(PLE // P):
                            x = pe.matmul(fo[0:r, h * HALF:(h + 1) * HALF], plT[:, k, 0:r], we[:, k, h * HALF:(h + 1) * HALF],
                                          start=(k == 0), stop=(k == PLE // P - 1))
                    x.then_inc(fin_pe, 1)

                def tile(t, k, b, r, nxt):
                    open_sum(t, b, r)
                    if nxt:
                        prepare(t + 1, 1 - b, nxt)
                    gather_loops(pe, iteration, t, b, r, nothing,
                                 (lambda: finish(t - 1, P)) if not (isinstance(t, int) and t == 0) else nothing)
                    close_sum(t, b, r)

                pe.wait_ge(w_in, 48)
                prepare(0, 0, P)
                pe.wait_ge(once, 2 + DK)
                over_tiles(pe, tile)
                finish(NPT, DEC)


class Held:

    def __init__(self, nc, whole, front):
        def sb(stack, name, shape, dt=F32):
            return stack.enter_context(nc.sbuf_tensor(name, shape, dt))

        self.ident = sb(whole, "ident", [P, P])
        self.ones = sb(front, "ones", [P, P])
        self.upper = sb(front, "upper", [P, P])
        self.below = sb(front, "below", [P, P])
        self.neghalf = sb(front, "neghalf", [P, 16])
        self.dt = sb(front, "dt", [P, NT, SH])


SCRATCH = {
    "chan": (C_V + SCD, T),
    "zs": (TP, SIN),
    "gs": (TP, 2 * D),
    "att": (TP, D),
    "xtok": (TP, SIN + SG * SN),
    "bc": (2 * SG * SN, TP),
    "yg": (TP, SIN),
    "x1": (TP, D),
}


def build(nc, io, dr):
    with ExitStack() as whole:
        with ExitStack() as front:
            c = Held(nc, whole, front)
            build_constants(nc, c)
            project_inputs(nc, io, dr, c)
            attend(nc, io, dr, c)
            causal_convolution(nc, io, dr, c)
            state_space(nc, io, dr, c)
            mix_branches(nc, io, dr, c)
        retrieve_and_finish(nc, io, dr, c)


_INS = ["x_prompt", "x_sample", "p_prompt", "p_sample", "cache_k", "cache_v", "state_conv", "state_ssm",
        "norm_mix_g", "w_in", "lam_q1", "lam_k1", "lam_q2", "lam_k2", "attn_subln_g", "w_attn_o",
        "conv_w", "conv_b", "dt_bias", "a_log", "d_skip", "ssm_norm_g", "w_ssm_o", "w_out",
        "norm_ffn_g", "peer_wq", "peer_k1", "peer_k2", "peer_u", "peer_v",
        "norm_ple_g", "ple_w_gate", "ple_w_proj", "final_norm_g"]
_OUTS = [("y_prompt_out", (SEQ, D), (1, SEQ, D)),
         ("y_sample_out", (DEC, D), (1, DEC, D)),
         ("k_prompt_out", (SEQ, D), (1, 1, SEQ, H, 2, AK)),
         ("v_prompt_out", (SEQ, D), (1, 1, SEQ, H, 2 * AK)),
         ("conv_prompt_out", (SCONV - 1, SCD), (1, 1, SCONV - 1, SCD)),
         ("ssm_prompt_out", (SIN, SN), (1, 1, SH, SP_, SN)),
         ("k_sample_out", (DEC, D), (1, 1, DEC, H, 2, AK)),
         ("v_sample_out", (DEC, D), (1, 1, DEC, H, 2 * AK)),
         ("conv_sample_out", (SCONV - 1, SCD), (1, 1, SCONV - 1, SCD)),
         ("ssm_sample_out", (SIN, SN), (1, 1, SH, SP_, SN))]


def kernel(**inputs):
    import numpy as _np
    import concourse.bacc as _bacc
    from concourse import mybir as _mybir
    from concourse.bass_utils import run_bass_kernel_spmd as _run

    nc = _bacc.Bacc("TRN2", target_bir_lowering=False, num_devices=1)
    arrays, io = {}, {}
    for name in _INS:
        a = _np.ascontiguousarray(inputs[name])
        arrays[f"in_{name}_dram"] = a
        io[name] = nc.dram_tensor(f"in_{name}_dram", a.shape, _mybir.dt.from_np(a.dtype), kind="ExternalInput").ap()
    for i, (name, shape, _) in enumerate(_OUTS):
        io[name] = nc.dram_tensor(f"out_{i}_dram", shape, F32, kind="ExternalOutput").ap()
    io["cache_k2"] = io["cache_k"].rearrange("a b t h j d -> (a b t) (h j d)")
    io["cache_v2"] = io["cache_v"].rearrange("a b t h d -> (a b t) (h d)")
    dr = {name: nc.dram_tensor(f"scratch_{name}", shape, F32, kind="Internal").ap() for name, shape in SCRATCH.items()}
    build(nc, io, dr)
    r = _run(nc, [arrays], core_ids=[0])
    got = tuple(r.results[0][f"out_{i}_dram"] for i in range(len(_OUTS)))
    return tuple(_np.asarray(g).reshape(shape) for g, (_, _, shape) in zip(got, _OUTS))
```

```python
from contextlib import ExitStack

import numpy as np

import concourse.bass as bass
from concourse import mybir

F32 = mybir.dt.float32
F32R = mybir.dt.float32r
U32 = mybir.dt.uint32
I32 = mybir.dt.int32
ALU = mybir.AluOpType
ACT = mybir.ActivationFunctionType
AX_X = mybir.AxisListType.X

P = 128
D = 1024
DK = D // P
SEQ, DEC, PAST = 1024, 32, 512
T = SEQ + DEC
NPT = SEQ // P
NT = NPT + 1
TP = NT * P
EPS = 1e-6
LAM_INIT = 0.8 - 0.6 * 1.0
H = 8
AK = 64
CH = 64
SIN = 2048
SH, SP_, SG, SN = 32, 64, 4, 128
SCONV, SCD = 4, 3072
PH, PNK, PTOP = 8, 128, 16
PSLOT = PH * PTOP
PLE = 256
C_Q, C_K, C_V, C_Z, C_XBC, C_DT, C_G = 0, 1024, 2048, 3072, 5120, 8192, 8224
IN_COLS = 10272
PANEL = 512
NSPLIT = 3
TS = T // NSPLIT
NEG = -1e30


def rows_of(t):
    return P if t < NPT else DEC


def hold(engine, gate, sem, value):
    engine.wait_ge(sem, value)
    engine.sem_inc(gate, 1)


class Stage:

    def __init__(self, nc, tag):
        self.nc, self.tag, self.stack, self.semaphores = nc, tag, ExitStack(), []

    def __enter__(self):
        self.stack.__enter__()
        return self

    def __exit__(self, *exc):
        if self.semaphores:
            self.nc.clear_and_free_semaphores(self.semaphores)
            self.nc.all_engine_barrier()
        return self.stack.__exit__(*exc)

    def sb(self, name, shape, dt=F32):
        return self.stack.enter_context(self.nc.sbuf_tensor(f"{self.tag}_{name}", shape, dt))

    def ps(self, name, shape, dt=F32):
        return self.stack.enter_context(self.nc.psum_tensor(f"{self.tag}_{name}", shape, dt))

    def sem(self, name):
        self.semaphores.append(self.nc.alloc_semaphore(name=f"{self.tag}_{name}"))
        return self.semaphores[-1]

    def sems(self, name, n):
        return [self.sem(f"{name}{i}") for i in range(n)]


def split(dve, x, lead, rest, sem, value):
    dve.tensor_copy(lead.bitcast(F32R), x).then_inc(sem, 1)
    dve.wait_ge(sem, value)
    dve.tensor_tensor(rest.bitcast(F32R), x, lead, ALU.subtract).then_inc(sem, 1)


def product(pe, out, left, right):
    last = len(left) - 1
    for k, ((a, ar), (b, br)) in enumerate(zip(left, right)):
        pe.matmul(out, a.bitcast(F32R), b.bitcast(F32R), start=(k == 0), stop=False)
        pe.matmul(out, a.bitcast(F32R), br.bitcast(F32R), start=False, stop=False)
        mm = pe.matmul(out, ar.bitcast(F32R), b.bitcast(F32R), start=False, stop=(k == last))
    return mm


def build_constants(nc, c):
    with Stage(nc, "cst") as s:
        filled, selected = s.sem("filled"), s.sem("selected")
        with nc.Block() as block:

            @block.gpsimd
            def _(pool):
                pool.memset(c.ident[:], 0.0).then_inc(filled, 1)
                pool.memset(c.ones[:], 1.0).then_inc(filled, 1)
                pool.memset(c.upper[:], 1.0).then_inc(filled, 1)
                pool.memset(c.below[:], 1.0).then_inc(filled, 1)
                pool.memset(c.neghalf[:], -0.5).then_inc(filled, 1)
                pool.memset(c.dt[:], 0.0).then_inc(filled, 1)
                pool.wait_ge(filled, 6)
                pool.affine_select(out=c.ident[:], in_=c.ident[:], compare_op=ALU.not_equal, fill=1.0, base=0,
                                   pattern=[[-1, P]], channel_multiplier=1).then_inc(selected, 1)
                pool.affine_select(out=c.upper[:], in_=c.upper[:], compare_op=ALU.is_ge, fill=0.0, base=0,
                                   pattern=[[1, P]], channel_multiplier=-1).then_inc(selected, 1)
                pool.affine_select(out=c.below[:], in_=c.below[:], compare_op=ALU.is_gt, fill=0.0, base=0,
                                   pattern=[[-1, P]], channel_multiplier=1).then_inc(selected, 1)
                pool.wait_ge(selected, 3)


def project_inputs(nc, io, dr, c):
    NB = 6
    with Stage(nc, "proj") as s:
        xt = s.sb("xt", [P, NT, D])
        hc = [s.sb(f"hc{i}", [P, 4, P]) for i in range(2)]
        wp = s.sb("wp", [P, DK, PANEL])
        wdt = s.sb("wdt", [P, DK, SH])
        hTh, hTr = s.sb("hTh", [P, DK, T]), s.sb("hTr", [P, DK, T])
        wph, wpr = ([s.sb(f"wp{n}{i}", [P, DK, PANEL]) for i in range(2)] for n in ("lead", "rest"))
        wdth, wdtr = s.sb("wdth", [P, DK, SH]), s.sb("wdtr", [P, DK, SH])
        stg = [s.sb(f"stg{i}", [P, PANEL]) for i in range(NB)]
        ss = s.sb("ss", [P, NT])
        rr = s.sb("rr", [P, NT])
        gm = s.sb("gm", [P, DK])
        bank = [s.ps(f"bank{i}", [P, PANEL]) for i in range(NB)]
        tb = [s.ps(f"tb{i}", [P, 4, P]) for i in range(2)]

        x_in, g_in, wdt_in = s.sems("x_in", NT), s.sem("g_in"), s.sem("wdt_in")
        ss_init, ss_done, ms_done, rr_done, xn_done = s.sem("ss_init"), s.sem("ss_done"), s.sem("ms_done"), s.sem("rr_done"), s.sem("xn_done")
        turned, hT_done = s.sem("turned"), s.sem("hT_done")
        panel_in, panel_used = s.sem("panel_in"), s.sems("panel_used", 2)
        mm_done, evac_done, stored = s.sems("mm_done", NB), s.sems("evac_done", NB), s.sems("stored", NB)
        gate, h_split, wdt_split, w_split = s.sem("gate"), s.sem("h_split"), s.sem("wdt_split"), s.sem("w_split")

        def w_cols(base, n=PANEL):
            return io["w_in"][0].rearrange("(k p) n -> p k n", p=P)[:, :, bass.ds(base, n)]

        RUNS = [("qk", 4, C_Q), ("xbc", 6, C_XBC), ("v", 2, C_V), ("z", 4, C_Z), ("g", 4, C_G)]
        UNITS = {"qk": 4 * NSPLIT, "xbc": 4 * NSPLIT, "v": NT, "z": NT, "g": NT}

        def runs(eng, body):
            pairs, visits = 0, 0
            for kind, n, col in RUNS:
                per = 2 * UNITS[kind] // NB
                if n == 2:
                    body(kind, 0, col, pairs, visits)
                else:
                    with eng.Fori(0, n // 2) as i:
                        body(kind, i, col, pairs, visits)
                pairs += n // 2
                visits += per * n // 2

        def per_pair(kind):
            return 2 * UNITS[kind] // NB

        with nc.Block() as block:

            @block.gpsimd
            def _(pool):
                for t in range(NT):
                    pool.wait_ge(ms_done, t + 1)
                    pool.tensor_tensor(rr[:, t:t + 1], ss[:, t:t + 1], c.neghalf[:, t:t + 1], ALU.pow).then_inc(rr_done, 1)

                def loads(kind, i, col, pairs, visits):
                    for b in range(2):
                        hold(pool, gate, w_split, i * 4 + (4 * pairs + 2 * b + 1))
                        pool.dma_start(wp[:], w_cols(i * (2 * PANEL) + (col + b * PANEL))).then_inc(panel_in, 16)

                runs(pool, loads)

            @block.sync
            def _(sp):
                sp.dma_start(gm[:], io["norm_mix_g"].rearrange("a (k p) -> p (a k)", p=P),
                             allow_slow_non_contiguous=True).then_inc(g_in, 16)
                for t in range(NT):
                    n = rows_of(t)
                    src = io["x_prompt"][0, t * P:(t + 1) * P, :] if t < NPT else io["x_sample"][0]
                    sp.dma_start(xt[0:n, t, :], src).then_inc(x_in[t], 16)
                sp.dma_start(wdt[:], w_cols(C_DT, SH)).then_inc(wdt_in, 16)

                for slot in range(NB):
                    sp.sem_inc(stored[slot], 16)

                def stores(kind, i, col, pairs, visits):
                    U = UNITS[kind]
                    for b in range(2):
                        for u in range(U):
                            j = b * U + u
                            slot = j % NB
                            sp.wait_ge(evac_done[slot], i * per_pair(kind) + (visits + j // NB + 2))
                            if kind in ("qk", "xbc"):
                                blk, sl = divmod(u, NSPLIT)
                                base = (C_XBC - C_V if kind == "xbc" else 0)
                                row = i * (2 * PANEL) + ((col - base) + b * PANEL + blk * P)
                                sp.dma_start(dr["chan"][bass.ds(row, P), sl * TS:(sl + 1) * TS],
                                             stg[slot][:, 0:TS]).then_inc(stored[slot], 16)
                            elif kind == "v":
                                n = rows_of(u)
                                dst = (io["v_prompt_out"][u * P:(u + 1) * P, b * PANEL:(b + 1) * PANEL] if u < NPT
                                       else io["v_sample_out"][:, b * PANEL:(b + 1) * PANEL])
                                sp.dma_start(dst, stg[slot][0:n, :]).then_inc(stored[slot], 16)
                            else:
                                n = rows_of(u)
                                name = "zs" if kind == "z" else "gs"
                                sp.dma_start(dr[name][u * P:u * P + n, bass.ds(i * (2 * PANEL) + b * PANEL, PANEL)],
                                             stg[slot][0:n, :]).then_inc(stored[slot], 16)

                runs(sp, stores)
                total = sum(n // 2 * per_pair(k) for k, n, _ in RUNS)
                for slot in range(NB):
                    sp.wait_ge(stored[slot], 16 * (total + 1))

            @block.vector
            def _(dve):
                def by_channel(t):
                    n = rows_of(t)
                    for h in range(2):
                        dve.wait_ge(turned, 2 * t + h + 1)
                        dve.tensor_tensor(hc[h][:, :, 0:n], tb[h][:, :, 0:n],
                                          gm[:, 4 * h:4 * h + 4].unsqueeze(2).broadcast_to([P, 4, n]),
                                          ALU.mult).then_inc(hT_done, 1)
                        dve.wait_ge(hT_done, 2 * t + h + 1)
                        here = slice(t * P, t * P + n)
                        split(dve, hc[h][:, :, 0:n], hTh[:, 4 * h:4 * h + 4, here], hTr[:, 4 * h:4 * h + 4, here],
                              h_split, 4 * t + 2 * h + 1)

                dve.memset(ss[:], 0.0).then_inc(ss_init, 1)
                dve.sem_inc(w_split, 1)
                for t in range(NT + 2):
                    if t < NT:
                        dve.wait_ge(ss_done, t + 1)
                        dve.tensor_scalar(ss[:, t:t + 1], ss[:, t:t + 1], 1.0 / D, EPS, ALU.mult, ALU.add).then_inc(ms_done, 1)
                    if 1 <= t <= NT:
                        n = rows_of(t - 1)
                        dve.wait_ge(rr_done, t)
                        dve.tensor_scalar(xt[0:n, t - 1, :], xt[0:n, t - 1, :], rr[0:n, t - 1:t], None, ALU.mult).then_inc(xn_done, 1)
                    if t == 2:
                        dve.wait_ge(g_in, 16)
                    if t >= 2:
                        by_channel(t - 2)
                dve.wait_ge(wdt_in, 16)
                split(dve, wdt[:], wdth[:], wdtr[:], wdt_split, 1)

                def panels(kind, i, col, pairs, visits):
                    for b in range(2):
                        dve.wait_ge(panel_used[b], i + (pairs + 1))
                        dve.wait_ge(panel_in, i * 32 + (32 * pairs + 16 * b + 16))
                        split(dve, wp[:], wph[b][:], wpr[b][:], w_split, i * 4 + (4 * pairs + 2 * b + 2))

                runs(dve, panels)

            @block.scalar
            def _(act):
                for b in range(2):
                    act.sem_inc(panel_used[b], 1)
                for slot in range(1, NB):
                    act.sem_inc(evac_done[slot], 1)
                act.wait_ge(ss_init, 1)
                for t in range(NT):
                    n = rows_of(t)
                    act.wait_ge(x_in[t], 16)
                    if t:
                        act.wait_ge(ss_done, t)
                    act.activation(wpr[1][0:n, 0:2, :].bitcast(F32R), xt[0:n, t, :].rearrange("p (a b) -> p a b", b=PANEL), ACT.Square, accum_out=ss[0:n, t:t + 1]).then_inc(ss_done, 1)
                act.wait_ge(mm_done[0], 1)
                act.activation(c.dt[:, 0:NPT, :], bank[0][:, 0:NPT * SH].rearrange("p (t h) -> p t h", h=SH), ACT.Copy)
                act.activation(c.dt[0:DEC, NPT, :], bank[0][0:DEC, NPT * SH:NT * SH], ACT.Copy).then_inc(evac_done[0], 1)

                def evacuate(kind, i, col, pairs, visits):
                    U = UNITS[kind]
                    f = {"z": ACT.Silu, "g": ACT.Sigmoid}.get(kind, ACT.Copy)
                    for j in range(2 * U):
                        slot, u = j % NB, j % U
                        chan = kind in ("qk", "xbc")
                        n, w = (P, TS) if chan else (rows_of(u), PANEL)
                        act.wait_ge(mm_done[slot], i * per_pair(kind) + (visits + j // NB + 1 + (slot == 0)))
                        act.wait_ge(stored[slot], (i * per_pair(kind) + (visits + j // NB + 1)) * 16)
                        act.activation(stg[slot][0:n, 0:w], bank[slot][0:n, 0:w], f).then_inc(evac_done[slot], 1)
                        if u == U - 1:
                            act.sem_inc(panel_used[j // U], 1)

                runs(act, evacuate)

            @block.tensor
            def _(pe):
                for t in range(NT):
                    n = rows_of(t)
                    pe.wait_ge(xn_done, t + 1)
                    for h in range(2):
                        if t:
                            pe.wait_ge(hT_done, 2 * (t - 1) + h + 1)
                        for k in range(4):
                            mm = pe.transpose(tb[h][:, k, 0:n], xt[0:n, t, (4 * h + k) * P:(4 * h + k + 1) * P],
                                              c.ident[0:n, 0:n])
                        mm.then_inc(turned, 1)
                pe.wait_ge(wdt_split, 2)
                pe.wait_ge(h_split, 4 * NT)
                for t in range(NT):
                    n = rows_of(t)
                    here = slice(t * P, t * P + n)
                    mm = product(pe, bank[0][0:n, t * SH:(t + 1) * SH], [(hTh[:, k, here], hTr[:, k, here]) for k in range(DK)],
                                 [(wdth[:, k, :], wdtr[:, k, :]) for k in range(DK)])
                mm.then_inc(mm_done[0], 1)

                def products(kind, i, col, pairs, visits):
                    U = UNITS[kind]
                    for b in range(2):
                        pe.wait_ge(w_split, i * 4 + (4 * pairs + 2 * b + 3))
                        for u in range(U):
                            j = b * U + u
                            slot = j % NB
                            pe.wait_ge(evac_done[slot], i * per_pair(kind) + (visits + j // NB + 1))
                            if kind in ("qk", "xbc"):
                                blk, sl = divmod(u, NSPLIT)
                                cols, toks = slice(blk * P, (blk + 1) * P), slice(sl * TS, (sl + 1) * TS)
                                mm = product(pe, bank[slot][:, 0:TS], [(wph[b][:, k, cols], wpr[b][:, k, cols]) for k in range(DK)],
                                             [(hTh[:, k, toks], hTr[:, k, toks]) for k in range(DK)])
                            else:
                                n = rows_of(u)
                                toks = slice(u * P, u * P + n)
                                mm = product(pe, bank[slot][0:n, :], [(hTh[:, k, toks], hTr[:, k, toks]) for k in range(DK)],
                                             [(wph[b][:, k, :], wpr[b][:, k, :]) for k in range(DK)])
                            mm.then_inc(mm_done[slot], 1)

                runs(pe, products)


def build_distances(nc, negdist):
    with Stage(nc, "dist") as s:
        dist_i, dist_done = s.sem("dist_i"), s.sem("dist_done")
        iot = s.sb("iot", [P, SEQ], I32)
        with nc.Block() as block:

            @block.gpsimd
            def _(pool):
                pool.iota(iot[:], [[-1, SEQ]], base=SEQ - P, channel_multiplier=1).then_inc(dist_i, 1)

            @block.vector
            def _(dve):
                dve.wait_ge(dist_i, 1)
                dve.tensor_copy(negdist[:], iot[:]).then_inc(dist_done, 1)
                dve.wait_ge(dist_done, 1)
                dve.tensor_scalar(negdist[:], negdist[:], 4.0, None, ALU.mult).then_inc(dist_done, 1)
                dve.wait_ge(dist_done, 2)
                dve.scalar_tensor_tensor(out=negdist[:], in0=negdist[:], scalar=-1.0, in1=negdist[:],
                                         op0=ALU.mult, op1=ALU.min).then_inc(dist_done, 1)
                dve.wait_ge(dist_done, 3)
                dve.memset(negdist[0:CH, SEQ - CH:SEQ], NEG).then_inc(dist_done, 1)
                dve.wait_ge(dist_done, 4)


def differential_attention(nc, io, dr, c, negdist):
    SAMPLE = NPT
    STEPS = 2 * NT
    KC = PAST // P

    def groups(n):
        blocks = [(k, P) for k in range(n + 1)] if n < SAMPLE else [(k, P) for k in range(KC)] + [(KC, DEC)]
        return [blocks[g:g + 4] for g in range(0, len(blocks), 4)]

    jobs = [("k", 0, g) for g in range(4)]
    for m in range(1, STEPS + 1):
        if m == NT - 1:
            jobs += [("k", 1, g) for g in range(4)]
        jobs += [("w", m - 1, g) for g in range(len(groups((m - 1) % NT)))]
    assert len(jobs) % 2 == 0
    turn_of = {job: j for j, job in enumerate(jobs)}
    TURNS = len(jobs) // 2

    with Stage(nc, "attn") as s:
        qT = [s.sb(f"qT{b}", [P, T]) for b in range(2)]
        kT = [s.sb(f"kT{b}", [P, T]) for b in range(2)]
        vt = [s.sb(f"vt{b}", [P, NT, P]) for b in range(2)]
        kc = [s.sb(f"kc{b}", [P, KC, P]) for b in range(2)]
        vc = [s.sb(f"vc{b}", [P, KC, P]) for b in range(2)]
        kcT = [s.sb(f"kcT{b}", [P, PAST]) for b in range(2)]
        krow = [s.sb(f"krow{b}", [P, NT, P]) for b in range(2)]
        orow = [s.sb(f"orow{b}", [P, NT, P]) for b in range(2)]
        e = [[s.sb(f"e{j}{p}", [P, SEQ]) for p in range(2)] for j in range(2)]
        w = [s.sb(f"w{p}", [P, SEQ]) for p in range(2)]
        wT = [s.sb(f"wT{p}", [P, 4, P]) for p in range(2)]
        top = [s.sb(f"top{p}", [P, 2]) for p in range(2)]
        ntop = [s.sb(f"ntop{p}", [P, 2]) for p in range(2)]
        tot = [s.sb(f"tot{p}", [P, 2]) for p in range(2)]
        inv = [s.sb(f"inv{p}", [P, 2]) for p in range(2)]
        lv = s.sb("lv", [P, 4, AK])
        lp = s.sb("lp", [P, 2, AK])
        ld = s.sb("ld", [P, 2])
        le = s.sb("le", [P, 2])
        lam = s.sb("lam", [P, 1])
        S = [s.ps(f"S{j}", [P, SEQ]) for j in range(2)]
        tp = [s.ps(f"tp{p}", [P, 4, P]) for p in range(2)]
        ob = [s.ps(f"ob{p}", [P, 512]) for p in range(2)]

        lam_in, lam_step, lam_exp = s.sem("lam_in"), s.sem("lam_step"), s.sem("lam_exp")
        head_in, head_used, stored = s.sems("head_in", 2), s.sems("head_used", 2), s.sems("stored", 2)
        scored, biased, ntop_done, exp_done = s.sems("scored", 2), s.sems("biased", 2), s.sem("ntop_done"), s.sems("exp_done", 2)
        inv_done, scaled, w_done, slope_done = s.sem("inv_done"), s.sem("scaled"), s.sem("w_done"), s.sem("slope_done")
        turned, turn_out, o_done, o_out, gate = s.sems("turned", 2), s.sems("turn_out", 2), s.sem("o_done"), s.sem("o_out"), s.sem("gate")
        dve_gate, pe_gate = s.sem("dve_gate"), s.sem("pe_gate")

        def step_of(i, m, ahead=1):
            return i * STEPS + (m + ahead)

        def turn_val(i, j, ahead=1):
            return i * TURNS + (j // 2 + ahead)

        with nc.Block() as block:

            @block.gpsimd
            def _(pool):
                with pool.Fori(0, H // 2) as i:
                    for b in range(2):
                        pool.wait_ge(head_used[b], i + 1)
                        pool.sem_inc(gate, 1)
                        col = i * (2 * P) + b * P
                        pool.dma_start(qT[b][:], dr["chan"][bass.ds(col, P), :]).then_inc(head_in[b], 16)
                        pool.dma_start(kT[b][:], dr["chan"][bass.ds(col + C_K, P), :]).then_inc(head_in[b], 16)
                        cols = bass.ds(col, P)
                        pool.dma_start(vt[b][:, 0:NPT, :], io["v_prompt_out"].rearrange("(t p) c -> p t c", p=P)[:, :, cols]
                                       ).then_inc(head_in[b], 16)
                        pool.dma_start(vt[b][0:DEC, NPT, :], io["v_sample_out"][:, cols]).then_inc(head_in[b], 16)
                        pool.dma_start(kc[b][:], io["cache_k2"].rearrange("(t p) c -> p t c", p=P)[:, :, cols]
                                       ).then_inc(head_in[b], 16)
                        pool.dma_start(vc[b][:], io["cache_v2"].rearrange("(t p) c -> p t c", p=P)[:, :, cols]
                                       ).then_inc(head_in[b], 16)

            @block.sync
            def _(sp):
                for n, name in enumerate(("lam_q1", "lam_k1", "lam_q2", "lam_k2")):
                    sp.dma_start(lv[:, n, :], io[name].broadcast_to([P, AK])).then_inc(lam_in, 16)
                for b in range(2):
                    sp.sem_inc(stored[b], 64)
                with sp.Fori(0, H // 2) as i:
                    for b in range(2):
                        sp.wait_ge(o_out, step_of(i, NT * b + NT - 1, 3))
                        cols = bass.ds(i * (2 * P) + b * P, P)
                        sp.dma_start(io["k_prompt_out"].rearrange("(t p) c -> p t c", p=P)[:, :, cols],
                                     krow[b][:, 0:NPT, :]).then_inc(stored[b], 16)
                        sp.dma_start(io["k_sample_out"][:, cols], krow[b][0:DEC, NPT, :]).then_inc(stored[b], 16)
                        sp.dma_start(dr["att"][0:SEQ, :].rearrange("(t p) c -> p t c", p=P)[:, :, cols],
                                     orow[b][:, 0:NPT, :]).then_inc(stored[b], 16)
                        sp.dma_start(dr["att"][SEQ:T, cols], orow[b][0:DEC, NPT, :]).then_inc(stored[b], 16)
                for b in range(2):
                    sp.wait_ge(stored[b], 64 * (H // 2 + 1))

            @block.vector
            def _(dve):
                for j in range(2):
                    dve.sem_inc(biased[j], 1)
                dve.sem_inc(w_done, 2)
                dve.sem_inc(slope_done, 1)
                dve.wait_ge(lam_in, 64)
                lq = lv[:].rearrange("p (a b) k -> p a b k", b=2)
                dve.tensor_tensor(lp[:], lq[:, :, 0, :], lq[:, :, 1, :], ALU.mult).then_inc(lam_step, 1)
                dve.wait_ge(lam_step, 1)
                dve.tensor_reduce(ld[:], lp[:], AX_X, ALU.add).then_inc(lam_step, 1)
                dve.wait_ge(lam_exp, 1)
                dve.tensor_tensor(lam[:], le[:, 0:1], le[:, 1:2], ALU.subtract).then_inc(lam_step, 1)
                dve.wait_ge(lam_step, 3)
                dve.tensor_scalar(lam[:], lam[:], LAM_INIT, None, ALU.add).then_inc(lam_step, 1)
                dve.wait_ge(lam_step, 4)

                def shape_of(m):
                    n = m % NT
                    return (P, (n + 1) * P, SEQ - (n + 1) * P) if n < SAMPLE else (DEC, PAST + DEC, SEQ - P - PAST)

                def bias_and_max(i, m):
                    p = m % 2
                    r, W, off = shape_of(m)
                    dve.wait_ge(slope_done, i * 2 + (m // NT + 1))
                    dve.wait_ge(w_done, step_of(i, m))
                    for j in range(2):
                        hold(dve, dve_gate, scored[j], step_of(i, m))
                        dve.tensor_tensor_reduce(e[j][p][0:r, 0:W], S[j][0:r, 0:W], negdist[0:r, off:off + W], 1.0, -3.0e38,
                                                 ALU.add, ALU.max, top[p][0:r, j:j + 1]).then_inc(biased[j], 1)
                    for j in range(2):
                        dve.wait_ge(biased[j], step_of(i, m, 2))
                    dve.tensor_scalar(ntop[p][0:r, :], top[p][0:r, :], -AK ** -0.5, None, ALU.mult).then_inc(ntop_done, 1)

                def combine(i, m):
                    p = m % 2
                    r, W, _ = shape_of(m)
                    for j in range(2):
                        dve.wait_ge(exp_done[j], step_of(i, m))
                    dve.reciprocal(inv[p][0:r, :], tot[p][0:r, :]).then_inc(inv_done, 1)
                    dve.wait_ge(inv_done, step_of(i, m))
                    dve.tensor_scalar(e[1][p][0:r, 0:W], e[1][p][0:r, 0:W], inv[p][0:r, 1:2], lam[0:r, 0:1],
                                      ALU.mult, ALU.mult).then_inc(scaled, 1)
                    dve.wait_ge(scaled, step_of(i, m))
                    dve.wait_ge(o_done, step_of(i, m))
                    dve.scalar_tensor_tensor(out=w[p][0:r, 0:W], in0=e[0][p][0:r, 0:W], scalar=inv[p][0:r, 0:1],
                                             in1=e[1][p][0:r, 0:W], op0=ALU.mult, op1=ALU.subtract).then_inc(w_done, 1)

                with dve.Fori(0, H // 2) as i:
                    for m in range(STEPS + 1):
                        if m < STEPS:
                            bias_and_max(i, m)
                        if m % NT == NT - 1:
                            dve.tensor_scalar(negdist[:], negdist[:], 0.5, None, ALU.mult).then_inc(slope_done, 1)
                        if m:
                            combine(i, m - 1)

            @block.scalar
            def _(act):
                for b in range(2):
                    act.sem_inc(head_used[b], 1)
                    act.sem_inc(turn_out[b], 1)
                act.sem_inc(o_out, 2)
                act.wait_ge(lam_step, 2)
                act.activation(le[:], ld[:], ACT.Exp).then_inc(lam_exp, 1)

                def exps(i, m):
                    p = m % 2
                    r, W = (P, (m % NT + 1) * P) if m % NT < SAMPLE else (DEC, PAST + DEC)
                    act.wait_ge(ntop_done, step_of(i, m))
                    for j in range(2):
                        act.activation(e[j][p][0:r, 0:W], e[j][p][0:r, 0:W], ACT.Exp, bias=ntop[p][0:r, j:j + 1],
                                       scale=AK ** -0.5, accum_out=tot[p][0:r, j:j + 1]).then_inc(exp_done[j], 1)

                def weights_out(i, m):
                    r = P if m % NT < SAMPLE else DEC
                    for g, blocks in enumerate(groups(m % NT)):
                        j = turn_of["w", m, g]
                        act.wait_ge(turned[j % 2], turn_val(i, j))
                        act.wait_ge(o_done, step_of(i, m, 2))
                        full = [q for q in blocks if q[1] == P]
                        if full:
                            f = len(full)
                            act.activation(wT[j % 2][:, 0:f, 0:r], tp[j % 2][:, 0:f, 0:r], ACT.Copy).then_inc(turn_out[j % 2], 1)
                        else:
                            act.activation(wT[j % 2][0:DEC, 0, 0:r], tp[j % 2][0:DEC, 0, 0:r], ACT.Copy).then_inc(turn_out[j % 2], 1)

                def keys_out(i, b):
                    act.wait_ge(stored[b], (i + 1) * 64)
                    for g in range(4):
                        j = turn_of["k", b, g]
                        act.wait_ge(turned[j % 2], turn_val(i, j))
                        if g < 2:
                            a = act.activation(krow[b][:, 4 * g:4 * g + 4, :], tp[j % 2][:], ACT.Copy)
                        elif g == 2:
                            a = act.activation(krow[b][0:DEC, NPT, :], tp[j % 2][0:DEC, 0, :], ACT.Copy)
                        else:
                            a = act.activation(kcT[b][:].rearrange("p (t k) -> p t k", k=P), tp[j % 2][:], ACT.Copy)
                        a.then_inc(turn_out[j % 2], 1)

                def o_to_rows(i, m):
                    n, b = m % NT, m // NT
                    r = P if n < SAMPLE else DEC
                    act.wait_ge(o_done, step_of(i, m, 3))
                    act.activation(orow[b][0:r, n, :], ob[m % 2][0:r, 0:P], ACT.Copy).then_inc(o_out, 1)
                    if n == SAMPLE:
                        act.sem_inc(head_used[b], 1)

                with act.Fori(0, H // 2) as i:
                    keys_out(i, 0)
                    for m in range(STEPS + 2):
                        if m < STEPS:
                            exps(i, m)
                        if m == NT - 1:
                            keys_out(i, 1)
                        if 1 <= m <= STEPS:
                            weights_out(i, m - 1)
                        if m >= 2:
                            o_to_rows(i, m - 2)

            @block.tensor
            def _(pe):
                pe.sem_inc(o_done, 2)

                def keys_turned(i, b):
                    pe.wait_ge(head_in[b], (i + 1) * 96)
                    for g in range(4):
                        j = turn_of["k", b, g]
                        pe.wait_ge(turn_out[j % 2], turn_val(i, j))
                        out = tp[j % 2]
                        if g < 2:
                            for k in range(4):
                                t = pe.transpose(out[:, k, :], kT[b][:, (4 * g + k) * P:(4 * g + k + 1) * P], c.ident[:])
                        elif g == 2:
                            t = pe.transpose(out[0:DEC, 0, :], kT[b][:, SEQ:T], c.ident[:])
                        else:
                            for k in range(KC):
                                t = pe.transpose(out[:, k, :], kc[b][:, k, :], c.ident[:])
                        t.then_inc(turned[j % 2], 1)

                def scores(i, m):
                    b, n = m // NT, m % NT
                    for j in range(2):
                        hold(pe, pe_gate, biased[j], step_of(i, m))
                        half = slice(AK * j, AK * j + AK)
                        if n < SAMPLE:
                            W = (n + 1) * P
                            for k in range(0, W, 512):
                                x = min(W, k + 512)
                                mm = pe.matmul(S[j][:, k:x], qT[b][half, n * P:(n + 1) * P], kT[b][half, k:x],
                                               start=True, stop=True)
                        else:
                            jj = turn_of["k", b, 3]
                            hold(pe, pe_gate, turn_out[jj % 2], turn_val(i, jj, 2))
                            pe.matmul(S[j][0:DEC, 0:PAST], qT[b][half, SEQ:T], kcT[b][half, :], start=True, stop=True)
                            mm = pe.matmul(S[j][0:DEC, PAST:PAST + DEC], qT[b][half, SEQ:T], kT[b][half, SEQ:T],
                                           start=True, stop=True)
                        mm.then_inc(scored[j], 1)

                def weights_turned(i, m):
                    r = P if m % NT < SAMPLE else DEC
                    pe.wait_ge(w_done, step_of(i, m, 3))
                    for g, blocks in enumerate(groups(m % NT)):
                        j = turn_of["w", m, g]
                        hold(pe, pe_gate, turn_out[j % 2], turn_val(i, j))
                        for k, (blk, size) in enumerate(blocks):
                            t = pe.transpose(tp[j % 2][0:size, k, 0:r], w[m % 2][0:r, blk * P:blk * P + size],
                                             c.ident[0:r, 0:r])
                        t.then_inc(turned[j % 2], 1)

                def product(i, m):
                    b, n = m // NT, m % NT
                    r = P if n < SAMPLE else DEC
                    pe.wait_ge(o_out, step_of(i, m))
                    gs = groups(n)
                    for g, blocks in enumerate(gs):
                        j = turn_of["w", m, g]
                        hold(pe, pe_gate, turn_out[j % 2], turn_val(i, j, 2))
                        for k, (blk, size) in enumerate(blocks):
                            val = (vt[b][:, blk, :] if n < SAMPLE else vc[b][:, blk, :] if size == P
                                   else vt[b][0:DEC, NPT, :])
                            mm = pe.matmul(ob[m % 2][0:r, 0:P], wT[j % 2][0:size, k, 0:r], val,
                                           start=(g == 0 and k == 0), stop=(g == len(gs) - 1 and k == len(blocks) - 1))
                    mm.then_inc(o_done, 1)

                with pe.Fori(0, H // 2) as i:
                    keys_turned(i, 0)
                    scores(i, 0)
                    for m in range(STEPS + 2):
                        if m == NT - 1:
                            keys_turned(i, 1)
                        if m + 1 < STEPS:
                            scores(i, m + 1)
                        if 1 <= m <= STEPS:
                            weights_turned(i, m - 1)
                        if m >= 2:
                            product(i, m - 2)


def attend(nc, io, dr, c):
    with Stage(nc, "bias") as s:
        negdist = s.sb("negdist", [P, SEQ])
        build_distances(nc, negdist)
        differential_attention(nc, io, dr, c, negdist)


def causal_convolution(nc, io, dr, c):
    BLOCKS = SCD // P
    RUNS = [("x", SIN // P), ("B", SG), ("C", SG)]
    PRE = SCONV - 1
    S0 = PRE + SEQ
    LEN = S0 + PRE + DEC
    OUT = LEN - PRE
    with Stage(nc, "conv") as s:
        taps = s.sb("taps", [(SCONV + 1) * BLOCKS, P])
        tapsT = s.sb("tapsT", [P, SCONV + 1, BLOCKS])
        past = s.sb("past", [PRE * BLOCKS, P])
        pastT = s.sb("pastT", [P, PRE, BLOCKS])
        tail = s.sb("tail", [P, 2, BLOCKS, PRE])
        tailr = s.sb("tailr", [P, 2, PRE, BLOCKS])
        tailT = s.sb("tailT", [PRE * BLOCKS, 2, P])
        xb = [s.sb(f"xb{b}", [P, LEN]) for b in range(2)]
        cv = [s.sb(f"cv{b}", [P, OUT]) for b in range(2)]
        ya = [s.sb(f"ya{b}", [P, OUT]) for b in range(2)]
        rows = [s.sb(f"rows{b}", [P, NT, P]) for b in range(2)]
        tp = [[s.ps(f"tp{b}{q}", [P, 4, P]) for q in range(3)] for b in range(2)]
        small = s.ps("small", [P, 512])

        taps_in, tail_in, small_turned, small_out, tail_regrouped = (s.sem(n) for n in ("taps_in", "tail_in", "small_turned", "small_out", "tail_regrouped"))
        xb_in, past_put, zeroed = s.sems("xb_in", 2), s.sems("past_put", 2), s.sem("zeroed")
        convolved, activated = s.sems("convolved", 2), s.sems("activated", 2)
        turned, rows_out = s.sems("turned", 2), s.sems("rows_out", 2)
        stored_rows, stored_chan, tail_stored, gate = s.sems("stored_rows", 2), s.sems("stored_chan", 2), s.sem("tail_stored"), s.sem("gate")

        def runs(eng, body):
            v = vr = vc = blk = 0
            for kind, n in RUNS:
                with eng.Fori(0, n // 2) as i:
                    body(kind, i, v, vr, vc, blk)
                v += n // 2
                vr += n // 2 if kind != "C" else 0
                vc += n // 2 if kind != "x" else 0
                blk += n

        with nc.Block() as block:

            @block.gpsimd
            def _(pool):
                for b in range(2):
                    pool.memset(xb[b][:, 0:PRE], 0.0).then_inc(zeroed, 1)
                pool.wait_ge(small_out, 2)

                def loads(kind, i, v, vr, vc, blk):
                    for b in range(2):
                        n = i * 2 + (blk + b)
                        hold(pool, gate, convolved[b], (i + (v + 1)) * 4)
                        row = i * (2 * P) + ((blk + b) * P + C_V)
                        pool.tensor_copy(xb[b][:, S0:S0 + PRE], pastT[:, :, bass.ds(n, 1)].rearrange("p r c -> p (r c)")).then_inc(past_put[b], 1)
                        pool.dma_start(xb[b][:, PRE:S0], dr["chan"][bass.ds(row, P), 0:SEQ]).then_inc(xb_in[b], 16)
                        pool.dma_start(xb[b][:, S0 + PRE:LEN], dr["chan"][bass.ds(row, P), SEQ:T]).then_inc(xb_in[b], 16)

                runs(pool, loads)

            @block.sync
            def _(sp):
                sp.dma_start(taps[0:SCONV * BLOCKS, :], io["conv_w"][0].rearrange("r (c p) -> (r c) p", p=P)).then_inc(taps_in, 16)
                sp.dma_start(taps[SCONV * BLOCKS:, :], io["conv_b"].rearrange("a (c p) -> (a c) p", p=P)).then_inc(taps_in, 16)
                sp.dma_start(past[:], io["state_conv"][0, 0].rearrange("r (c p) -> (r c) p", p=P)).then_inc(taps_in, 16)
                xbc = dr["chan"][C_V:C_V + SCD, :].rearrange("(c p) t -> p c t", p=P)
                sp.dma_start(tail[:, 0, :, :], xbc[:, :, SEQ - PRE:SEQ]).then_inc(tail_in, 16)
                sp.dma_start(tail[:, 1, :, :], xbc[:, :, T - PRE:T]).then_inc(tail_in, 16)
                sp.wait_ge(small_out, 4)
                for q, name in enumerate(("conv_prompt_out", "conv_sample_out")):
                    sp.dma_start(io[name].rearrange("r (c p) -> (r c) p", p=P), tailT[:, q, :]).then_inc(tail_stored, 16)
                for b in range(2):
                    sp.sem_inc(stored_rows[b], 32)
                    sp.sem_inc(stored_chan[b], 32)

                def stores(kind, i, v, vr, vc, blk):
                    for b in range(2):
                        if kind != "x":
                            row = i * (2 * P) + (blk + b - SIN // P) * P
                            sp.wait_ge(activated[b], i + (v + 2))
                            sp.dma_start(dr["bc"][bass.ds(row, P), 0:SEQ], ya[b][:, 0:SEQ]).then_inc(stored_chan[b], 16)
                            sp.dma_start(dr["bc"][bass.ds(row, P), SEQ:T], ya[b][:, S0:S0 + DEC]).then_inc(stored_chan[b], 16)
                        if kind != "C":
                            cols = bass.ds(i * (2 * P) + (blk + b) * P, P)
                            sp.wait_ge(rows_out[b], (i + (vr + 2)) * 3)
                            sp.dma_start(dr["xtok"][0:SEQ, :].rearrange("(t p) c -> p t c", p=P)[:, :, cols],
                                         rows[b][:, 0:NPT, :]).then_inc(stored_rows[b], 16)
                            sp.dma_start(dr["xtok"][SEQ:T, cols], rows[b][0:DEC, NPT, :]).then_inc(stored_rows[b], 16)

                runs(sp, stores)
                sp.wait_ge(tail_stored, 32)
                for b in range(2):
                    sp.wait_ge(stored_rows[b], 32 * (1 + (SIN // P + SG) // 2))
                    sp.wait_ge(stored_chan[b], 32 * (1 + SG))

            @block.vector
            def _(dve):
                for b in range(2):
                    dve.sem_inc(convolved[b], 4)
                dve.wait_ge(tail_in, 32)
                for q in range(2):
                    dve.tensor_copy(tailr[:, q, :, :], tail[:, q, :, :].rearrange("p c r -> p r c")).then_inc(tail_regrouped, 1)
                dve.wait_ge(zeroed, 2)
                dve.wait_ge(small_out, 2)

                def convolve(kind, i, v, vr, vc, blk):
                    for b in range(2):
                        n = i * 2 + (blk + b)
                        base = (i + (v + 1)) * 4

                        def tap(k):
                            return tapsT[:, k, bass.ds(n, 1)]

                        dve.wait_ge(xb_in[b], (i + (v + 1)) * 32)
                        dve.wait_ge(past_put[b], i + (v + 1))
                        dve.wait_ge(activated[b], i + (v + 1))
                        dve.tensor_scalar(cv[b][:], xb[b][:, PRE:LEN], tap(PRE), tap(SCONV), ALU.mult, ALU.add).then_inc(convolved[b], 1)
                        for k in range(PRE):
                            dve.wait_ge(convolved[b], base + (k + 1))
                            dve.scalar_tensor_tensor(out=cv[b][:], in0=xb[b][:, k:k + OUT], scalar=tap(k), in1=cv[b][:],
                                                     op0=ALU.mult, op1=ALU.add).then_inc(convolved[b], 1)

                runs(dve, convolve)

            @block.scalar
            def _(act):
                for b in range(2):
                    act.sem_inc(activated[b], 1)
                    act.sem_inc(rows_out[b], 3)
                act.wait_ge(small_turned, 4)
                act.activation(tapsT[:].rearrange("p r c -> p (r c)"), small[:, 0:(SCONV + 1) * BLOCKS], ACT.Copy).then_inc(small_out, 1)
                act.activation(pastT[:].rearrange("p r c -> p (r c)"), small[:, P:P + PRE * BLOCKS], ACT.Copy).then_inc(small_out, 1)
                for q in range(2):
                    act.activation(tailT[:, q, :], small[0:PRE * BLOCKS, (2 + q) * P:(3 + q) * P], ACT.Copy).then_inc(small_out, 1)

                def activate(kind, i, v, vr, vc, blk):
                    for b in range(2):
                        act.wait_ge(convolved[b], (i + (v + 2)) * 4)
                        act.wait_ge(turned[b], i * (3 if kind != "C" else 0) + (vr + 1) * 3)
                        act.wait_ge(stored_chan[b], i * (32 if kind != "x" else 0) + (vc + 1) * 32)
                        act.activation(ya[b][:], cv[b][:], ACT.Silu).then_inc(activated[b], 1)
                    for b in range(2):
                        if kind == "C":
                            continue
                        act.wait_ge(stored_rows[b], (i + (vr + 1)) * 32)
                        for q in range(3):
                            act.wait_ge(turned[b], i * 3 + (vr * 3 + q + 4))
                            if q < 2:
                                a = act.activation(rows[b][:, 4 * q:4 * q + 4, :], tp[b][q][:], ACT.Copy)
                            else:
                                a = act.activation(rows[b][0:DEC, NPT, :], tp[b][q][0:DEC, 0, :], ACT.Copy)
                            a.then_inc(rows_out[b], 1)

                runs(act, activate)

            @block.tensor
            def _(pe):
                for b in range(2):
                    pe.sem_inc(turned[b], 3)
                pe.wait_ge(taps_in, 48)
                n = (SCONV + 1) * BLOCKS
                pe.transpose(small[:, 0:n], taps[:], c.ident[0:n, 0:n]).then_inc(small_turned, 1)
                n = PRE * BLOCKS
                pe.transpose(small[:, P:P + n], past[:], c.ident[0:n, 0:n]).then_inc(small_turned, 1)
                for q in range(2):
                    pe.wait_ge(tail_regrouped, q + 1)
                    pe.transpose(small[0:n, (2 + q) * P:(3 + q) * P], tailr[:, q, :, :].rearrange("p r c -> p (r c)"),
                                 c.ident[:]).then_inc(small_turned, 1)

                def turn(kind, i, v, vr, vc, blk):
                    if kind == "C":
                        return
                    for b in range(2):
                        pe.wait_ge(activated[b], i + (v + 2))
                        for q in range(3):
                            pe.wait_ge(rows_out[b], i * 3 + (vr * 3 + q + 1))
                            if q < 2:
                                for k in range(4):
                                    t = pe.transpose(tp[b][q][:, k, :], ya[b][:, (4 * q + k) * P:(4 * q + k + 1) * P], c.ident[:])
                            else:
                                t = pe.transpose(tp[b][q][0:DEC, 0, :], ya[b][:, S0:S0 + DEC], c.ident[:])
                            t.then_inc(turned[b], 1)

                runs(pe, turn)


def step_sizes(nc, io, c, m):
    with Stage(nc, "dt") as s:
        W = [P, NT, SH]
        bias, alog = s.sb("bias", [P, SH]), s.sb("alog", [P, SH])
        z, e, u, ln, d0, one, acum = (s.sb(n, W) for n in ("z", "e", "u", "ln", "d0", "one", "acum"))
        cum, last = s.ps("cum", [P, 512]), s.ps("last", [P, 512])
        vec_in, v, a, p = s.sem("vec_in"), s.sem("dve_step"), s.sem("act_step"), s.sem("pe_step")

        def wide(x):
            return x[:].unsqueeze(1).broadcast_to(W)

        def flat(x):
            return x[:].rearrange("p t h -> p (t h)")

        cums, lasts = cum[:, 0:NT * SH], last[:, 0:NT * SH]
        with nc.Block() as block:

            @block.sync
            def _(sp):
                sp.dma_start(bias[:], io["dt_bias"].broadcast_to([P, SH])).then_inc(vec_in, 16)
                sp.dma_start(alog[:], io["a_log"].broadcast_to([P, SH])).then_inc(vec_in, 16)

            @block.vector
            def _(dve):
                count = [0]

                def step(ins):
                    ins.then_inc(v, 1)
                    count[0] += 1
                    dve.wait_ge(v, count[0])

                dve.wait_ge(vec_in, 32)
                step(dve.tensor_tensor(z[:], c.dt[:], wide(bias), ALU.add))
                step(dve.scalar_tensor_tensor(out=flat(e), in0=flat(z), scalar=-1.0, in1=flat(z), op0=ALU.mult, op1=ALU.min))
                dve.wait_ge(a, 1)
                step(dve.tensor_scalar(u[:], e[:], 1.0, None, ALU.add))
                step(dve.tensor_scalar(d0[:], u[:], -1.0, None, ALU.add))
                step(dve.tensor_scalar(one[:], d0[:], 0.0, None, ALU.is_equal))
                step(dve.tensor_tensor(d0[:], d0[:], one[:], ALU.add))
                step(dve.reciprocal(d0[:], d0[:]))
                step(dve.tensor_tensor(d0[:], d0[:], e[:], ALU.mult))
                dve.wait_ge(a, 2)
                step(dve.tensor_tensor(ln[:], ln[:], one[:], ALU.add))
                step(dve.tensor_tensor(ln[:], ln[:], d0[:], ALU.mult))
                step(dve.scalar_tensor_tensor(out=flat(c.dt), in0=flat(z), scalar=0.0, in1=flat(ln), op0=ALU.max, op1=ALU.add))
                step(dve.memset(c.dt[DEC:2 * DEC, NPT, :], 0.0))
                step(dve.memset(c.dt[2 * DEC:P, NPT, :], 0.0))
                dve.wait_ge(a, 3)
                step(dve.tensor_scalar(alog[:], alog[:], -1.0, None, ALU.mult))
                step(dve.tensor_tensor(m.da[:], c.dt[:], wide(alog), ALU.mult))
                assert count[0] == 15
                dve.wait_ge(p, 3)
                dve.wait_ge(a, 5)
                step(dve.tensor_copy(flat(acum), cums))
                step(dve.tensor_tensor(flat(acum), lasts, flat(acum), ALU.subtract))
                dve.wait_ge(a, 6)
                step(dve.tensor_tensor(m.wdec[:], m.wdec[:], c.dt[:], ALU.mult))

            @block.scalar
            def _(act):
                act.wait_ge(v, 2)
                act.activation(e[:], e[:], ACT.Exp).then_inc(a, 1)
                act.wait_ge(v, 3)
                act.activation(ln[:], u[:], ACT.Ln).then_inc(a, 1)
                act.wait_ge(vec_in, 32)
                act.activation(alog[:], alog[:], ACT.Exp).then_inc(a, 1)
                act.wait_ge(p, 3)
                act.activation(flat(m.ecum), cums, ACT.Exp).then_inc(a, 1)
                act.activation(flat(m.elast), lasts, ACT.Exp).then_inc(a, 1)
                act.wait_ge(v, 17)
                act.activation(m.wdec[:], acum[:], ACT.Exp).then_inc(a, 1)

            @block.tensor
            def _(pe):
                pe.wait_ge(v, 15)
                pe.matmul(cums, c.upper[:], flat(m.da), start=True, stop=True).then_inc(p, 1)
                pe.matmul(last[:, 0:NPT * SH], c.ones[:], m.da[:, 0:NPT, :].rearrange("p t h -> p (t h)"),
                          start=True, stop=True).then_inc(p, 1)
                pe.matmul(last[:, NPT * SH:NT * SH], c.ones[0:DEC, :], m.da[0:DEC, NPT, :], start=True, stop=True).then_inc(p, 1)


def state_in(nc, src, m, c):
    with Stage(nc, "hin") as s:
        raw = s.sb("raw", [P, SIN // P, P])
        tp = [s.ps(f"tp{q}", [P, 4, P]) for q in range(4)]
        raw_in, turned, out = s.sem("raw_in"), s.sem("turned"), s.sem("out")
        with nc.Block() as block:

            @block.gpsimd
            def _(pool):
                pool.dma_start(raw[:], src.rearrange("(b p) n -> p b n", p=P)).then_inc(raw_in, 16)

            @block.tensor
            def _(pe):
                pe.wait_ge(raw_in, 16)
                for q in range(4):
                    for k in range(4):
                        t = pe.transpose(tp[q][:, k, :], raw[:, 4 * q + k, :], c.ident[:])
                    t.then_inc(turned, 1)

            @block.vector
            def _(dve):
                for q in range(4):
                    dve.wait_ge(turned, q + 1)
                    dve.tensor_copy(m.state[:, 512 * q:512 * q + 512], tp[q][:].rearrange("p k n -> p (k n)")).then_inc(out, 1)


def state_out(nc, dst, m, c, tag):
    with Stage(nc, tag) as s:
        raw = s.sb("raw", [P, SIN // P, P])
        tp = [s.ps(f"tp{q}", [P, 4, P]) for q in range(4)]
        turned, out, stored = s.sem("turned"), s.sem("out"), s.sem("stored")
        with nc.Block() as block:

            @block.tensor
            def _(pe):
                for q in range(4):
                    for k in range(4):
                        t = pe.transpose(tp[q][:, k, :], m.state[:, (4 * q + k) * P:(4 * q + k + 1) * P], c.ident[:])
                    t.then_inc(turned, 1)

            @block.vector
            def _(dve):
                for q in range(4):
                    dve.wait_ge(turned, q + 1)
                    dve.tensor_copy(raw[:, 4 * q:4 * q + 4, :], tp[q][:]).then_inc(out, 1)

            @block.sync
            def _(sp):
                sp.wait_ge(out, 4)
                sp.dma_start(dst.rearrange("(b p) n -> p b n", p=P), raw[:]).then_inc(stored, 16)
                sp.wait_ge(stored, 16)


def ssd_scan(nc, io, dr, c, m, sample):
    G = SG
    GH = SH // SG
    GW = GH * SP_
    r = DEC if sample else P
    TL = r
    PAIRS = 1 if sample else NPT // 2
    BODY = 1 if sample else 2
    with Stage(nc, "ssds" if sample else "ssdp") as s:
        xt = [s.sb(f"xt{b}", [P, SIN + G * SN]) for b in range(2)]
        bc = [s.sb(f"bc{b}", [P, 2 * G, TL]) for b in range(2)]
        zt = [s.sb(f"zt{b}", [P, SIN]) for b in range(2)]
        R = [s.sb(f"R{q}", [P, GH, TL]) for q in range(2)]
        L = [s.sb(f"L{q}", [P, GH, TL]) for q in range(2)]
        M = [s.sb(f"M{g}", [P, GH, TL]) for g in range(G)]
        cbm = s.sb("cbm", [P, G, TL])
        dtx, dx, wx = s.sb("dtx", [P, SIN]), s.sb("dx", [P, SIN]), s.sb("wx", [P, SIN])
        carried = s.sb("carried", [P, GW])
        y = [s.sb(f"y{b}", [P, SIN]) for b in range(2)]
        yn = [s.sb(f"yn{b}", [P, SIN]) for b in range(2)]
        ss, ms, rr = (s.sb(n, [P, G]) for n in ("ss", "ms", "rr"))
        skip = s.sb("skip", [P, SH])
        seg = [s.ps(f"seg{q}", [P, GH * TL if not sample else 1024]) for q in range(2)]
        cb, yp, yi, hs = (s.ps(n, [P, 512]) for n in ("cb", "yp", "yi", "hs"))

        new_state = [hs, cb]

        pe_gate, pool_gate = s.sem("pe_gate"), s.sem("pool_gate")
        skip_in, tile_in, tile_used, yn_stored = s.sem("skip_in"), s.sems("tile_in", 2), s.sems("tile_used", 2), s.sems("yn_stored", 2)
        R_done, seg_done, L_done, M_done = s.sem("R_done"), s.sem("seg_done"), s.sem("L_done"), s.sem("M_done")
        cb_done, cbm_done, dtx_done, dx_done, wx_done = (s.sem(n) for n in ("cb_done", "cbm_done", "dtx_done", "dx_done", "wx_done"))
        yi_done, yp_done, y_step, hs_done, h_step = (s.sem(n) for n in ("yi_done", "yp_done", "y_step", "hs_done", "h_step"))
        ss_done, ms_done, rr_done, yn_done, state_zero = (s.sem(n) for n in ("ss_done", "ms_done", "rr_done", "yn_done", "state_zero"))

        def tiles(eng, body):
            if sample:
                body(0, 0)
            else:
                with eng.Fori(0, PAIRS) as i:
                    for b in range(BODY):
                        body(i, b)

        def val(i, b, per, ahead):
            return i * (BODY * per) + (b * per + ahead)

        def cols(i, b):
            return slice(NPT, NT) if sample else bass.ds(i * 2 + b, 1)

        def tok(i, b):
            return slice(SEQ, T) if sample else bass.ds(i * (2 * P) + b * P, P)

        def by_head(x, i, b, width, g0=0, g1=SH):
            return x[0:r, cols(i, b), g0:g1].rearrange("p t h -> p (t h)").unsqueeze(2).broadcast_to([r, g1 - g0, width])

        def heads(x):
            return x.rearrange("p (h q) -> p h q", q=SP_)

        def of_group(g):
            return slice(g * GW, (g + 1) * GW)

        with nc.Block() as block:

            @block.sync
            def _(sp):
                sp.dma_start(skip[:], io["d_skip"].broadcast_to([P, SH])).then_inc(skip_in, 16)

                def loads(i, b):
                    sp.wait_ge(tile_used[b], i + 1)
                    sp.dma_start(xt[b][0:r, :], dr["xtok"][tok(i, b), :]).then_inc(tile_in[b], 16)
                    sp.dma_start(bc[b][:], dr["bc"].rearrange("(g p) t -> p g t", p=P)[:, :, tok(i, b)]).then_inc(tile_in[b], 16)
                    sp.dma_start(zt[b][0:r, :], dr["zs"][tok(i, b), :]).then_inc(tile_in[b], 16)

                tiles(sp, loads)
                for b in range(BODY):
                    sp.wait_ge(yn_stored[b], 16 * (PAIRS + 1))

            @block.gpsimd
            def _(pool):
                pool.wait_ge(skip_in, 16)

                def tile(i, b):
                    pool.wait_ge(tile_in[b], (i + 1) * 48)
                    pool.wait_ge(h_step, val(i, b, 5, 5))
                    pool.tensor_tensor(heads(dx[0:r, :]), heads(xt[b][0:r, 0:SIN]),
                                       skip[0:r, :].unsqueeze(2).broadcast_to([r, SH, SP_]), ALU.mult).then_inc(dx_done, 1)
                    pool.tensor_tensor(heads(wx[0:r, :]), heads(xt[b][0:r, 0:SIN]), by_head(m.wdec, i, b, SP_), ALU.mult).then_inc(wx_done, 1)
                    hold(pool, pool_gate, ss_done, val(i, b, G, G))
                    pool.tensor_scalar(ms[0:r, :], ss[0:r, :], 1.0 / GW, EPS, ALU.mult, ALU.add).then_inc(ms_done, 1)
                    pool.wait_ge(ms_done, val(i, b, 1, 1))
                    pool.tensor_tensor(rr[0:r, :], ms[0:r, :], c.neghalf[0:r, 0:G], ALU.pow).then_inc(rr_done, 1)

                tiles(pool, tile)

            @block.scalar
            def _(act):
                act.sem_inc(L_done, 2)
                act.sem_inc(yn_done, 2 * G)
                for b in range(BODY):
                    act.sem_inc(yn_stored[b], 16)

                def tile(i, b):
                    for g in range(G):
                        act.wait_ge(seg_done, val(i, b, G, g + 3))
                        act.wait_ge(M_done, val(i, b, G, g + 1))
                        act.activation(L[g % 2][0:r], seg[g % 2][0:r, 0:GH * TL].rearrange("p (h l) -> p h l", h=GH),
                                       ACT.Exp).then_inc(L_done, 1)
                    act.wait_ge(yn_stored[b], (i + 1) * 16)
                    for g in range(G):
                        act.wait_ge(y_step, val(i, b, 4 * G, 4 * g + 8))
                        act.activation(yn[b][0:r, of_group(g)], y[b][0:r, of_group(g)], ACT.Square, accum_out=ss[0:r, g:g + 1]).then_inc(ss_done, 1)
                    act.wait_ge(rr_done, val(i, b, 1, 1))
                    for g in range(G):
                        act.activation(yn[b][0:r, of_group(g)], y[b][0:r, of_group(g)], ACT.Copy,
                                       scale=rr[0:r, g:g + 1]).then_inc(yn_done, 1)
                    act.wait_ge(yn_done, val(i, b, G, 3 * G))
                    act.dma_start(dr["yg"][tok(i, b), :], yn[b][0:r, :]).then_inc(yn_stored[b], 16)

                tiles(act, tile)

            @block.vector
            def _(dve):
                dve.sem_inc(M_done, 2)
                dve.sem_inc(cbm_done, 1)
                dve.sem_inc(y_step, 4)
                dve.sem_inc(h_step, 5)
                if not sample:
                    dve.memset(m.state[:], 0.0).then_inc(state_zero, 1)
                    dve.wait_ge(state_zero, 1)
                for b in range(BODY):
                    dve.sem_inc(tile_used[b], 1)

                def tile(i, b):
                    def decays(g):
                        dve.wait_ge(seg_done, val(i, b, G, g + 1))
                        dve.tensor_tensor(R[g % 2][0:r], by_head(m.da, i, b, TL, g * GH, (g + 1) * GH),
                                          c.upper[0:r, 0:TL].unsqueeze(1).broadcast_to([r, GH, TL]), ALU.mult).then_inc(R_done, 1)

                    def mix(g):
                        dve.wait_ge(L_done, val(i, b, G, g + 3))
                        dve.tensor_tensor(M[g][0:r], L[g % 2][0:r], cbm[0:r, g, :].unsqueeze(1).broadcast_to([r, GH, TL]),
                                          ALU.mult).then_inc(M_done, 1)

                    def output(g):
                        own = val(i, b, 4 * G, 4 * g + 4)
                        dve.wait_ge(yi_done, val(i, b, G, g + 1))
                        dve.tensor_tensor(heads(carried[0:r, :]), heads(yi[0:r, 0:GW]), by_head(m.ecum, i, b, SP_, g * GH, (g + 1) * GH),
                                          ALU.mult).then_inc(y_step, 1)
                        dve.wait_ge(y_step, own + 1)
                        dve.wait_ge(yp_done, val(i, b, G, g + 1))
                        dve.wait_ge(yn_done, val(i, b, G, G))
                        dve.tensor_tensor(y[b][0:r, of_group(g)], yp[0:r, 0:GW], carried[0:r, :], ALU.add).then_inc(y_step, 1)
                        dve.wait_ge(y_step, own + 2)
                        dve.wait_ge(dx_done, val(i, b, 1, 1))
                        dve.tensor_tensor(y[b][0:r, of_group(g)], y[b][0:r, of_group(g)], dx[0:r, of_group(g)], ALU.add).then_inc(y_step, 1)
                        dve.wait_ge(y_step, own + 3)
                        dve.tensor_tensor(y[b][0:r, of_group(g)], y[b][0:r, of_group(g)], zt[b][0:r, of_group(g)], ALU.mult).then_inc(y_step, 1)

                    dve.wait_ge(tile_in[b], (i + 1) * 48)
                    decays(0)
                    decays(1)
                    dve.wait_ge(cb_done, val(i, b, 1, 1))
                    dve.tensor_tensor(cbm[0:r], cb[0:r, 0:G * TL].rearrange("p (g l) -> p g l", g=G),
                                      c.upper[0:r, 0:TL].unsqueeze(1).broadcast_to([r, G, TL]), ALU.mult).then_inc(cbm_done, 1)
                    dve.tensor_tensor(heads(dtx[0:r, :]), heads(xt[b][0:r, 0:SIN]), by_head(c.dt, i, b, SP_), ALU.mult).then_inc(dtx_done, 1)
                    dve.wait_ge(cbm_done, val(i, b, 1, 2))
                    mix(0)
                    decays(2)
                    mix(1)
                    decays(3)
                    mix(2)
                    output(0)
                    mix(3)
                    output(1)
                    output(2)
                    output(3)
                    elast = m.elast[:, cols(i, b), :].rearrange("p t h -> p (t h)").unsqueeze(2).broadcast_to([P, SH, SP_])
                    dve.tensor_tensor(heads(m.state[:]), heads(m.state[:]), elast, ALU.mult).then_inc(h_step, 1)
                    dve.wait_ge(h_step, val(i, b, 5, 6))
                    for g in range(G):
                        dve.wait_ge(hs_done, val(i, b, G, g + 1))
                        dve.tensor_tensor(m.state[:, of_group(g)], m.state[:, of_group(g)], new_state[g % 2][:, 0:GW], ALU.add).then_inc(h_step, 1)
                    dve.wait_ge(h_step, val(i, b, 5, 10))
                    dve.sem_inc(tile_used[b], 1)

                tiles(dve, tile)

            @block.tensor
            def _(pe):
                pe.sem_inc(seg_done, 2)

                def tile(i, b):
                    def decay_sums(g):
                        pe.wait_ge(R_done, val(i, b, G, g + 1))
                        hold(pe, pe_gate, L_done, val(i, b, G, g + 1))
                        flat = R[g % 2][0:r].rearrange("p h l -> p (h l)")
                        for k in range(0, GH * TL, 512):
                            x = min(k + 512, GH * TL)
                            mm = pe.matmul(seg[g % 2][0:r, k:x], c.below[0:r, 0:r], flat[:, k:x], start=True, stop=True)
                        mm.then_inc(seg_done, 1)

                    def from_state(g):
                        hold(pe, pe_gate, y_step, val(i, b, 4 * G, 4 * g + 1))
                        pe.matmul(yi[0:r, 0:GW], bc[b][:, G + g, :], m.state[:, of_group(g)], start=True, stop=True).then_inc(yi_done, 1)

                    def within(g):
                        pe.wait_ge(M_done, val(i, b, G, g + 3))
                        hold(pe, pe_gate, y_step, val(i, b, 4 * G, 4 * g + 2))
                        for h in range(GH):
                            at = (g * GH + h) * SP_
                            mm = pe.matmul(yp[0:r, h * SP_:(h + 1) * SP_], M[g][0:r, h, :], dtx[0:r, at:at + SP_], start=True, stop=True)
                        mm.then_inc(yp_done, 1)

                    pe.wait_ge(tile_in[b], (i + 1) * 48)
                    hold(pe, pe_gate, h_step, val(i, b, 5, 5))
                    for g in range(G):
                        mm = pe.matmul(cb[0:r, g * TL:(g + 1) * TL], bc[b][:, g, :], bc[b][:, G + g, :], start=True, stop=True)
                    mm.then_inc(cb_done, 1)
                    decay_sums(0)
                    decay_sums(1)
                    from_state(0)
                    pe.wait_ge(dtx_done, val(i, b, 1, 1))
                    within(0)
                    decay_sums(2)
                    decay_sums(3)
                    for g in range(1, G):
                        from_state(g)
                        within(g)
                    pe.wait_ge(wx_done, val(i, b, 1, 1))
                    for g in range(G):
                        hold(pe, pe_gate, h_step, val(i, b, 5, g + 5 if g > 1 else 5))
                        pe.matmul(new_state[g % 2][:, 0:GW], xt[b][0:r, SIN + g * SN:SIN + (g + 1) * SN], wx[0:r, of_group(g)],
                                  start=True, stop=True).then_inc(hs_done, 1)

                tiles(pe, tile)


class SsmHeld:

    def __init__(self, s):
        self.da, self.ecum, self.elast, self.wdec = (s.sb(n, [P, NT, SH]) for n in ("da", "ecum", "elast", "wdec"))
        self.state = s.sb("state", [P, SIN])


def state_space(nc, io, dr, c):
    with Stage(nc, "ssm") as s:
        m = SsmHeld(s)
        step_sizes(nc, io, c, m)
        ssd_scan(nc, io, dr, c, m, sample=False)
        state_out(nc, io["ssm_prompt_out"], m, c, "houtp")
        state_in(nc, io["state_ssm"][0, 0].rearrange("h p n -> (h p) n"), m, c)
        ssd_scan(nc, io, dr, c, m, sample=True)
        state_out(nc, io["ssm_sample_out"], m, c, "houts")


def over_tiles(eng, step):
    step(0, 0, 0, P, P)
    with eng.Fori(0, (NPT - 2) // 2) as i:
        step(i * 2 + 1, i, 1, P, P)
        step(i * 2 + 2, i + 1, 0, P, P)
    step(NPT - 1, NPT // 2 - 1, 1, P, DEC)
    step(NPT, NPT // 2, 0, DEC, None)


def tokens(t, r):
    return slice(SEQ, T) if r == DEC else bass.ds(t * P, P)


def mix_branches(nc, io, dr, c):
    OT, YT = D // P, SIN // P
    HALF = 512
    OY = 2 + 4
    with Stage(nc, "mix") as s:
        wa, ws, wo = s.sb("wa", [P, OT, D]), s.sb("ws", [P, YT, D]), s.sb("wo", [P, OT, D])
        gsub, gssm = s.sb("gsub", [P, 1]), s.sb("gssm", [P, YT])
        ot = s.sb("ot", [P, D])
        yt = s.sb("yt", [P, SIN])
        gt = [s.sb(f"gt{b}", [P, 2 * D]) for b in range(2)]
        xt = [s.sb(f"xt{b}", [P, D]) for b in range(2)]
        sq = s.sb("sq", [P, D])
        oT, yT, sT = s.sb("oT", [P, OT, P]), s.sb("yT", [P, YT, P]), s.sb("sT", [P, OT, P])
        ss, ms, rr = (s.sb(n, [P, H]) for n in ("ss", "ms", "rr"))
        tb = [s.ps(f"tb{q}", [P, 4, P]) for q in range(2)]
        oa, os_, xo = (s.ps(n, [P, D]) for n in ("oa", "os", "xo"))

        w_in, g_in, weighted = s.sems("w_in", 3), s.sem("g_in"), s.sem("weighted")
        o_in, y_in, gt_in, xt_in, x1_stored = s.sem("o_in"), s.sem("y_in"), s.sems("gt_in", 2), s.sems("xt_in", 2), s.sems("x1_stored", 2)
        squared, summed, ms_done, rr_done, o_normed = (s.sem(n) for n in ("squared", "summed", "ms_done", "rr_done", "o_normed"))
        oy_turned, oy_out, s_turned, s_out = (s.sem(n) for n in ("oy_turned", "oy_out", "s_turned", "s_out"))
        projected, gated, multiplied, added = (s.sem(n) for n in ("projected", "gated", "multiplied", "added"))
        pe_gate, pool_gate = s.sem("pe_gate"), s.sem("pool_gate")

        with nc.Block() as block:

            @block.sync
            def _(sp):
                sp.dma_start(gsub[:], io["attn_subln_g"].rearrange("a p -> p a"), allow_slow_non_contiguous=True).then_inc(g_in, 16)
                sp.dma_start(gssm[:], io["ssm_norm_g"].rearrange("a (k p) -> p (a k)", p=P), allow_slow_non_contiguous=True).then_inc(g_in, 16)
                for dst, name, q in ((wa, "w_attn_o", 0), (ws, "w_ssm_o", 1), (wo, "w_out", 2)):
                    if q == 1:
                        sp.wait_ge(o_in, 16)
                        sp.wait_ge(y_in, 16)
                    sp.dma_start(dst[:], io[name][0].rearrange("(k p) n -> p k n", p=P)).then_inc(w_in[q], 16)

                def store(t, k, b, r, nxt):
                    sp.wait_ge(added, t + 2)
                    sp.dma_start(dr["x1"][tokens(t, r), :], xt[b][0:r, :]).then_inc(x1_stored[b], 16)

                over_tiles(sp, store)
                for b in range(2):
                    sp.wait_ge(x1_stored[b], 16 * (NT // 2 + 2 - b))

            @block.gpsimd
            def _(pool):
                for b in range(2):
                    pool.sem_inc(x1_stored[b], 16)

                def tile(t, k, b, r, nxt):
                    rows = tokens(t, r)
                    x = io["x_sample"][0] if r == DEC else io["x_prompt"][0, rows, :]
                    hold(pool, pool_gate, oy_turned, t * OY + 2)
                    pool.dma_start(ot[0:r, :], dr["att"][rows, :]).then_inc(o_in, 16)
                    hold(pool, pool_gate, oy_turned, t * OY + OY)
                    pool.dma_start(yt[0:r, :], dr["yg"][rows, :]).then_inc(y_in, 16)
                    hold(pool, pool_gate, ms_done, t + 1)
                    pool.tensor_tensor(rr[0:r, :], ms[0:r, :], c.neghalf[0:r, 0:H], ALU.pow).then_inc(rr_done, 1)
                    hold(pool, pool_gate, x1_stored[b], (k + 1) * 16)
                    pool.dma_start(xt[b][0:r, :], x).then_inc(xt_in[b], 16)
                    hold(pool, pool_gate, s_turned, t * 2 + 2)
                    pool.dma_start(gt[b][0:r, :], dr["gs"][rows, :]).then_inc(gt_in[b], 16)

                over_tiles(pool, tile)

            @block.vector
            def _(dve):
                dve.sem_inc(gated, 3)
                dve.sem_inc(added, 1)
                dve.sem_inc(o_normed, 1)
                dve.wait_ge(g_in, 32)
                dve.wait_ge(w_in[0], 16)
                dve.tensor_scalar(wa[:].rearrange("p k n -> p (k n)"), wa[:].rearrange("p k n -> p (k n)"), gsub[:, 0:1],
                                  1.0 - LAM_INIT, ALU.mult, ALU.mult).then_inc(weighted, 1)

                def norm(t, r):
                    dve.wait_ge(squared, t + 1)
                    dve.tensor_reduce(ss[0:r, :], sq[0:r, :].rearrange("p (h v) -> p h v", h=H), AX_X, ALU.add).then_inc(summed, 1)
                    dve.wait_ge(summed, t + 1)
                    dve.tensor_scalar(ms[0:r, :], ss[0:r, :], 1.0 / P, EPS, ALU.mult, ALU.add).then_inc(ms_done, 1)
                    dve.wait_ge(rr_done, t + 1)
                    o3 = ot[0:r, :].rearrange("p (h v) -> p h v", h=H)
                    dve.tensor_tensor(o3, o3, rr[0:r, :].unsqueeze(2).broadcast_to([r, H, P]), ALU.mult).then_inc(o_normed, 1)

                def gate(t, k, b, r):
                    g = gt[b]
                    dve.wait_ge(gt_in[b], (k + 1) * 16)
                    dve.wait_ge(projected, t * 2 + 3)
                    dve.tensor_tensor(g[0:r, 0:D], g[0:r, 0:D], oa[0:r, :], ALU.mult).then_inc(gated, 1)
                    dve.wait_ge(projected, t * 2 + 4)
                    dve.tensor_tensor(g[0:r, D:2 * D], g[0:r, D:2 * D], os_[0:r, :], ALU.mult).then_inc(gated, 1)
                    dve.wait_ge(gated, t * 3 + 5)
                    dve.tensor_tensor(g[0:r, 0:D], g[0:r, 0:D], g[0:r, D:2 * D], ALU.add).then_inc(gated, 1)

                def add(t, k, b, r):
                    dve.wait_ge(xt_in[b], (k + 1) * 16)
                    dve.wait_ge(multiplied, t + 2)
                    dve.tensor_tensor(xt[b][0:r, :], xt[b][0:r, :], xo[0:r, :], ALU.add).then_inc(added, 1)

                def tile(t, k, b, r, nxt):
                    if nxt:
                        norm(t + 1, nxt)
                    gate(t, k, b, r)
                    if not (isinstance(t, int) and t == 0):
                        add(t - 1, k - 1 + b, 1 - b, P)

                norm(0, P)
                dve.wait_ge(w_in[1], 16)
                for k in range(YT):
                    dve.tensor_scalar(ws[:, k, :], ws[:, k, :], gssm[:, k:k + 1], None, ALU.mult).then_inc(weighted, 1)
                over_tiles(dve, tile)
                add(NPT, NPT // 2, 0, DEC)

            @block.scalar
            def _(act):
                act.sem_inc(s_out, 4)

                def square(t, r):
                    act.wait_ge(o_in, t * 16 + 16)
                    act.activation(sq[0:r, :], ot[0:r, :], ACT.Square).then_inc(squared, 1)

                def tile(t, k, b, r, nxt):
                    act.wait_ge(projected, t * 2 + 2)
                    for j in range(OY):
                        act.wait_ge(oy_turned, t * OY + (OY + j + 1))
                        dst = oT[:, 4 * j:4 * j + 4, 0:r] if j < 2 else yT[:, 4 * (j - 2):4 * (j - 2) + 4, 0:r]
                        act.activation(dst, tb[j % 2][:, :, 0:r], ACT.Copy).then_inc(oy_out, 1)
                    if nxt:
                        square(t + 1, nxt)
                    if not (isinstance(t, int) and t == 0):
                        sums_out(t - 1, P)

                def sums_out(t, r):
                    act.wait_ge(multiplied, t + 1)
                    for j in range(2):
                        act.wait_ge(s_turned, t * 2 + (4 + j + 1))
                        act.activation(sT[:, 4 * j:4 * j + 4, 0:r], tb[j][:, :, 0:r], ACT.Copy).then_inc(s_out, 1)

                square(0, P)
                over_tiles(act, tile)
                sums_out(NPT, DEC)

            @block.tensor
            def _(pe):
                pe.sem_inc(oy_turned, OY)
                pe.sem_inc(s_turned, 4)
                pe.sem_inc(projected, 2)
                pe.sem_inc(multiplied, 1)
                pe.wait_ge(weighted, 1)

                def project(t, k, b, r):
                    for j in range(OY):
                        if j == 0:
                            pe.wait_ge(o_normed, t + 2)
                        if j == 2:
                            pe.wait_ge(y_in, t * 16 + 16)
                        if j < 2:
                            hold(pe, pe_gate, s_out, t * 2 + (j + 1))
                        else:
                            hold(pe, pe_gate, oy_out, t * OY + (j - 1))
                        src = ot if j < 2 else yt
                        for q in range(4):
                            at = (4 * (j if j < 2 else j - 2) + q) * P
                            x = pe.transpose(tb[j % 2][:, q, 0:r], src[0:r, at:at + P], c.ident[0:r, 0:r])
                        x.then_inc(oy_turned, 1)
                    for out, xT, w, n, need, step in ((oa, oT, wa, OT, 2, 1), (os_, yT, ws, YT, OY, 2)):
                        pe.wait_ge(oy_out, t * OY + need)
                        hold(pe, pe_gate, gated, t * 3 + step)
                        if isinstance(t, int) and t == 0 and w is ws:
                            pe.wait_ge(weighted, 1 + YT)
                        for h in range(0, D, HALF):
                            for q in range(n):
                                x = pe.matmul(out[0:r, h:h + HALF], xT[:, q, 0:r], w[:, q, h:h + HALF], start=(q == 0), stop=(q == n - 1))
                        x.then_inc(projected, 1)

                def multiply(t, b, r, last):
                    pe.wait_ge(gated, t * 3 + 6)
                    for j in range(2):
                        if last:
                            pe.wait_ge(s_out, t * 2 + (j + 3))
                            pe.wait_ge(oy_out, t * OY + OY)
                        else:
                            hold(pe, pe_gate, oy_out, t * OY + (OY + 5 + j))
                        for q in range(4):
                            x = pe.transpose(tb[j][:, q, 0:r], gt[b][0:r, (4 * j + q) * P:(4 * j + q + 1) * P], c.ident[0:r, 0:r])
                        x.then_inc(s_turned, 1)
                    pe.wait_ge(s_out, t * 2 + 6)
                    hold(pe, pe_gate, added, t + 1)
                    for h in range(0, D, HALF):
                        for q in range(OT):
                            x = pe.matmul(xo[0:r, h:h + HALF], sT[:, q, 0:r], wo[:, q, h:h + HALF], start=(q == 0), stop=(q == OT - 1))
                    x.then_inc(multiplied, 1)

                def tile(t, k, b, r, nxt):
                    project(t, k, b, r)
                    if isinstance(t, int) and t == 0:
                        pe.wait_ge(w_in[2], 16)
                    else:
                        multiply(t - 1, 1 - b, P, False)

                over_tiles(pe, tile)
                multiply(NPT, 0, DEC, True)


def retrieve_and_finish(nc, io, dr, c):
    CHUNK8 = 8
    ITS = PSLOT // CHUNK8
    HALF = 512
    PREP_ACT, PREP_PE, PREP_DVE = 10, 6, 7
    FIN_ACT, FIN_PE, FIN_DVE = 10, 6, 15
    TK = 22
    TK_NEG = 14
    with Stage(nc, "peer") as s:
        wq, wg, we = s.sb("wq", [P, DK, D]), s.sb("wg", [P, DK, D]), s.sb("we", [P, PLE // P, D])
        gffn, gfin, gple = s.sb("gffn", [P, D]), s.sb("gfin", [P, D]), s.sb("gple", [P, DK])
        keys = s.sb("keys", [P, P])
        keysT = s.sb("keysT", [P, P])
        zero = s.sb("zero", [P, P])
        fold = s.sb("fold", [P, DEC])
        iota16 = s.sb("iota16", [P, PTOP])
        x1 = [s.sb(f"x1{b}", [P, D]) for b in range(2)]
        h2 = [s.sb(f"h2{b}", [P, D]) for b in range(2)]
        idx = [s.sb(f"idx{b}", [P, PSLOT], U32) for b in range(2)]
        gw = [s.sb(f"gw{b}", [P, PSLOT]) for b in range(2)]
        hT, qT = s.sb("hT", [P, DK, P]), s.sb("qT", [P, PH, P])
        s12 = s.sb("s12", [P, 2, PH, PNK])
        u = [s.sb(f"u{q}", [P, D]) for q in range(CHUNK8)]
        v = [s.sb(f"v{q}", [P, D]) for q in range(CHUNK8)]
        diag = [s.sb(f"diag{q}", [P, P]) for q in range(CHUNK8)]
        stage = [s.sb(f"stage{q}", [P, CHUNK8], U32) for q in range(2)]
        pre, ge, aw = ([s.sb(f"{n}{q}", [P, CHUNK8]) for q in range(2)] for n in ("pre", "ge", "aw"))
        cs, cs2 = s.sb("cs", [P, 2, PNK]), s.sb("cs2", [P, 2, PNK])
        top, topi, topf = s.sb("top", [P, 2, PTOP]), s.sb("topi", [P, 2, PTOP], U32), s.sb("topf", [P, 2, PTOP])
        cand, cand2 = s.sb("cand", [P, PTOP * PTOP]), s.sb("cand2", [P, PTOP * PTOP])
        best, pos, ab, abf = s.sb("best", [P, PTOP]), s.sb("pos", [P, PTOP], U32), s.sb("ab", [P, 2, PTOP], U32), s.sb("abf", [P, 2, PTOP])
        hot, sel = s.sb("hot", [P, 2, PTOP, PTOP]), s.sb("sel", [P, 2, PTOP])
        negbest, ex, tot, rtot = s.sb("negbest", [P, 1]), s.sb("ex", [P, PTOP]), s.sb("tot", [P, 1]), s.sb("rtot", [P, 1])
        pss, pr, pt = s.sb("pss", [P, 1]), s.sb("pr", [P, 1]), s.sb("pt", [P, 1])
        fss, fr, ft = s.sb("fss", [P, 1]), s.sb("fr", [P, 1]), s.sb("ft", [P, 1])
        x2, h3, y = s.sb("x2", [P, D]), s.sb("h3", [P, D]), s.sb("y", [P, D])
        pl, plT = s.sb("pl", [P, PLE]), s.sb("plT", [P, PLE // P, P])

        acc = s.ps("acc", [P, D])
        tb = [s.ps(f"tb{q}", [P, 4, P]) for q in range(2)]
        sb_ = [s.ps(f"sb{q}", [P, 4, P]) for q in range(2)]
        fo = s.ps("fo", [P, D])

        wq_in = s.sem("wq_in")
        w_in, vec_in, once, once_pe, once_act, iota_done = (s.sem(n) for n in ("w_in", "vec_in", "once", "once_pe", "once_act", "iota_done"))
        x1_in, pl_in, y_stored = s.sems("x1_in", 2), s.sem("pl_in"), s.sem("y_stored")
        prep_act, prep_pe, prep_dve = s.sem("prep_act"), s.sem("prep_pe"), s.sem("prep_dve")
        fin_act, fin_pe, fin_dve = s.sem("fin_act"), s.sem("fin_pe"), s.sem("fin_dve")
        tk, exp_done, idx_done = s.sem("tk"), s.sem("exp_done"), s.sem("idx_done")
        staged, u_in, v_in = s.sem("staged"), s.sems("u_in", CHUNK8), s.sems("v_in", CHUNK8)
        u_done, v_done, gelu_done, aw_done, diag_done = (s.sem(n) for n in ("u_done", "v_done", "gelu_done", "aw_done", "diag_done"))
        acc_done, acc_out = s.sem("acc_done"), s.sem("acc_out")
        pool_gate, pe_gate, dve_gate = s.sem("pool_gate"), s.sem("pe_gate"), s.sem("dve_gate")

        PIECES = {0: [("prepare", 0), ("finish", 0)], 1: [("prepare", 1)], 2: [("prepare", 2)],
                  3: [("finish", 1)], 4: [("finish", 2)]}
        CHOSEN = {3: 0, 4: 1, 5: 2, 7: 3}
        SAMPLE_PIECES = {0: [("finish", 0), ("finish", 1)], 1: [("finish", 2)]}

        def heads(eng, iteration, t, b, m, piece, choose, last):
            for i in range(PH // 2):
                for q in range(2):
                    iteration(t, b, m, i, q)
                    at = 2 * i + q
                    if at in CHOSEN:
                        choose(CHOSEN[at])
                    for kind, part in PIECES.get(at, []):
                        piece(kind, part)
                    if at == last:
                        piece("finish", 3)
            with eng.Fori(PH // 2, PH) as i:
                for q in range(2):
                    iteration(t, b, m, i, q)
                choose(i)

        def first_heads(eng, iteration, piece, choose):
            for at in range(PH):
                iteration(0, 0, P, at // 2, at % 2)
                if at + 2 < PH:
                    choose(0, at + 2)
                if at >= PH - 3:
                    piece("prepare", at - (PH - 3))
            with eng.Fori(0, PH // 2) as j:
                for q in range(2):
                    iteration(0, 0, P, j + PH // 2, q)
                    choose(1, j * 2 + q)

        def sample_heads(iteration, b, piece, last):
            for i in range(PH * DEC // P):
                for q in range(2):
                    iteration(NPT, b, DEC, i, q)
                    for kind, part in SAMPLE_PIECES.get(2 * i + q, []):
                        piece(kind, part)
                    if 2 * i + q == last:
                        piece("finish", 3)

        def count(t, i, q):
            return t * ITS + (i * 2 + q)

        def nothing(*a):
            pass

        with nc.Block() as block:

            @block.sync
            def _(sp):
                sp.dma_start(gffn[:], io["norm_ffn_g"].broadcast_to([P, D])).then_inc(vec_in, 16)
                sp.dma_start(gfin[:], io["final_norm_g"].rearrange("(a d) -> a d", a=1).broadcast_to([P, D])).then_inc(vec_in, 16)
                sp.dma_start(keys[:, 0:P // 2], io["peer_k1"][0]).then_inc(vec_in, 16)
                sp.dma_start(keys[:, P // 2:P], io["peer_k2"][0]).then_inc(vec_in, 16)
                sp.dma_start(gple[:], io["norm_ple_g"].rearrange("a (k p) -> p (a k)", p=P), allow_slow_non_contiguous=True).then_inc(vec_in, 16)

                def load_x1(t, b, r):
                    sp.wait_ge(acc_done, t + 1)
                    for copy in range(0, P, r):
                        sp.dma_start(x1[b][copy:copy + r, :], dr["x1"][tokens(t, r), :]).then_inc(x1_in[b], 16)

                def finish(t, r):
                    src = io["p_sample"][0, 0] if r == DEC else io["p_prompt"][0, 0, tokens(t, r), :]
                    dst = io["y_sample_out"] if r == DEC else io["y_prompt_out"][tokens(t, r), :]
                    sp.wait_ge(fin_pe, t * FIN_PE + 3)
                    sp.dma_start(pl[0:r, :], src).then_inc(pl_in, 16)
                    sp.wait_ge(fin_dve, t * FIN_DVE + FIN_DVE)
                    sp.dma_start(dst, y[0:r, :]).then_inc(y_stored, 16)

                load_x1(0, 0, P)
                sp.dma_start(wq[:], io["peer_wq"][0].rearrange("(k p) n -> p k n", p=P)).then_inc(wq_in, 16)
                sp.dma_start(wg[:], io["ple_w_gate"][0].rearrange("(k p) n -> p k n", p=P)).then_inc(w_in, 16)
                sp.dma_start(we[:], io["ple_w_proj"][0].rearrange("(k p) n -> p k n", p=P)).then_inc(w_in, 16)

                def tile(t, k, b, r, nxt):
                    if nxt:
                        load_x1(t + 1, 1 - b, nxt)
                    if not (isinstance(t, int) and t == 0):
                        finish(t - 1, P)

                sp.sem_inc(y_stored, 16)
                over_tiles(sp, tile)
                finish(NPT, DEC)
                sp.wait_ge(y_stored, 16 * (NT + 1))

            @block.gpsimd
            def _(pool):
                pool.iota(stage[0][:].bitcast(I32), [[1, CHUNK8]], base=0, channel_multiplier=0).then_inc(iota_done, 1)
                pool.iota(stage[1][:].bitcast(I32), [[1, CHUNK8]], base=CHUNK8, channel_multiplier=0).then_inc(iota_done, 1)
                pool.memset(zero[:], 0.0).then_inc(iota_done, 1)
                pool.wait_ge(once, 2)

                def iteration(t, b, r, i, q):
                    g = count(t, i, q)
                    if q == 0 and r == P:
                        hold(pool, pool_gate, idx_done, t * PH + (i + 1))
                    pool.tensor_copy(stage[q][:], idx[b][:, bass.ds(i * (2 * CHUNK8) + q * CHUNK8, CHUNK8)]).then_inc(staged, 1)
                    hold(pool, pool_gate, staged, g + 1)
                    for table, ring, arrived, used in (("peer_u", u, u_in, u_done), ("peer_v", v, v_in, v_done)):
                        for k in range(CHUNK8):
                            hold(pool, pool_gate, used, g * CHUNK8 + (k + 1))
                            pool.indirect_dma_start(ring[k][:], None, io[table][0], bass.IndirectOffsetOnAxis(
                                ap=stage[q][:, k:k + 1], axis=0)).then_inc(arrived[k], 16)

                def tile(t, k, b, r, nxt):
                    if isinstance(t, int) and t == 0:
                        first_heads(pool, iteration, nothing, nothing)
                    elif nxt:
                        heads(pool, iteration, t, b, r, nothing, nothing, None)
                    else:
                        hold(pool, pool_gate, idx_done, NT * PH + 1)
                        sample_heads(iteration, b, nothing, None)

                over_tiles(pool, tile)

            @block.vector
            def _(dve):
                dve.wait_ge(iota_done, 3)
                for q in range(2):
                    dve.tensor_copy(iota16[:, q * CHUNK8:(q + 1) * CHUNK8], stage[q][:]).then_inc(once, 1)
                dve.tensor_reduce(fold[:], c.ident[:].rearrange("p (q m) -> p m q", m=DEC), AX_X, ALU.add).then_inc(once, 1)
                dve.sem_inc(u_done, CHUNK8)
                dve.wait_ge(vec_in, 80)

                def rsqrt(step, ms, root, tmp, act_sem, act_val):
                    step(dve.tensor_scalar(ms, ms, 1.0 / D, EPS, ALU.mult, ALU.add))
                    dve.wait_ge(act_sem, act_val)
                    step(dve.reciprocal(root, tmp))
                    step(dve.tensor_tensor(tmp, root, root, ALU.mult))
                    step(dve.tensor_tensor(tmp, tmp, ms, ALU.mult))
                    step(dve.tensor_scalar(tmp, tmp, -0.5, 1.5, ALU.mult, ALU.add))
                    step(dve.tensor_tensor(root, root, tmp, ALU.mult))

                def stepper(sem, base):
                    done = [0]

                    def step(ins):
                        ins.then_inc(sem, 1)
                        done[0] += 1
                        hold(dve, dve_gate, sem, base + done[0])
                    return step, done

                def prepare(t, b, part):
                    if part:
                        return
                    r = P
                    step, done = stepper(prep_dve, t * PREP_DVE)
                    dve.wait_ge(prep_act, t * PREP_ACT + 1)
                    rsqrt(step, pss[0:r, :], pr[0:r, :], pt[0:r, :], prep_act, t * PREP_ACT + 2)
                    step(dve.scalar_tensor_tensor(out=h2[b][0:r, :], in0=x1[b][0:r, :], scalar=pr[0:r, 0:1], in1=gffn[0:r, :],
                                                  op0=ALU.mult, op1=ALU.mult))
                    assert done[0] == PREP_DVE

                def choose(t, b, r, i):
                    n = t * PH + i
                    base = n * TK
                    step, done = stepper(tk, base)

                    def both(make):
                        for m in range(2):
                            make(m).then_inc(tk, 1)
                        done[0] += 2
                        hold(dve, dve_gate, tk, base + done[0])

                    dve.wait_ge(prep_act, t * PREP_ACT + PREP_ACT)
                    step(dve.tensor_copy(cs[0:r], s12[0:r, :, bass.ds(i, 1), :].rearrange("p m h n -> p m (h n)")))
                    both(lambda m: dve.max(top[0:r, m, 0:8], cs[0:r, m, :]))
                    both(lambda m: dve.match_replace(cs2[0:r, m, :], top[0:r, m, 0:8], cs[0:r, m, :], -3.0e38))
                    both(lambda m: dve.max(top[0:r, m, 8:16], cs2[0:r, m, :]))
                    for m in range(2):
                        dve.max_index(topi[0:r, m, 0:8], top[0:r, m, 0:8], cs[0:r, m, :])
                        dve.max_index(topi[0:r, m, 8:16], top[0:r, m, 8:16], cs2[0:r, m, :])
                    step(dve.tensor_tensor(cand[0:r, :].rearrange("p (a b) -> p a b", b=PTOP),
                                           top[0:r, 0, :].unsqueeze(2).broadcast_to([r, PTOP, PTOP]),
                                           top[0:r, 1, :].unsqueeze(1).broadcast_to([r, PTOP, PTOP]), ALU.add))
                    step(dve.max(best[0:r, 0:8], cand[0:r, :]))
                    step(dve.match_replace(cand2[0:r, :], best[0:r, 0:8], cand[0:r, :], -3.0e38))
                    step(dve.max(best[0:r, 8:16], cand2[0:r, :]))
                    dve.max_index(pos[0:r, 0:8], best[0:r, 0:8], cand[0:r, :])
                    step(dve.max_index(pos[0:r, 8:16], best[0:r, 8:16], cand2[0:r, :]))
                    step(dve.tensor_copy(topf[0:r], topi[0:r]))
                    step(dve.tensor_scalar(negbest[0:r, :], best[0:r, 0:1], -1.0, None, ALU.mult))
                    assert done[0] == TK_NEG, done
                    dve.tensor_scalar(ab[0:r, 0, :], pos[0:r, :], 4, None, ALU.logical_shift_right)
                    step(dve.tensor_scalar(ab[0:r, 1, :], pos[0:r, :], PTOP - 1, None, ALU.bitwise_and))
                    step(dve.tensor_copy(abf[0:r], ab[0:r]))
                    for m in range(2):
                        hm = dve.tensor_tensor(hot[0:r, m], abf[0:r, m, :].unsqueeze(2).broadcast_to([r, PTOP, PTOP]),
                                               iota16[0:r, :].unsqueeze(1).broadcast_to([r, PTOP, PTOP]), ALU.is_equal)
                    step(hm)
                    for m in range(2):
                        hm = dve.tensor_tensor(hot[0:r, m], hot[0:r, m], topf[0:r, m, :].unsqueeze(1).broadcast_to([r, PTOP, PTOP]), ALU.mult)
                    step(hm)
                    step(dve.tensor_reduce(sel[0:r], hot[0:r], AX_X, ALU.add))
                    step(dve.scalar_tensor_tensor(out=idx[b][0:r, bass.ds(i * PTOP, PTOP)], in0=sel[0:r, 0, :], scalar=float(PNK),
                                                  in1=sel[0:r, 1, :], op0=ALU.mult, op1=ALU.add))
                    dve.wait_ge(exp_done, n + 1)
                    step(dve.reciprocal(rtot[0:r, :], tot[0:r, :]))
                    step(dve.tensor_scalar(gw[b][0:r, bass.ds(i * PTOP, PTOP)], ex[0:r, :], rtot[0:r, 0:1], None, ALU.mult))
                    assert done[0] == TK, done
                    dve.sem_inc(idx_done, 1)

                def iteration(t, b, r, i, q):
                    g = count(t, i, q)
                    for k in range(CHUNK8):
                        dve.wait_ge(u_in[k], g * 16 + 16)
                        dve.tensor_tensor_reduce(u[k][:], u[k][:], h2[b][:], 1.0, 0.0, ALU.mult, ALU.add,
                                                 pre[q][:, k:k + 1]).then_inc(u_done, 1)
                    dve.wait_ge(gelu_done, g + 1)
                    dve.tensor_tensor(aw[q][:], ge[q][:], gw[b][:, bass.ds(i * (2 * CHUNK8) + q * CHUNK8, CHUNK8)],
                                      ALU.mult).then_inc(aw_done, 1)

                def place_copies(b):
                    n = PSLOT * DEC // P
                    for q in range(1, P // DEC):
                        rows, src = slice(q * DEC, (q + 1) * DEC), slice(q * n, (q + 1) * n)
                        dve.tensor_copy(idx[b][rows, 0:n], idx[b][rows, src])
                        x = dve.tensor_copy(gw[b][rows, 0:n], gw[b][rows, src])
                    x.then_inc(idx_done, 1)
                    dve.wait_ge(idx_done, NT * PH + 1)

                def finish(t, r, part):
                    a, d = t * FIN_ACT, t * FIN_DVE
                    if part == 0:
                        step, done = stepper(fin_dve, d)
                        dve.wait_ge(fin_act, a + 1)
                        rsqrt(step, fss[0:r, :], fr[0:r, :], ft[0:r, :], fin_act, a + 2)
                    elif part == 3:
                        step, done = stepper(fin_dve, d + 6)
                        dve.wait_ge(fin_act, a + 8)
                        dve.wait_ge(fin_pe, t * FIN_PE + 6 + 3)
                        step(dve.tensor_tensor(y[0:r, :], y[0:r, :], fo[0:r, :], ALU.mult))
                        step(dve.tensor_tensor(y[0:r, :], y[0:r, :], x2[0:r, :], ALU.add))
                        dve.wait_ge(fin_act, a + 9)
                        rsqrt(step, fss[0:r, :], fr[0:r, :], ft[0:r, :], fin_act, a + 10)
                        step(dve.scalar_tensor_tensor(out=y[0:r, :], in0=y[0:r, :], scalar=fr[0:r, 0:1], in1=gfin[0:r, :],
                                                      op0=ALU.mult, op1=ALU.mult))
                        assert 6 + done[0] == FIN_DVE, done

                def tile(t, k, b, r, nxt):
                    def piece(kind, part):
                        if kind == "prepare":
                            prepare(t + 1, 1 - b, part)
                        else:
                            finish(t - 1, P, part)
                    if isinstance(t, int) and t == 0:
                        first_heads(dve, iteration, piece, lambda u, i: choose(u, u, P, i))
                    elif nxt:
                        heads(dve, iteration, t, b, r, piece, lambda i: choose(t + 1, 1 - b, P, i), 7)
                        if nxt == DEC:
                            place_copies(1 - b)
                    else:
                        sample_heads(iteration, b, piece, 3)

                for part in range(3):
                    prepare(0, 0, part)
                for i in range(2):
                    choose(0, 0, P, i)
                dve.wait_ge(w_in, 32)
                for k in range(DK):
                    dve.tensor_scalar(wg[:, k, :], wg[:, k, :], gple[:, k:k + 1], None, ALU.mult).then_inc(once, 1)
                over_tiles(dve, tile)
                for part in range(4):
                    finish(NPT, DEC, part)

            @block.scalar
            def _(act):
                act.sem_inc(acc_out, 1)
                act.wait_ge(once_pe, 1)
                act.activation(keysT[:], tb[0][:, 0, :], ACT.Copy).then_inc(once_act, 1)

                def prepare(t, k, b, copies, part):
                    a = t * PREP_ACT
                    if part == 0:
                        act.wait_ge(x1_in[b], k * 16 + 16 * copies)
                        act.activation(h2[b][:], x1[b][:], ACT.Square, accum_out=pss[:]).then_inc(prep_act, 1)
                        act.wait_ge(prep_dve, t * PREP_DVE + 1)
                        act.activation(pt[:], pss[:], ACT.Sqrt).then_inc(prep_act, 1)
                    elif part == 1:
                        for j in range(2):
                            act.wait_ge(prep_pe, t * PREP_PE + (j + 1))
                            act.activation(hT[:, 4 * j:4 * j + 4, :], tb[j][:], ACT.Copy).then_inc(prep_act, 1)
                        for j in range(2):
                            act.wait_ge(prep_pe, t * PREP_PE + (j + 3))
                            act.activation(qT[:, 4 * j:4 * j + 4, :], tb[j][:], ACT.Copy).then_inc(prep_act, 1)
                    else:
                        for j in range(2):
                            act.wait_ge(prep_pe, t * PREP_PE + (j + 5))
                            for m in range(2):
                                act.activation(s12[:, m, 4 * j:4 * j + 4, :], sb_[m][:], ACT.Copy).then_inc(prep_act, 1)

                def choose(t, b, r, i):
                    n = t * PH + i
                    act.wait_ge(tk, n * TK + TK_NEG)
                    act.activation(ex[0:r, :], best[0:r, :], ACT.Exp, bias=negbest[0:r, 0:1], accum_out=tot[0:r, :]).then_inc(exp_done, 1)

                def iteration(t, b, r, i, q):
                    g = count(t, i, q)
                    act.wait_ge(u_done, g * CHUNK8 + 2 * CHUNK8)
                    act.activation(ge[q][:], pre[q][:], ACT.Gelu_apprx_tanh).then_inc(gelu_done, 1)
                    act.wait_ge(aw_done, g + 1)
                    for k in range(CHUNK8):
                        act.wait_ge(v_done, g * CHUNK8 + (k + 1))
                        act.activation(diag[k][:, 0:r], c.ident[:] if r == P else fold[:], ACT.Copy, scale=aw[q][:, k:k + 1]).then_inc(diag_done, 1)

                def sum_out(t, r):
                    act.wait_ge(acc_done, t + 3)
                    act.activation(x2[0:r, :], acc[0:r, :], ACT.Copy).then_inc(acc_out, 1)

                def finish(t, r, part):
                    d, p = t * FIN_DVE, t * FIN_PE + 3
                    if part == 0:
                        act.wait_ge(acc_out, t + 2)
                        if r == DEC:
                            act.wait_ge(fin_dve, d)
                        act.activation(h3[0:r, :], x2[0:r, :], ACT.Square, accum_out=fss[0:r, :]).then_inc(fin_act, 1)
                        act.wait_ge(fin_dve, d + 1)
                        act.activation(ft[0:r, :], fss[0:r, :], ACT.Sqrt).then_inc(fin_act, 1)
                        act.wait_ge(fin_dve, d + 6)
                        act.activation(h3[0:r, :], x2[0:r, :], ACT.Copy, scale=fr[0:r, 0:1]).then_inc(fin_act, 1)
                    elif part == 1:
                        for j in range(2):
                            act.wait_ge(fin_pe, p + (j + 1))
                            act.activation(hT[:, 4 * j:4 * j + 4, 0:r], tb[j][:, :, 0:r], ACT.Copy).then_inc(fin_act, 1)
                        act.wait_ge(fin_pe, p + 3)
                        act.activation(plT[:, :, 0:r], sb_[0][:, 0:2, 0:r], ACT.Copy).then_inc(fin_act, 1)
                    elif part == 2:
                        act.wait_ge(y_stored, t * 16 + 16)
                        for j in range(2):
                            act.wait_ge(fin_pe, p + (j + 4))
                            act.activation(y[0:r, j * HALF:(j + 1) * HALF], fo[0:r, j * HALF:(j + 1) * HALF], ACT.Sigmoid).then_inc(fin_act, 1)
                    else:
                        act.wait_ge(fin_dve, d + 8)
                        act.activation(h3[0:r, :], y[0:r, :], ACT.Square, accum_out=fss[0:r, :]).then_inc(fin_act, 1)
                        act.wait_ge(fin_dve, d + 9)
                        act.activation(ft[0:r, :], fss[0:r, :], ACT.Sqrt).then_inc(fin_act, 1)

                def tile(t, k, b, r, nxt):
                    def piece(kind, part):
                        if kind == "prepare":
                            prepare(t + 1, k + b, 1 - b, P // nxt, part)
                        else:
                            finish(t - 1, P, part)
                    if isinstance(t, int) and t == 0:
                        first_heads(act, iteration, piece, lambda u, i: choose(u, u, P, i))
                    elif nxt:
                        heads(act, iteration, t, b, r, piece, lambda i: choose(t + 1, 1 - b, P, i), 7)
                    else:
                        sample_heads(iteration, b, piece, 3)
                    sum_out(t, r)

                for part in range(3):
                    prepare(0, 0, 0, 1, part)
                act.wait_ge(once, 3)
                for i in range(2):
                    choose(0, 0, P, i)
                over_tiles(act, tile)
                for part in range(4):
                    finish(NPT, DEC, part)

            @block.tensor
            def _(pe):
                pe.sem_inc(acc_done, 2)
                pe.sem_inc(v_done, CHUNK8)
                pe.sem_inc(fin_pe, 3)
                pe.wait_ge(vec_in, 80)
                pe.transpose(tb[0][:, 0, :], keys[:], c.ident[:]).then_inc(once_pe, 1)
                pe.wait_ge(once_act, 1)
                pe.wait_ge(iota_done, 3)

                def turn(src, r):
                    for j in range(2):
                        for q in range(4):
                            at = (4 * j + q) * P
                            x = pe.transpose(tb[j][:, q, 0:r], src[0:r, at:at + P], c.ident[0:r, 0:r])
                        yield x

                def prepare(t, b, part):
                    a = t * PREP_ACT
                    if part == 1:
                        hold(pe, pe_gate, prep_dve, t * PREP_DVE + PREP_DVE)
                        for x in turn(h2[b], P):
                            x.then_inc(prep_pe, 1)
                        hold(pe, pe_gate, prep_act, a + 4)
                        for j in range(2):
                            for h in range(4):
                                for k in range(DK):
                                    at = (4 * j + h) * P
                                    x = pe.matmul(tb[j][:, h, :], wq[:, k, at:at + P], hT[:, k, :], start=(k == 0), stop=(k == DK - 1))
                            x.then_inc(prep_pe, 1)
                    elif part == 2:
                        for j in range(2):
                            hold(pe, pe_gate, prep_act, a + (6 if j == 0 else 8))
                            for m in range(2):
                                half = slice(m * P // 2, (m + 1) * P // 2)
                                for h in range(4):
                                    x = pe.matmul(sb_[m][:, h, :], qT[half, 4 * j + h, :], keysT[half, :], start=True, stop=True)
                            x.then_inc(prep_pe, 1)

                def iteration(t, b, r, i, q):
                    g = count(t, i, q)
                    for k in range(CHUNK8):
                        pe.wait_ge(diag_done, g * CHUNK8 + (k + 1))
                        hold(pe, pe_gate, v_in[k], g * 16 + 16)
                        for h in range(0, D, HALF):
                            x = pe.matmul(acc[0:r, h:h + HALF], diag[k][:, 0:r], v[k][:, h:h + HALF], start=False, stop=False)
                        x.then_inc(v_done, 1)

                def open_sum(t, b, r):
                    hold(pe, pe_gate, acc_out, t + 1)
                    for h in range(0, D, HALF):
                        pe.matmul(acc[0:r, h:h + HALF], c.ident[0:r, 0:r], x1[b][0:r, h:h + HALF], start=True, stop=False)

                def close_sum(t, b, r):
                    for h in range(0, D, HALF):
                        x = pe.matmul(acc[0:r, h:h + HALF], zero[0:r, 0:r], x1[b][0:r, h:h + HALF], start=False, stop=True)
                    x.then_inc(acc_done, 1)

                def finish(t, r, part):
                    a = t * FIN_ACT
                    if part == 1:
                        hold(pe, pe_gate, pl_in, t * 16 + 16)
                        hold(pe, pe_gate, fin_act, a + 3)
                        for x in turn(h3, r):
                            x.then_inc(fin_pe, 1)
                        for q in range(PLE // P):
                            x = pe.transpose(sb_[0][:, q, 0:r], pl[0:r, q * P:(q + 1) * P], c.ident[0:r, 0:r])
                        x.then_inc(fin_pe, 1)
                    elif part == 2:
                        hold(pe, pe_gate, fin_act, a + 5)
                        for h in range(2):
                            for k in range(DK):
                                x = pe.matmul(fo[0:r, h * HALF:(h + 1) * HALF], hT[:, k, 0:r], wg[:, k, h * HALF:(h + 1) * HALF],
                                              start=(k == 0), stop=(k == DK - 1))
                            x.then_inc(fin_pe, 1)
                    elif part == 3:
                        hold(pe, pe_gate, fin_act, a + 8)
                        for h in range(2):
                            for k in range(PLE // P):
                                x = pe.matmul(fo[0:r, h * HALF:(h + 1) * HALF], plT[:, k, 0:r], we[:, k, h * HALF:(h + 1) * HALF],
                                              start=(k == 0), stop=(k == PLE // P - 1))
                        x.then_inc(fin_pe, 1)

                def tile(t, k, b, r, nxt):
                    def piece(kind, part):
                        if kind == "prepare":
                            prepare(t + 1, 1 - b, part)
                        else:
                            finish(t - 1, P, part)
                    open_sum(t, b, r)
                    if isinstance(t, int) and t == 0:
                        first_heads(pe, iteration, piece, nothing)
                    elif nxt:
                        heads(pe, iteration, t, b, r, piece, nothing, 5)
                    else:
                        sample_heads(iteration, b, piece, 2)
                    close_sum(t, b, r)

                pe.wait_ge(wq_in, 16)
                for part in range(3):
                    prepare(0, 0, part)
                pe.wait_ge(once, 3 + DK)
                pe.wait_ge(w_in, 32)
                over_tiles(pe, tile)
                for part in range(4):
                    finish(NPT, DEC, part)


class Held:

    def __init__(self, nc, whole, front):
        def sb(stack, name, shape, dt=F32):
            return stack.enter_context(nc.sbuf_tensor(name, shape, dt))

        self.ident = sb(whole, "ident", [P, P])
        self.ones = sb(front, "ones", [P, P])
        self.upper = sb(front, "upper", [P, P])
        self.below = sb(front, "below", [P, P])
        self.neghalf = sb(front, "neghalf", [P, 16])
        self.dt = sb(front, "dt", [P, NT, SH])


SCRATCH = {
    "chan": (C_V + SCD, T),
    "zs": (TP, SIN),
    "gs": (TP, 2 * D),
    "att": (TP, D),
    "xtok": (TP, SIN + SG * SN),
    "bc": (2 * SG * SN, TP),
    "yg": (TP, SIN),
    "x1": (TP, D),
}


def build(nc, io, dr):
    with ExitStack() as whole:
        with ExitStack() as front:
            c = Held(nc, whole, front)
            build_constants(nc, c)
            project_inputs(nc, io, dr, c)
            attend(nc, io, dr, c)
            causal_convolution(nc, io, dr, c)
            state_space(nc, io, dr, c)
            mix_branches(nc, io, dr, c)
        retrieve_and_finish(nc, io, dr, c)


_INS = ["x_prompt", "x_sample", "p_prompt", "p_sample", "cache_k", "cache_v", "state_conv", "state_ssm",
        "norm_mix_g", "w_in", "lam_q1", "lam_k1", "lam_q2", "lam_k2", "attn_subln_g", "w_attn_o",
        "conv_w", "conv_b", "dt_bias", "a_log", "d_skip", "ssm_norm_g", "w_ssm_o", "w_out",
        "norm_ffn_g", "peer_wq", "peer_k1", "peer_k2", "peer_u", "peer_v",
        "norm_ple_g", "ple_w_gate", "ple_w_proj", "final_norm_g"]
_OUTS = [("y_prompt_out", (SEQ, D), (1, SEQ, D)),
         ("y_sample_out", (DEC, D), (1, DEC, D)),
         ("k_prompt_out", (SEQ, D), (1, 1, SEQ, H, 2, AK)),
         ("v_prompt_out", (SEQ, D), (1, 1, SEQ, H, 2 * AK)),
         ("conv_prompt_out", (SCONV - 1, SCD), (1, 1, SCONV - 1, SCD)),
         ("ssm_prompt_out", (SIN, SN), (1, 1, SH, SP_, SN)),
         ("k_sample_out", (DEC, D), (1, 1, DEC, H, 2, AK)),
         ("v_sample_out", (DEC, D), (1, 1, DEC, H, 2 * AK)),
         ("conv_sample_out", (SCONV - 1, SCD), (1, 1, SCONV - 1, SCD)),
         ("ssm_sample_out", (SIN, SN), (1, 1, SH, SP_, SN))]


def kernel(**inputs):
    import numpy as _np
    import concourse.bacc as _bacc
    from concourse import mybir as _mybir
    from concourse.bass_utils import run_bass_kernel_spmd as _run

    nc = _bacc.Bacc("TRN2", target_bir_lowering=False, num_devices=1)
    arrays, io = {}, {}
    for name in _INS:
        a = _np.ascontiguousarray(inputs[name])
        arrays[f"in_{name}_dram"] = a
        io[name] = nc.dram_tensor(f"in_{name}_dram", a.shape, _mybir.dt.from_np(a.dtype), kind="ExternalInput").ap()
    for i, (name, shape, _) in enumerate(_OUTS):
        io[name] = nc.dram_tensor(f"out_{i}_dram", shape, F32, kind="ExternalOutput").ap()
    io["cache_k2"] = io["cache_k"].rearrange("a b t h j d -> (a b t) (h j d)")
    io["cache_v2"] = io["cache_v"].rearrange("a b t h d -> (a b t) (h d)")
    dr = {name: nc.dram_tensor(f"scratch_{name}", shape, F32, kind="Internal").ap() for name, shape in SCRATCH.items()}
    build(nc, io, dr)
    r = _run(nc, [arrays], core_ids=[0])
    got = tuple(r.results[0][f"out_{i}_dram"] for i in range(len(_OUTS)))
    return tuple(_np.asarray(g).reshape(shape) for g, (_, _, shape) in zip(got, _OUTS))
```
